# Optimizing a Trainium2 kernel written in Bass

```python
import math
import jax, jax.numpy as jnp
from jax import lax
import numpy as np

D_MODEL = 1024
BATCH = 1
SEQ = 1024
DEPTH = 2

N_EVEN = (DEPTH + 1) // 2
N_ODD = DEPTH // 2
DN_ALPHA = (2.0 * DEPTH) ** 0.25
DN_BETA = (8.0 * DEPTH) ** -0.25

RNN_WIDTH = D_MODEL // 2
RNN_HEADS = 8
RNN_HEAD_DIM = RNN_WIDTH // RNN_HEADS
CONV_WIDTH = 4
RG_C = 8.0

MLA_HEADS = 8
MLA_NOPE = 64
MLA_ROPE = 32
MLA_V = 64
MLA_Q_RANK = D_MODEL // 4
MLA_KV_RANK = D_MODEL // 8
MLA_WIDTH = MLA_HEADS * MLA_V
ROPE_THETA = 10000.0
Q_BLOCK = 128

AB_WIDTH = RNN_WIDTH + MLA_WIDTH
AB_IN = RNN_WIDTH + AB_WIDTH + MLA_Q_RANK + MLA_KV_RANK + MLA_ROPE

SSD_INNER = 2 * D_MODEL
SSD_HEAD_DIM = 64
SSD_HEADS = SSD_INNER // SSD_HEAD_DIM
SSD_GROUPS = 4
SSD_STATE = 128
SSD_CHUNK = 128
SSD_CONV_DIM = SSD_INNER + 2 * SSD_GROUPS * SSD_STATE
SSD_IN = SSD_INNER + SSD_CONV_DIM + SSD_HEADS


def _rmsnorm(x, g, eps=1e-6):
    xf = x.astype(jnp.float32)
    y = xf * lax.rsqrt(jnp.mean(xf * xf, axis=-1, keepdims=True) + eps)
    return (y * g.astype(jnp.float32)).astype(x.dtype)

def _layernorm(x, g, b, eps=1e-5):
    xf = x.astype(jnp.float32)
    mu = jnp.mean(xf, axis=-1, keepdims=True)
    xc = xf - mu
    var = jnp.mean(xc * xc, axis=-1, keepdims=True)
    y = xc * lax.rsqrt(var + eps) * g.astype(jnp.float32) + b.astype(jnp.float32)
    return y.astype(x.dtype)

def _causal_conv(x, w, b):
    k_taps = w.shape[0]
    seqlen = x.shape[1]
    xp = jnp.pad(x, ((0, 0), (k_taps - 1, 0), (0, 0)))
    return sum(xp[:, k:k + seqlen] * w[k] for k in range(k_taps)) + b

def _rope(x, cos, sin):
    half = x.shape[-1] // 2
    x1, x2 = x[..., :half], x[..., half:]
    return jnp.concatenate([x1 * cos - x2 * sin, x2 * cos + x1 * sin], axis=-1)

def _rg_lru(x, w_a, b_a, w_x, b_x, lam):
    bsz, seqlen, _ = x.shape
    xh = x.reshape(bsz, seqlen, RNN_HEADS, RNN_HEAD_DIM)
    r = jax.nn.sigmoid(jnp.einsum('bshi,hij->bshj', xh, w_a).reshape(bsz, seqlen, RNN_WIDTH) + b_a)
    i = jax.nn.sigmoid(jnp.einsum('bshi,hij->bshj', xh, w_x).reshape(bsz, seqlen, RNN_WIDTH) + b_x)
    log_a = (-RG_C * r.astype(jnp.float32)) * jax.nn.softplus(-lam.astype(jnp.float32))
    a = jnp.exp(log_a)
    mult = jnp.sqrt(-jnp.expm1(2.0 * log_a))
    u = mult * (i * x).astype(jnp.float32)

    def combine(c1, c2):
        a1, b1 = c1
        a2, b2 = c2
        return a1 * a2, a2 * b1 + b2

    _, h = lax.associative_scan(combine, (a, u), axis=1)
    return h.astype(x.dtype)

def _mla_attention(q_nope, q_rope, k_nope, k_rope, v):
    seqlen = q_nope.shape[1]
    scale = (MLA_NOPE + MLA_ROPE) ** -0.5
    outs = []
    for blk in range(seqlen // Q_BLOCK):
        q0 = blk * Q_BLOCK
        kend = q0 + Q_BLOCK
        s = (jnp.einsum('bqhd,bkhd->bhqk', q_nope[:, q0:kend], k_nope[:, :kend])
             + jnp.einsum('bqhr,bkr->bhqk', q_rope[:, q0:kend], k_rope[:, :kend]))
        s = s.astype(jnp.float32) * scale
        mask = jnp.arange(kend)[None, :] <= (q0 + jnp.arange(Q_BLOCK))[:, None]
        s = jnp.where(mask, s, -jnp.inf)
        p = jax.nn.softmax(s, axis=-1).astype(v.dtype)
        outs.append(jnp.einsum('bhqk,bkhd->bqhd', p, v[:, :kend]))
    return jnp.concatenate(outs, axis=1)

def _rglru_mla_layer(x, cos, sin, w_in, conv_w, conv_b, gate_a_w, gate_a_b, gate_x_w,
                     gate_x_b, lam, q_norm, kv_norm, w_uq, w_ukv, w_out):
    bsz, seqlen, _ = x.shape
    proj = jnp.einsum('bsd,de->bse', x, w_in)
    x_rnn, gate, c_q, c_kv, k_rope = jnp.split(
        proj, [RNN_WIDTH, RNN_WIDTH + AB_WIDTH, RNN_WIDTH + AB_WIDTH + MLA_Q_RANK,
               RNN_WIDTH + AB_WIDTH + MLA_Q_RANK + MLA_KV_RANK], axis=-1)
    x_rnn = _causal_conv(x_rnn, conv_w, conv_b)
    y_rnn = _rg_lru(x_rnn, gate_a_w, gate_a_b, gate_x_w, gate_x_b, lam)
    q = jnp.einsum('bsr,re->bse', _rmsnorm(c_q, q_norm), w_uq)
    q = q.reshape(bsz, seqlen, MLA_HEADS, MLA_NOPE + MLA_ROPE)
    q_nope = q[..., :MLA_NOPE]
    q_rope = _rope(q[..., MLA_NOPE:], cos[:, :, None], sin[:, :, None])
    kv = jnp.einsum('bsr,re->bse', _rmsnorm(c_kv, kv_norm), w_ukv)
    kv = kv.reshape(bsz, seqlen, MLA_HEADS, MLA_NOPE + MLA_V)
    k_nope, v = kv[..., :MLA_NOPE], kv[..., MLA_NOPE:]
    k_rope = _rope(k_rope, cos, sin)
    y_mla = _mla_attention(q_nope, q_rope, k_nope, k_rope, v).reshape(bsz, seqlen, MLA_WIDTH)
    y = jnp.concatenate([y_rnn, y_mla], axis=-1) * jax.nn.silu(gate)
    return jnp.einsum('bse,ed->bsd', y, w_out)

def _ssd_scan(x, dt, a_neg, bm, cm):
    bsz, seqlen, n_heads, p_dim = x.shape
    n_groups, n_state = bm.shape[2], bm.shape[3]
    hpg = n_heads // n_groups
    nc, L = seqlen // SSD_CHUNK, SSD_CHUNK
    xf = (x.astype(jnp.float32) * dt[..., None]).reshape(bsz, nc, L, n_groups, hpg, p_dim)
    a_dt = (dt * a_neg).reshape(bsz, nc, L, n_groups, hpg)
    bc = bm.astype(jnp.float32).reshape(bsz, nc, L, n_groups, n_state)
    cc = cm.astype(jnp.float32).reshape(bsz, nc, L, n_groups, n_state)
    cs = jnp.cumsum(a_dt, axis=2)
    cs_h = jnp.transpose(cs, (0, 1, 3, 4, 2))
    seg = cs_h[..., :, None] - cs_h[..., None, :]
    causal = jnp.tril(jnp.ones((L, L), dtype=bool))
    decay = jnp.where(causal, jnp.exp(jnp.where(causal, seg, 0.0)), 0.0)
    cb = jnp.einsum('bclgn,bcsgn->bcgls', cc, bc)
    y_diag = jnp.einsum('bcghls,bcsghp->bclghp', cb[:, :, :, None] * decay, xf)
    decay_states = jnp.exp(cs[:, :, -1:] - cs)
    states = jnp.einsum('bclgn,bclghp->bcghpn', bc, xf * decay_states[..., None])
    chunk_decay = jnp.exp(cs[:, :, -1])

    def step(h, inp):
        dec, st = inp
        return h * dec[..., None, None] + st, h

    h0 = jnp.zeros((bsz, n_groups, hpg, p_dim, n_state), jnp.float32)
    _, prev = lax.scan(step, h0, (jnp.moveaxis(chunk_decay, 1, 0), jnp.moveaxis(states, 1, 0)))
    prev = jnp.moveaxis(prev, 0, 1)
    y_off = jnp.einsum('bclgn,bcghpn->bclghp', cc, prev) * jnp.exp(cs)[..., None]
    return (y_diag + y_off).reshape(bsz, seqlen, n_heads, p_dim)

def _ssd_layer(x, w_in, conv_w, conv_b, dt_bias, a_log, d_skip, norm_w, w_out):
    bsz, seqlen, _ = x.shape
    proj = jnp.einsum('bsd,de->bse', x, w_in)
    z, xbc, dt = jnp.split(proj, [SSD_INNER, SSD_INNER + SSD_CONV_DIM], axis=-1)
    xbc = jax.nn.silu(_causal_conv(xbc, conv_w, conv_b))
    xs, bm, cm = jnp.split(xbc, [SSD_INNER, SSD_INNER + SSD_GROUPS * SSD_STATE], axis=-1)
    xs = xs.reshape(bsz, seqlen, SSD_HEADS, SSD_HEAD_DIM)
    bm = bm.reshape(bsz, seqlen, SSD_GROUPS, SSD_STATE)
    cm = cm.reshape(bsz, seqlen, SSD_GROUPS, SSD_STATE)
    dt = jax.nn.softplus(dt.astype(jnp.float32) + dt_bias.astype(jnp.float32))
    a_neg = -jnp.exp(a_log.astype(jnp.float32))
    y = _ssd_scan(xs, dt, a_neg, bm, cm) + d_skip.astype(jnp.float32)[:, None] * xs.astype(jnp.float32)
    y = y.reshape(bsz, seqlen, SSD_INNER) * jax.nn.silu(z.astype(jnp.float32))
    yg = y.reshape(bsz, seqlen, SSD_GROUPS, SSD_INNER // SSD_GROUPS)
    yg = yg * lax.rsqrt(jnp.mean(yg * yg, axis=-1, keepdims=True) + 1e-6)
    y = (yg.reshape(bsz, seqlen, SSD_INNER) * norm_w.astype(jnp.float32)).astype(x.dtype)
    return jnp.einsum('bse,ed->bsd', y, w_out)

def first_inputs(seed: int = 0) -> dict:
    key = jax.random.key(seed)
    ks = jax.random.split(key, 32)
    f32 = jnp.float32
    nrm = lambda k, shape, s: jax.random.normal(k, shape, f32) * s

    x = jax.random.normal(ks[0], (BATCH, SEQ, D_MODEL), f32)
    offset = jax.random.randint(ks[1], (BATCH, 1), 0, 1024, dtype=jnp.int32)
    positions = offset + jnp.arange(SEQ, dtype=jnp.int32)[None, :]

    ab_w_in = nrm(ks[2], (N_EVEN, D_MODEL, AB_IN), D_MODEL ** -0.5)
    ab_conv_w = nrm(ks[3], (N_EVEN, CONV_WIDTH, RNN_WIDTH), CONV_WIDTH ** -0.5)
    ab_conv_b = nrm(ks[4], (N_EVEN, RNN_WIDTH), 0.02)
    ab_gate_a_w = nrm(ks[5], (N_EVEN, RNN_HEADS, RNN_HEAD_DIM, RNN_HEAD_DIM), RNN_HEAD_DIM ** -0.5)
    ab_gate_a_b = nrm(ks[6], (N_EVEN, RNN_WIDTH), 0.1)
    ab_gate_x_w = nrm(ks[7], (N_EVEN, RNN_HEADS, RNN_HEAD_DIM, RNN_HEAD_DIM), RNN_HEAD_DIM ** -0.5)
    ab_gate_x_b = nrm(ks[8], (N_EVEN, RNN_WIDTH), 0.1)
    u = jax.random.uniform(ks[9], (N_EVEN, RNN_WIDTH), f32, 0.9, 0.999)
    a0 = u ** (1.0 / RG_C)
    ab_lambda = jnp.log(a0) - jnp.log1p(-a0)
    mla_q_norm = 1.0 + nrm(ks[10], (N_EVEN, MLA_Q_RANK), 0.05)
    mla_kv_norm = 1.0 + nrm(ks[11], (N_EVEN, MLA_KV_RANK), 0.05)
    mla_w_uq = nrm(ks[12], (N_EVEN, MLA_Q_RANK, MLA_HEADS * (MLA_NOPE + MLA_ROPE)), MLA_Q_RANK ** -0.5)
    mla_w_ukv = nrm(ks[13], (N_EVEN, MLA_KV_RANK, MLA_HEADS * (MLA_NOPE + MLA_V)), MLA_KV_RANK ** -0.5)
    ab_w_out = nrm(ks[14], (N_EVEN, AB_WIDTH, D_MODEL), DN_BETA * math.sqrt(2.0 / (AB_WIDTH + D_MODEL)))
    ab_ln_g = 1.0 + nrm(ks[15], (N_EVEN, D_MODEL), 0.05)
    ab_ln_b = nrm(ks[16], (N_EVEN, D_MODEL), 0.02)

    ssd_w_in = nrm(ks[17], (N_ODD, D_MODEL, SSD_IN), D_MODEL ** -0.5)
    ssd_conv_w = nrm(ks[18], (N_ODD, CONV_WIDTH, SSD_CONV_DIM), CONV_WIDTH ** -0.5)
    ssd_conv_b = nrm(ks[19], (N_ODD, SSD_CONV_DIM), 0.02)
    dt0 = jnp.exp(jax.random.uniform(ks[20], (N_ODD, SSD_HEADS), f32, math.log(1e-3), math.log(1e-1)))
    ssd_dt_bias = dt0 + jnp.log(-jnp.expm1(-dt0))
    ssd_a_log = jnp.log(jax.random.uniform(ks[21], (N_ODD, SSD_HEADS), f32, 1.0, 16.0))
    ssd_d = 1.0 + nrm(ks[22], (N_ODD, SSD_HEADS), 0.1)
    ssd_norm = 1.0 + nrm(ks[23], (N_ODD, SSD_INNER), 0.05)
    ssd_w_out = nrm(ks[24], (N_ODD, SSD_INNER, D_MODEL), DN_BETA * math.sqrt(2.0 / (SSD_INNER + D_MODEL)))
    ssd_ln_g = 1.0 + nrm(ks[25], (N_ODD, D_MODEL), 0.05)
    ssd_ln_b = nrm(ks[26], (N_ODD, D_MODEL), 0.02)

    return {"x": x, "positions": positions,
            "ab_w_in": ab_w_in, "ab_conv_w": ab_conv_w, "ab_conv_b": ab_conv_b,
            "ab_gate_a_w": ab_gate_a_w, "ab_gate_a_b": ab_gate_a_b,
            "ab_gate_x_w": ab_gate_x_w, "ab_gate_x_b": ab_gate_x_b,
            "ab_lambda": ab_lambda, "mla_q_norm": mla_q_norm, "mla_kv_norm": mla_kv_norm,
            "mla_w_uq": mla_w_uq, "mla_w_ukv": mla_w_ukv, "ab_w_out": ab_w_out,
            "ab_ln_g": ab_ln_g, "ab_ln_b": ab_ln_b,
            "ssd_w_in": ssd_w_in, "ssd_conv_w": ssd_conv_w, "ssd_conv_b": ssd_conv_b,
            "ssd_dt_bias": ssd_dt_bias, "ssd_a_log": ssd_a_log, "ssd_d": ssd_d,
            "ssd_norm": ssd_norm, "ssd_w_out": ssd_w_out,
            "ssd_ln_g": ssd_ln_g, "ssd_ln_b": ssd_ln_b}

def first_block(x, positions, ab_w_in, ab_conv_w, ab_conv_b, ab_gate_a_w, ab_gate_a_b,
              ab_gate_x_w, ab_gate_x_b, ab_lambda, mla_q_norm, mla_kv_norm, mla_w_uq,
              mla_w_ukv, ab_w_out, ab_ln_g, ab_ln_b, ssd_w_in, ssd_conv_w, ssd_conv_b,
              ssd_dt_bias, ssd_a_log, ssd_d, ssd_norm, ssd_w_out, ssd_ln_g, ssd_ln_b):
    inv_freq = ROPE_THETA ** (-jnp.arange(0, MLA_ROPE, 2, dtype=jnp.float32) / MLA_ROPE)
    ang = positions.astype(jnp.float32)[..., None] * inv_freq
    cos = jnp.cos(ang).astype(x.dtype)
    sin = jnp.sin(ang).astype(x.dtype)
    for layer in range(DEPTH):
        j = layer // 2
        if layer % 2 == 0:
            y = _rglru_mla_layer(x, cos, sin, ab_w_in[j], ab_conv_w[j], ab_conv_b[j],
                                 ab_gate_a_w[j], ab_gate_a_b[j], ab_gate_x_w[j], ab_gate_x_b[j],
                                 ab_lambda[j], mla_q_norm[j], mla_kv_norm[j], mla_w_uq[j],
                                 mla_w_ukv[j], ab_w_out[j])
            x = _layernorm(DN_ALPHA * x + y, ab_ln_g[j], ab_ln_b[j])
        else:
            y = _ssd_layer(x, ssd_w_in[j], ssd_conv_w[j], ssd_conv_b[j], ssd_dt_bias[j],
                           ssd_a_log[j], ssd_d[j], ssd_norm[j], ssd_w_out[j])
            x = _layernorm(DN_ALPHA * x + y, ssd_ln_g[j], ssd_ln_b[j])
    return x


DEPTH_2 = 1

MIX_WIDTH = D_MODEL
ATTN_WIDTH = MIX_WIDTH // 2
SSM_WIDTH = MIX_WIDTH - ATTN_WIDTH
HEAD_DIM = 64
N_HEADS = ATTN_WIDTH // HEAD_DIM
DILATED_BRANCHES = ((128, 1), (512, 4), (2048, 16))
BLOCK = 128
SSM_GROUP = 16
N_SSM_GROUPS = SSM_WIDTH // SSM_GROUP
STATE_DIM = 64
D_FF = 2816
IN_WIDTH = 3 * ATTN_WIDTH + SSM_WIDTH
NORM_EPS = 1e-6
DT_MIN = 1e-3
DT_MAX = 1e-1


def rms_norm(x, g):
    xf = x.astype(jnp.float32)
    y = xf * lax.rsqrt(jnp.mean(xf * xf, axis=-1, keepdims=True) + NORM_EPS)
    return (y * g.astype(jnp.float32)).astype(x.dtype)

def swiglu(x, w_in, w_out):
    gate, up = jnp.split(x @ w_in, 2, axis=-1)
    return (jax.nn.silu(gate) * up) @ w_out

def alibi_slopes(n_heads):
    return 2.0 ** (-8.0 * jnp.arange(1, n_heads + 1, dtype=jnp.float32) / n_heads)

def dilated_window_branch(q, k, v, slopes, window, dilation):
    B, S, H, E = q.shape
    n_back = window // dilation
    L = -(-S // dilation)
    nb = -(-L // BLOCK)
    Lp = nb * BLOCK

    def to_blocks(t):
        t = jnp.pad(t, ((0, 0), (0, L * dilation - S), (0, 0), (0, 0)))
        t = t.reshape(B, L, dilation, H, E).transpose(0, 2, 1, 3, 4)
        t = jnp.pad(t, ((0, 0), (0, 0), (0, Lp - L), (0, 0), (0, 0)))
        return t.reshape(B, dilation, nb, BLOCK, H, E)

    def with_prev(t):
        prev = jnp.pad(t[:, :, :-1], ((0, 0), (0, 0), (1, 0), (0, 0), (0, 0), (0, 0)))
        return jnp.concatenate([prev, t], axis=3)

    def from_blocks(t):
        tail = t.shape[4:]
        t = t.reshape((B, dilation, Lp) + tail)[:, :, :L]
        t = jnp.moveaxis(t, 1, 2).reshape((B, L * dilation) + tail)
        return t[:, :S]

    qb, kb, vb = to_blocks(q), to_blocks(k), to_blocks(v)
    kk, vv = with_prev(kb), with_prev(vb)
    s = jnp.einsum('brnqhe,brnkhe->brnhqk', qb, kk) * (HEAD_DIM ** -0.5)

    qi = jnp.arange(BLOCK)[:, None]
    ci = jnp.arange(2 * BLOCK)[None, :]
    steps = BLOCK + qi - ci
    key_pos = (jnp.arange(nb)[:, None, None] - 1) * BLOCK + ci[None]
    valid = ((steps >= 0) & (steps <= n_back))[None] & (key_pos >= 0)
    dist = (steps * dilation).astype(jnp.float32)
    bias = -slopes[:, None, None] * dist[None]
    s = jnp.where(valid[None, None, :, None], s + bias, -jnp.inf)

    m = jnp.max(s, axis=-1, keepdims=True)
    p = jnp.exp(s - m)
    denom = jnp.sum(p, axis=-1, keepdims=True)
    o = jnp.einsum('brnhqk,brnkhe->brnqhe', p, vv)
    o = o * jnp.swapaxes(1.0 / denom[..., 0], -1, -2)[..., None]
    lse = jnp.swapaxes((m + jnp.log(denom))[..., 0], -1, -2)
    return from_blocks(o), from_blocks(lse)

def dilated_attention(q, k, v):
    B, S, _ = q.shape
    q, k, v = (t.astype(jnp.float32).reshape(B, S, N_HEADS, HEAD_DIM) for t in (q, k, v))
    slopes = alibi_slopes(N_HEADS)
    outs, lses = [], []
    for window, dilation in DILATED_BRANCHES:
        o, l = dilated_window_branch(q, k, v, slopes, window, dilation)
        outs.append(o)
        lses.append(l)
    w = jax.nn.softmax(jnp.stack(lses, axis=-1), axis=-1)
    o = jnp.einsum('bshn,nbshe->bshe', w, jnp.stack(outs, axis=0))
    return o.reshape(B, S, ATTN_WIDTH)

def s5_mixer(u, a_re, a_im, log_dt, b_re, b_im, c_re, c_im, d_skip, w_glu, b_glu):
    B, S, _ = u.shape
    f32 = jnp.float32
    uf = u.astype(f32).reshape(B, S, N_SSM_GROUPS, SSM_GROUP)
    dt = jnp.exp(log_dt.astype(f32))[:, None]
    a = lax.complex(a_re.astype(f32), a_im.astype(f32))
    a_bar = jnp.exp(dt * a)
    b = lax.complex(b_re.astype(f32), b_im.astype(f32))
    b_bar = ((a_bar - 1.0) / a)[..., None] * b
    bu = jnp.einsum('bsgc,gpc->bsgp', uf.astype(jnp.complex64), b_bar)
    a_seq = jnp.broadcast_to(a_bar, bu.shape)

    def combine(left, right):
        a_l, x_l = left
        a_r, x_r = right
        return a_r * a_l, a_r * x_l + x_r

    _, states = lax.associative_scan(combine, (a_seq, bu), axis=1)
    c = lax.complex(c_re.astype(f32), c_im.astype(f32))
    y = jnp.real(jnp.einsum('bsgp,gcp->bsgc', states, c))
    y = y + d_skip.astype(f32).reshape(N_SSM_GROUPS, SSM_GROUP) * uf
    y = jax.nn.gelu(y.reshape(B, S, SSM_WIDTH))
    return y * jax.nn.sigmoid(y @ w_glu.astype(f32) + b_glu.astype(f32))

def second_inputs(seed: int = 0) -> dict:
    key = jax.random.key(seed)
    ks = jax.random.split(key, 24)
    f32 = jnp.float32
    L = DEPTH_2

    def nrm(k, shape, scale):
        return jax.random.normal(k, shape, f32) * scale

    def gain(k):
        return 1.0 + 0.05 * jax.random.normal(k, (L, D_MODEL), f32)

    n_idx = jnp.arange(STATE_DIM, dtype=f32)
    a_re = -0.5 + 0.01 * jax.random.normal(ks[9], (L, N_SSM_GROUPS, STATE_DIM), f32)
    a_im = math.pi * n_idx + 0.01 * jax.random.normal(ks[10], (L, N_SSM_GROUPS, STATE_DIM), f32)
    log_dt = jax.random.uniform(ks[11], (L, N_SSM_GROUPS), f32,
                                math.log(DT_MIN), math.log(DT_MAX))
    return {
        "x": jax.random.normal(ks[0], (BATCH, SEQ, D_MODEL), f32),
        "ffn1_pre_g": gain(ks[1]),
        "ffn1_w_in": nrm(ks[2], (L, D_MODEL, 2 * D_FF), D_MODEL ** -0.5),
        "ffn1_w_out": nrm(ks[3], (L, D_FF, D_MODEL), D_FF ** -0.5),
        "ffn1_post_g": gain(ks[4]),
        "mix_pre_g": gain(ks[5]),
        "w_mix_in": nrm(ks[6], (L, D_MODEL, IN_WIDTH), D_MODEL ** -0.5),
        "a_re": a_re,
        "a_im": a_im,
        "log_dt": log_dt,
        "b_re": nrm(ks[12], (L, N_SSM_GROUPS, STATE_DIM, SSM_GROUP), (2 * SSM_GROUP) ** -0.5),
        "b_im": nrm(ks[13], (L, N_SSM_GROUPS, STATE_DIM, SSM_GROUP), (2 * SSM_GROUP) ** -0.5),
        "c_re": nrm(ks[14], (L, N_SSM_GROUPS, SSM_GROUP, STATE_DIM), (2 * STATE_DIM) ** -0.5),
        "c_im": nrm(ks[15], (L, N_SSM_GROUPS, SSM_GROUP, STATE_DIM), (2 * STATE_DIM) ** -0.5),
        "d_skip": nrm(ks[16], (L, SSM_WIDTH), 1.0),
        "w_glu": nrm(ks[17], (L, SSM_WIDTH, SSM_WIDTH), SSM_WIDTH ** -0.5),
        "b_glu": nrm(ks[18], (L, SSM_WIDTH), 0.01),
        "w_mix_out": nrm(ks[19], (L, MIX_WIDTH, D_MODEL), MIX_WIDTH ** -0.5),
        "mix_post_g": gain(ks[20]),
        "ffn2_pre_g": gain(ks[21]),
        "ffn2_w_in": nrm(ks[22], (L, D_MODEL, 2 * D_FF), D_MODEL ** -0.5),
        "ffn2_w_out": nrm(ks[23], (L, D_FF, D_MODEL), D_FF ** -0.5),
        "ffn2_post_g": gain(ks[7]),
    }

def second_block(x, ffn1_pre_g, ffn1_w_in, ffn1_w_out, ffn1_post_g, mix_pre_g, w_mix_in,
              a_re, a_im, log_dt, b_re, b_im, c_re, c_im, d_skip, w_glu, b_glu,
              w_mix_out, mix_post_g, ffn2_pre_g, ffn2_w_in, ffn2_w_out, ffn2_post_g):
    for l in range(DEPTH_2):
        h = rms_norm(x, ffn1_pre_g[l])
        x = x + 0.5 * rms_norm(swiglu(h, ffn1_w_in[l], ffn1_w_out[l]), ffn1_post_g[l])
        h = rms_norm(x, mix_pre_g[l])
        proj = h @ w_mix_in[l]
        q, k, v, u = jnp.split(proj, [ATTN_WIDTH, 2 * ATTN_WIDTH, 3 * ATTN_WIDTH], axis=-1)
        attn = dilated_attention(q, k, v).astype(x.dtype)
        ssm = s5_mixer(u, a_re[l], a_im[l], log_dt[l], b_re[l], b_im[l], c_re[l], c_im[l],
                       d_skip[l], w_glu[l], b_glu[l]).astype(x.dtype)
        mixed = jnp.concatenate([attn, ssm], axis=-1) @ w_mix_out[l]
        x = x + rms_norm(mixed, mix_post_g[l])
        h = rms_norm(x, ffn2_pre_g[l])
        x = x + 0.5 * rms_norm(swiglu(h, ffn2_w_in[l], ffn2_w_out[l]), ffn2_post_g[l])
    return x


def setup_inputs(seed=0):
    out = dict(first_inputs(seed))
    for name, value in second_inputs(seed + 1).items():
        if name != "x":
            out[name + "_2"] = value
    return out


def reference(
    x, positions, ab_w_in, ab_conv_w, ab_conv_b, ab_gate_a_w, ab_gate_a_b, ab_gate_x_w,
    ab_gate_x_b, ab_lambda, mla_q_norm, mla_kv_norm, mla_w_uq, mla_w_ukv, ab_w_out, ab_ln_g,
    ab_ln_b, ssd_w_in, ssd_conv_w, ssd_conv_b, ssd_dt_bias, ssd_a_log, ssd_d, ssd_norm,
    ssd_w_out, ssd_ln_g, ssd_ln_b, ffn1_pre_g_2, ffn1_w_in_2, ffn1_w_out_2, ffn1_post_g_2,
    mix_pre_g_2, w_mix_in_2, a_re_2, a_im_2, log_dt_2, b_re_2, b_im_2, c_re_2, c_im_2, d_skip_2,
    w_glu_2, b_glu_2, w_mix_out_2, mix_post_g_2, ffn2_pre_g_2, ffn2_w_in_2, ffn2_w_out_2,
    ffn2_post_g_2,
):
    x = first_block(
        x, positions, ab_w_in, ab_conv_w, ab_conv_b, ab_gate_a_w, ab_gate_a_b, ab_gate_x_w,
        ab_gate_x_b, ab_lambda, mla_q_norm, mla_kv_norm, mla_w_uq, mla_w_ukv, ab_w_out, ab_ln_g,
        ab_ln_b, ssd_w_in, ssd_conv_w, ssd_conv_b, ssd_dt_bias, ssd_a_log, ssd_d, ssd_norm,
        ssd_w_out, ssd_ln_g, ssd_ln_b,
    )
    return second_block(
        x, ffn1_pre_g_2, ffn1_w_in_2, ffn1_w_out_2, ffn1_post_g_2, mix_pre_g_2, w_mix_in_2,
        a_re_2, a_im_2, log_dt_2, b_re_2, b_im_2, c_re_2, c_im_2, d_skip_2, w_glu_2, b_glu_2,
        w_mix_out_2, mix_post_g_2, ffn2_pre_g_2, ffn2_w_in_2, ffn2_w_out_2, ffn2_post_g_2,
    )


_drawn_inputs = setup_inputs


def setup_inputs(seed=0):
    import zlib

    import numpy as np

    out = dict(_drawn_inputs(seed))
    spreads = {}
    factors = {'ab_conv_b': 2.693,
     'ab_gate_a_b': 8.0,
     'ab_gate_x_b': 8.0,
     'mla_q_norm': 8.0,
     'mla_kv_norm': 8.0,
     'ssd_conv_b': 4.148,
     'a_re_2': 200.0,
     'b_glu_2': 23.167,
     'ffn2_post_g_2': 3.542,
     'a_im_2': 33.296,
     'log_dt_2': 37.944,
     'b_re_2': 45.32,
     'b_im_2': 46.936,
     'c_re_2': 45.472,
     'c_im_2': 46.256}
    for name, (base, spread) in spreads.items():
        noise = np.random.default_rng([zlib.crc32(name.encode()), seed]).standard_normal(out[name].shape)
        drawn = base * np.exp(spread * noise) if base else spread * noise
        out[name] = __import__('jax').numpy.asarray(drawn.astype(out[name].dtype))
    for name, factor in factors.items():
        out[name] = (out[name] * factor).astype(out[name].dtype)
    return out
```

```python
import math
from contextlib import ExitStack

import numpy as np

import concourse.bass as bass
from concourse import mybir

F32 = mybir.dt.float32
F32R = mybir.dt.float32r
I32 = mybir.dt.int32
ALU = mybir.AluOpType
ACT = mybir.ActivationFunctionType
AX_X = mybir.AxisListType.X

P = 128
SEQ = 1024
D = 1024
KT = D // P
TT = SEQ // P
HALF = 512

RNN = 512
MLA_HEADS, NOPE, ROPE, MLA_V = 8, 64, 32, 64
Q_RANK, KV_RANK = 256, 128
AB_IN = RNN + 1024 + Q_RANK + KV_RANK + ROPE
MLA_SCALE = (NOPE + ROPE) ** -0.5
DN_ALPHA = 4.0 ** 0.25

SSD_INNER, SSD_HEADS, SSD_GROUPS, SSD_P = 2048, 32, 4, 64
HPG = SSD_HEADS // SSD_GROUPS
GW = SSD_INNER // SSD_GROUPS
SSD_CONV = SSD_INNER + 2 * SSD_GROUPS * P

D_FF = 2816
FT = D_FF // P
FFN_PARTS = (8, 7, 7)
ATT_HEADS, HD = 8, 64
NEG = -1.0e30

S5_GROUPS, S5_STATE, S5_CH = 32, 64, 16
S5_T = 8
S5_N = SEQ // S5_T
S5_Q = S5_GROUPS // 2

B_IN = 0
B_OUT = B_IN + 16
B_DT = B_OUT + KT
B_SSD = B_DT + 1
SSD_BLOCKS = 18
B_FFN1 = B_SSD + SSD_GROUPS * SSD_BLOCKS
FFN_BLOCKS = 2 * FT + KT * len(FFN_PARTS)
B_MIX = B_FFN1 + FFN_BLOCKS
B_GLU = B_MIX + 16
B_MIXOUT = B_GLU + 4
B_FFN2 = B_MIXOUT + KT
B_END = B_FFN2 + FFN_BLOCKS

VEC = {}


def _vec_layout():
    at = 0
    for name, n in (("conv_w", 16), ("conv_b", 4), ("ga_b", 4), ("gx_b", 4), ("lam", 4), ("qn", 2), ("kvn", 1),
                    ("ln1_g", 8), ("ln1_b", 8), ("ssd", SSD_GROUPS * 34), ("ln2_g", 8), ("ln2_b", 8),
                    ("f1_pre", 8), ("f1_post", 8), ("m_pre", 8), ("m_post", 8), ("f2_pre", 8), ("f2_post", 8),
                    ("dsk", 4), ("bglu", 4), ("dtb", 32), ("alog", 32), ("ssd_d", 32)):
        VEC[name] = (at, n)
        at += n
    return at


VEC_COLS = _vec_layout()


class Steps:

    def __init__(self, eng, sem):
        self.eng, self.sem, self.n, self.i, self.per = eng, sem, 0, None, 0

    def __call__(self, ins):
        self.n += 1
        ins.then_inc(self.sem, 1)
        return self.n

    def wait(self, mark=None):
        k = self.n if mark is None else mark
        self.eng.wait_ge(self.sem, k if self.i is None else k + self.i * self.per)

    def link(self, ins):
        self(ins)
        self.wait()

    def enter(self, i, per):
        self.i, self.per, self.start = i, per, self.n

    def leave(self, turns):
        assert self.n - self.start == self.per, (self.n - self.start, self.per)
        self.n, self.i = self.start + turns * self.per, None


def build(nc, ins, out):
    ctx = ExitStack()
    with ctx:
        _build(nc, ctx, ins, out)


def _build(nc, ctx, ins, out):
    sems = {}

    def sem(name):
        if name not in sems:
            sems[name] = ctx.enter_context(nc.semaphore(name))
        return sems[name]

    base = 16512
    def at(name, kib, shape, dt=F32):
        return nc.alloc_sbuf_tensor_at(name, shape, dt, offset=base + int(kib * 1024))

    WS = at("WS", 0, [P, 2, 1024])
    WH = at("WH", 8, [P, 2, 1024], F32R)
    WL = at("WL", 16, [P, 2, 1024], F32R)
    IDENT = at("IDENT", 24, [P, P])
    ONES = at("ONES", 24.5, [P, P])
    GT = at("GT", 25, [P, P])
    LE = at("LE", 25.5, [P, P])
    CMASK = at("CMASK", 26, [P, P])
    VT = at("VT", 26.5, [P, VEC_COLS])
    SM = at("SM", 28.25, [P, 320])
    GV = at("GV", 29.5, [P, 34])
    EP = at("EP", 29.65625, [P, 24])
    EDX = at("EDX", 29.75, [P, TT, SSD_HEADS])
    CDEC = at("CDEC", 30.75, [P, TT, SSD_HEADS])
    ACC = at("ACC", 32, [P, KT, SEQ])
    XH = at("XH", 64, [P, KT, SEQ], F32R)
    XL = at("XL", 96, [P, KT, SEQ], F32R)
    HH = at("HH", 128, [P, KT, SEQ], F32R)
    HL = at("HL", 160, [P, KT, SEQ], F32R)
    T = [at(f"T{k}", 192 + 4 * k, [P, SEQ]) for k in range(3)]
    DTT = at("DTT", 204, [P, TT, SSD_HEADS])
    ADT = at("ADT", 205, [P, TT, SSD_HEADS])
    ECS = at("ECS", 206, [P, TT, SSD_HEADS])
    XIN = at("XIN", 128, [P, TT, D])
    G = at("G", 128, [P, KT, SEQ])
    Y = at("Y", 160, [P, KT, SEQ])
    RG = [at(f"RG{k}", 64 + 16 * k, [P, 4, SEQ]) for k in range(4)]
    BD = at("BD", 112, [P, 2, 4, P])
    NB = [at(f"NB{k}", 116 + 4 * k, [P, SEQ]) for k in range(3)]
    POSI = at("POSI", 200, [P, SEQ], I32)
    QT = at("QT", 64, [P, 2, SEQ])
    KTT = at("KTT", 72, [P, 2, SEQ])
    VTOK = at("VTOK", 80, [P, TT, 512])
    PP = at("PP", 96, [P, 2, SEQ])
    PT = at("PT", 104, [P, 2, SEQ])
    YTOK = at("YTOK", 112, [P, TT, 512])
    WUQ = at("WUQ", 204, [P, 2, 2, P])
    WUKV = at("WUKV", 200, [P, 1024])
    WK = at("WK", 206, [P, 2, NOPE])
    COS = at("COS", 192, [P, SEQ])
    SIN = at("SIN", 196, [P, SEQ])
    YGH = at("YGH", 128, [P, 4, SEQ], F32R)
    YGL = at("YGL", 144, [P, 4, SEQ], F32R)
    XST = at("XST", 128, [P, 4, SEQ])
    SYT = at("SYT", 128, [P, TT, GW])
    BT = at("BT", 144, [P, SEQ])
    CT = at("CT", 148, [P, SEQ])
    BTOK = at("BTOK", 152, [P, TT, P])
    PREV = at("PREV", 156, [P, GW])
    YOS = at("YOS", 158, [P, GW])
    ZT = at("ZT", 160, [P, 4, SEQ])
    XTOK = at("XTOK", 176, [P, TT, GW])
    SEGR = at("SEGR", 192, [P, HPG, P])
    DEC = at("DEC", 196, [P, HPG, P])
    XDT = at("XDT", 200, [P, GW])
    XDD = at("XDD", 202, [P, GW])
    CBM = at("CBM", 26, [P, P])
    MQ = at("MQ", 128, [P, 4, SEQ])
    MK = at("MK", 144, [P, 4, SEQ])
    MV = at("MV", 160, [P, TT, 512])
    MU = at("MU", 176, [P, 4, SEQ])
    DIST = at("DIST", 192, [P, SEQ])
    LOGC = at("LOGC", 196, [P, SEQ])
    BIAS = at("BIAS", 200, [P, SEQ])
    UG = at("UG", 64, [P, S5_GROUPS, P])
    GP = at("GP", 64, [P, 2, S5_Q, P])
    TOE = at("TOE", 80, [P, S5_GROUPS, P])
    GIN = at("GIN", 96, [P, S5_Q, 2, P])
    RMT = at("RMT", 96, [P, S5_Q, S5_N])
    TMP = at("TMP", 104, [P, S5_Q, S5_N])
    CA = at("CA", 112, [P, 2, S5_Q, S5_T + 1, S5_CH])
    RE = at("RE", 130, [P, S5_Q, S5_N])
    RI = at("RI", 138, [P, S5_Q, S5_N])
    SR = at("SR", 146, [P, S5_Q, S5_N])
    SI = at("SI", 154, [P, S5_Q, S5_N])
    K0S = at("K0S", 146, [P, S5_GROUPS, P])
    VR = at("VR", 48, [P, S5_Q, S5_N])
    VI = at("VI", 56, [P, S5_Q, S5_N])
    CTMP = at("CTMP", 48, [P, S5_Q, S5_T + 1, S5_CH])
    PW = at("PW", 192, [P, 2, S5_T + 1, S5_Q])
    BB = at("BB", 193.5, [P, 2, S5_Q, S5_CH])
    CC = at("CC", 195.5, [P, 2, S5_Q, S5_CH])
    BR = at("BR", 197.5, [P, 2, S5_Q, S5_CH])
    BTMP = at("BTMP", 199.5, [P, S5_Q, S5_CH])
    CN = at("CN", 200.5, [P, 2, 4, S5_STATE])
    S5Y = at("S5Y", 64, [P, 4, SEQ])
    ZH = at("ZH", 128, [P, 4, SEQ], F32R)
    ZL = at("ZL", 144, [P, 4, SEQ], F32R)
    RL = at("RL", 128, [P, KT, SEQ])

    PS = [ctx.enter_context(nc.psum_tensor(f"PS{k}", [P, 1024], F32)) for k in range(2)]
    PA = ctx.enter_context(nc.psum_tensor("PA", [P, 1024], F32))
    PB = ctx.enter_context(nc.psum_tensor("PB", [P, 1024], F32))

    XRES = nc.dram_tensor("x_residual", [KT, P, SEQ], F32, kind="Internal").ap()

    def vec(name, k=0, n=1):
        a = VEC[name][0] + k
        return VT[:, a:a + n]

    W_LOADED = [sem(f"w_loaded{s}") for s in range(2)]
    W_HI = [sem(f"w_hi{s}") for s in range(2)]
    W_LO = [sem(f"w_lo{s}") for s in range(2)]
    BLOCK_DONE = [sem(f"block_done{s}") for s in range(2)]
    PS_READ = [sem(f"ps_read{s}") for s in range(2)]

    def times(b, i=None, per=0):
        n = b // 2 + 1
        return n if i is None else n + i * (per // 2)

    def load_block(sp, b, src, cols=1024, i=None, per=0, kt=KT, view=None):
        s, n = b % 2, times(b, i, per)
        if i is not None or n > 1:
            sp.wait_ge(W_LO[s], n - 1)
        for dst, part in (view(WS[:, s]) if view else [(WS[:, s, 0:cols].rearrange("p (k c) -> p k c", k=kt), src)]):
            sp.dma_start(dst, part).then_inc(W_LOADED[s], 16)

    def split_hi(act, b, i=None, per=0, cols=1024):
        if b >= B_END:
            return
        s, n = b % 2, times(b, i, per)
        act.wait_ge(W_LOADED[s], load_count(b, i, per))
        if i is not None or n > 1:
            act.wait_ge(BLOCK_DONE[s], n - 1)
        nc.scalar.activation(WH[:, s, 0:cols], WS[:, s, 0:cols], ACT.Copy).then_inc(W_HI[s], 1)

    def split_lo(dve, b, i=None, per=0, cols=1024):
        if b >= B_END:
            return
        s, n = b % 2, times(b, i, per)
        dve.wait_ge(W_HI[s], n)
        nc.vector.tensor_tensor(WL[:, s, 0:cols], WS[:, s, 0:cols], WH[:, s, 0:cols].bitcast(F32),
                                ALU.subtract).then_inc(W_LO[s], 1)

    KR_BLOCK = B_IN + 15
    KR_DMAS = 8

    def load_count(b, i=None, per=0):
        n = 16 * (b // 2 + 1)
        if b >= KR_BLOCK and b % 2 == KR_BLOCK % 2:
            n += 16 * (KR_DMAS - 1)
        return n if i is None else n + i * (8 * per)

    def block_products(pe, b, hi, lo, kt=KT, i=None, per=0, after=None, width=P):
        s, n = b % 2, times(b, i, per)
        pe.wait_ge(W_LO[s], n)
        if i is not None or n > 1:
            pe.wait_ge(PS_READ[s], n - 1)
        for k in range(kt):
            if after:
                after(k)
            terms = [(WH, hi), (WH, lo), (WL, hi)]
            for j, (w, x) in enumerate(terms):
                for h in range(2):
                    last = nc.tensor.matmul(PS[s][:, h * HALF:(h + 1) * HALF], w[:, s, k * width:(k + 1) * width],
                                            x[:, k, h * HALF:(h + 1) * HALF],
                                            start=(k == 0 and j == 0), stop=(k == kt - 1 and j == 2))
        last.then_inc(BLOCK_DONE[s], 1)

    def token_products(pe, b, i=None, per=0, n_cols=P):
        s, n = b % 2, times(b, i, per)
        pe.wait_ge(W_LO[s], n)
        if i is not None or n > 1:
            pe.wait_ge(PS_READ[s], n - 1)
        for t in range(TT):
            o = PS[s][:, t * P:t * P + n_cols]
            for k in range(KT):
                for j, (x, w) in enumerate(((XH, WH), (XH, WL), (XL, WH))):
                    last = nc.tensor.matmul(o, x[:, k, t * P:(t + 1) * P], w[:, s, k * n_cols:(k + 1) * n_cols],
                                            start=(k == 0 and j == 0), stop=(k == KT - 1 and j == 2))
        last.then_inc(BLOCK_DONE[s], 1)

    SQ, SUMMED, ROWSUM, RSTD, MEAN_USED = (sem(n) for n in ("squares", "squares_summed", "row_sums", "rstd", "mean_used"))
    MSUM, MROW = sem("mean_summed"), sem("mean_row_sums")
    NORM = {}
    at_sq = 0
    for name, kts in (("q", 2), ("kv", 1), ("ln1", 8), ("g0", 4), ("g1", 4), ("g2", 4), ("g3", 4), ("ln2", 8),
                      ("f1pre", 8), ("f1post", 8), ("mpre", 8), ("mpost", 8), ("f2pre", 8), ("f2post", 8)):
        NORM[name] = (len(NORM), at_sq, kts)
        at_sq += kts

    def norm_squares(act, name, x, wait=None, i=None, bufs=T):
        turn, sq0, kts = NORM[name]
        d_turn, d_sq = (0, 0) if i is None else (i, i * kts)
        for k in range(kts):
            if wait:
                wait(k)
            if k >= 2:
                act.wait_ge(SUMMED, sq0 + k - 1 + d_sq)
            nc.scalar.activation(bufs[k % 2][:], x(k), ACT.Square).then_inc(SQ, 1)

    def norm_rstd(act, steps, name, n, eps, i=None, bufs=T):
        turn, sq0, kts = NORM[name]
        d_turn = 0 if i is None else i
        act.wait_ge(ROWSUM, turn + 1 + d_turn)
        steps.link(nc.scalar.activation(bufs[0][:], PA[:], ACT.Ln, bias=EP[:, eps:eps + 1], scale=1.0 / n))
        nc.scalar.activation(bufs[1][:], bufs[0][:], ACT.Exp, scale=-0.5).then_inc(RSTD, 1)

    def norm_sum(dve, name, i=None, bufs=T):
        turn, sq0, kts = NORM[name]
        d_sq = 0 if i is None else i * kts
        for k in range(kts):
            dve.wait_ge(SQ, sq0 + k + 1 + d_sq)
            if k == 0:
                nc.vector.tensor_copy(bufs[2][:], bufs[0][:]).then_inc(SUMMED, 1)
            else:
                dve.wait_ge(SUMMED, sq0 + k + d_sq)
                nc.vector.tensor_tensor(bufs[2][:], bufs[2][:], bufs[k % 2][:], ALU.add).then_inc(SUMMED, 1)

    def norm_rows(pe, name, i=None, bufs=T):
        turn, sq0, kts = NORM[name]
        d_sq = 0 if i is None else i * kts
        pe.wait_ge(SUMMED, sq0 + kts + d_sq)
        for h in range(2):
            last = nc.tensor.matmul(PA[:, h * HALF:(h + 1) * HALF], ONES[:], bufs[2][:, h * HALF:(h + 1) * HALF],
                                    start=True, stop=True)
        last.then_inc(ROWSUM, 1)

    X_OK = sem("x_parts")
    CONST, VECS = sem("constants"), sem("vectors_loaded")
    EPS6, EPS5 = 0, 1

    def const_pool(pool, st):
        ms = nc.gpsimd.memset
        for tile in (IDENT, CMASK):
            st(ms(tile[:], 0.0))
        st(ms(ONES[:], 1.0))
        st(ms(SM[:], 0.0))
        st(ms(EP[:, 0:1], 1e-6))
        st(ms(EP[:, 1:2], 1e-5))
        st(ms(EP[:, 2:3], 0.5))
        st.wait()
        sel = nc.gpsimd.affine_select
        st(sel(out=IDENT[:], in_=IDENT[:], compare_op=ALU.not_equal, fill=1.0, base=0, pattern=[[-1, P]], channel_multiplier=1))
        st(sel(out=CMASK[:], in_=CMASK[:], compare_op=ALU.is_ge, fill=NEG, base=0, pattern=[[-1, P]], channel_multiplier=1))
        st(sel(out=GT[:], in_=ONES[:], compare_op=ALU.is_gt, fill=0.0, base=0, pattern=[[-1, P]], channel_multiplier=1))
        st(sel(out=LE[:], in_=ONES[:], compare_op=ALU.is_ge, fill=0.0, base=0, pattern=[[1, P]], channel_multiplier=-1))
        for k in range(ROPE // 2):
            f = float(np.float32(10000.0) ** np.float32(-2.0 * k / ROPE))
            for half, sign in ((0, -1.0), (1, 1.0)):
                c = NOPE + 16 * half + k
                st(ms(SM[0:1, c:c + 1], f))
                st(ms(SM[0:1, P + c:P + c + 1], sign))
        st.wait()
        ms(EP[:, 20:21], 0.0).then_inc(CONST, 1)


    def vec_loads():
        rows = lambda a: a.rearrange("(k p) -> p k", p=P)
        yield vec("conv_w", 0, 16).rearrange("p (t k) -> p t k", k=4), ins["ab_conv_w"][0].rearrange("k (t p) -> p t k", p=P)
        for name, src in (("conv_b", "ab_conv_b"), ("ga_b", "ab_gate_a_b"), ("gx_b", "ab_gate_x_b"), ("lam", "ab_lambda"),
                          ("qn", "mla_q_norm"), ("kvn", "mla_kv_norm"), ("ln1_g", "ab_ln_g"), ("ln1_b", "ab_ln_b"),
                          ("ln2_g", "ssd_ln_g"), ("ln2_b", "ssd_ln_b"), ("f1_pre", "ffn1_pre_g_2"),
                          ("f1_post", "ffn1_post_g_2"), ("m_pre", "mix_pre_g_2"), ("m_post", "mix_post_g_2"),
                          ("f2_pre", "ffn2_pre_g_2"), ("f2_post", "ffn2_post_g_2"), ("dsk", "d_skip_2"), ("bglu", "b_glu_2")):
            yield vec(name, 0, VEC[name][1]), rows(ins[src][0])
        for g in range(SSD_GROUPS):
            for c0, n, ch in ((0, 4, g * GW), (4, 1, SSD_INNER + g * P), (5, 1, SSD_INNER + SSD_GROUPS * P + g * P)):
                yield (vec("ssd", 34 * g + 4 * c0, 4 * n).rearrange("p (t k) -> p t k", k=4),
                       ins["ssd_conv_w"][0][:, ch:ch + n * P].rearrange("k (t p) -> p t k", p=P))
                yield vec("ssd", 34 * g + 24 + c0, n), rows(ins["ssd_conv_b"][0][ch:ch + n * P])
            yield vec("ssd", 34 * g + 30, 4), rows(ins["ssd_norm"][0][g * GW:(g + 1) * GW])
        for name, src in (("dtb", "ssd_dt_bias"), ("alog", "ssd_a_log"), ("ssd_d", "ssd_d")):
            yield vec(name, 0, SSD_HEADS), ins[src].broadcast_to([P, SSD_HEADS])


    def vecs_sync(eng):
        for dst, src in vec_loads():
            parts = [(dst, src)]
            if len(dst.shape) == 3:
                parts = [(dst[:, t], src[:, t]) for t in range(dst.shape[1])]
            for d, s in parts:
                eng.dma_start(d, s, allow_slow_non_contiguous=True).then_inc(VECS, 16)
        eng.dma_start(POSI[NOPE:NOPE + ROPE, :], ins["positions"].broadcast_to([ROPE, SEQ])).then_inc(VECS, 16)

    N_VECS = 16 * (sum(d.shape[1] if len(d.shape) == 3 else 1 for d, _ in vec_loads()) + 1)

    XLD = [sem(f"x_tile_loaded{s}") for s in range(TT)]
    XTURNED, XHI, XCOP = sem("x_tile_turned"), sem("x_tile_hi"), sem("x_tile_copied")
    PAB = (PA, PB)

    def x_sync(sp):
        for t in range(TT):
            sp.dma_start(XIN[:, t], ins["x"][0, t * P:(t + 1) * P, :]).then_inc(XLD[t], 16)

    def x_tensor(pe):
        pe.wait_ge(CONST, 1)
        for t in range(TT):
            pe.wait_ge(XLD[t], 16)
            if t >= 2:
                pe.wait_ge(X_OK, t - 1)
            for k in range(KT):
                last = nc.tensor.transpose(PAB[t % 2][:, k * P:(k + 1) * P], XIN[:, t, k * P:(k + 1) * P], IDENT[:])
            last.then_inc(XTURNED, 1)

    def x_scalar(act):
        for t in range(TT):
            act.wait_ge(XCOP, t + 1)
            nc.scalar.activation(XH[:, :, t * P:(t + 1) * P], ACC[:, :, t * P:(t + 1) * P], ACT.Copy).then_inc(XHI, 1)

    def x_vector(dve, st):
        for t in range(TT):
            tok = slice(t * P, (t + 1) * P)
            dve.wait_ge(XTURNED, t + 1)
            nc.vector.tensor_copy(ACC[:, :, tok], PAB[t % 2][:].rearrange("p (k c) -> p k c", k=KT)).then_inc(XCOP, 1)
            dve.wait_ge(XHI, t + 1)
            nc.vector.tensor_tensor(XL[:, :, tok], ACC[:, :, tok], XH[:, :, tok].bitcast(F32), ALU.subtract).then_inc(X_OK, 1)
            dve.wait_ge(X_OK, t + 1)
            st(nc.vector.tensor_scalar(ACC[:, :, tok], ACC[:, :, tok], DN_ALPHA, None, ALU.mult))

    MAGIC, INV2PI = 12582912.0, 1.0 / (2.0 * math.pi)
    C1 = 6.28125
    C2 = float(np.float32(np.floor((2 * math.pi - C1) * 2 ** 20) / 2 ** 20))
    C3 = float(np.float32(2 * math.pi - C1 - C2))
    PI_LOW = 3.1415925

    def wrap(st, r, k, x, turns):
        v = nc.vector
        st.link(v.tensor_scalar(k, x, INV2PI, turns, ALU.mult, ALU.add))
        st.link(v.tensor_scalar(k, k, MAGIC, None, ALU.add))
        st.link(v.tensor_scalar(k, k, -MAGIC, None, ALU.add))
        st.link(v.scalar_tensor_tensor(r, k, -C1, x, ALU.mult, ALU.add))
        st.link(v.scalar_tensor_tensor(r, k, -C2, r, ALU.mult, ALU.add))
        st.link(v.scalar_tensor_tensor(r, k, -C3, r, ALU.mult, ALU.add))
        st.link(v.tensor_scalar(r, r, 2 * math.pi * turns, PI_LOW, ALU.add, ALU.min))
        st.link(v.tensor_scalar(r, r, -PI_LOW, None, ALU.max))

    def log1p_exp(st, q, s, e):
        v = nc.vector
        st.link(v.tensor_scalar(q, e, 2.0, None, ALU.add))
        st.link(v.reciprocal(s, q))
        st.link(v.tensor_tensor(s, s, e, ALU.mult))
        st.link(v.tensor_tensor(e, s, s, ALU.mult))
        st.link(v.tensor_scalar(q, e, 1.0 / 19, None, ALU.mult))
        for k in range(8, 0, -1):
            st.link(v.scalar_tensor_tensor(q, q, 1.0 / (2 * k + 1), e, ALU.add, ALU.mult))
        st.link(v.scalar_tensor_tensor(q, q, 1.0, s, ALU.add, ALU.mult))
        st.link(v.tensor_scalar(q, q, 2.0, None, ALU.mult))

    ROPE_F, ROPE_R, SWAP1, KR_OK = sem("rope_columns"), sem("rope_angles"), sem("rope_swapped"), sem("k_rope")
    TRIG = sem("rope_tables")
    LAM_ABS, LAM_EXP = sem("lambda_abs"), sem("lambda_exp")
    RR = slice(NOPE, NOPE + ROPE)
    RS_ = slice(NOPE + ROPE, P)
    w_ab = ins["ab_w_in"][0].rearrange("(k p) c -> p k c", p=P)

    def in1_cols(j):
        return j * P if j < 4 else (RNN + (j - 4) * P if j < 12 else RNN + 1024 + (j - 12) * P)

    def kr_view(ws):
        w = ws.rearrange("p (k c) -> p k c", k=KT)
        c0 = AB_IN - ROPE
        for r in range(4):
            for half in range(2):
                src = c0 + 16 * (half if r % 2 == 0 else 1 - half)
                yield w[:, :, 32 * r + 16 * half:32 * r + 16 * half + 16], w_ab[:, :, src:src + 16]

    def in1_sync(sp):
        for j in range(15):
            load_block(sp, B_IN + j, w_ab[:, :, in1_cols(j):in1_cols(j) + P])
        load_block(sp, KR_BLOCK, None, view=kr_view)

    def rope_tensor(pe):
        pe.wait_ge(X_OK, TT)
        nc.tensor.matmul(PB[:, 0:1], SM[0:1, 0:P], ONES[0:1, 0:1], start=True, stop=True)
        nc.tensor.matmul(PB[:, 1:2], SM[0:1, P:2 * P], ONES[0:1, 0:1], start=True, stop=True).then_inc(ROPE_F, 1)

    def rope_vector(dve, st):
        v = nc.vector
        dve.wait_ge(ROPE_F, 1)
        st.link(v.tensor_copy(SM[:, 300:302], PB[:, 0:2]))
        dve.wait_ge(VECS, N_VECS)
        st.link(v.tensor_copy(COS[RR], POSI[RR]))
        st.link(v.tensor_scalar(T[2][RR], COS[RR], SM[RR, 300:301], None, ALU.mult))
        wrap(st, SIN[RR], PB[RR], T[2][RR], 0.0)
        wrap(st, COS[RR], PB[RR], T[2][RR], 0.25)
        v.tensor_copy(SM[:, 302:303], SM[:, 301:302]).then_inc(ROPE_R, 1)
        dve.wait_ge(TRIG, 1)
        st.link(v.tensor_scalar(SIN[RR], SIN[RR], SM[RR, 301:302], None, ALU.mult))
        for name in ("f1_post", "f2_post"):
            st.link(v.tensor_scalar(vec(name, 0, 8), vec(name, 0, 8), 0.5, None, ALU.mult))
        lam = vec("lam", 0, 4)
        st.link(v.tensor_scalar(SM[:, 256:260], lam, -1.0, None, ALU.mult))
        v.tensor_tensor(SM[:, 260:264], SM[:, 256:260], lam, ALU.max).then_inc(LAM_ABS, 1)
        dve.wait_ge(LAM_EXP, 1)
        log1p_exp(st, SM[:, 264:268], SM[:, 268:272], SM[:, 272:276])
        st.link(v.tensor_scalar(SM[:, 256:260], SM[:, 256:260], 0.0, None, ALU.max))
        st.link(v.tensor_tensor(SM[:, 264:268], SM[:, 264:268], SM[:, 256:260], ALU.add))
        st.link(v.tensor_scalar(SM[:, 264:268], SM[:, 264:268], -8.0, None, ALU.mult))

    def rope_scalar(act):
        act.wait_ge(ROPE_R, 1)
        nc.scalar.activation(COS[RR], COS[RR], ACT.Sin)
        nc.scalar.activation(SIN[RR], SIN[RR], ACT.Sin).then_inc(TRIG, 1)
        act.wait_ge(LAM_ABS, 1)
        nc.scalar.activation(SM[:, 272:276], SM[:, 260:264], ACT.Exp, scale=-1.0).then_inc(LAM_EXP, 1)

    def conv(st, dst, b, taps, bias, last_sem):
        v, src = nc.vector, PS[b % 2]
        st.link(v.tensor_scalar(dst, src[:], taps(3), bias, ALU.mult, ALU.add))
        for d in range(1, 4):
            i_ = v.scalar_tensor_tensor(dst[:, d:], src[:, :SEQ - d], taps(3 - d), dst[:, d:], ALU.mult, ALU.add)
            if d < 3:
                st.link(i_)
        i_.then_inc(last_sem, 1)

    def in1_tensor(pe):
        for j in range(16):
            block_products(pe, B_IN + j, XH, XL)

    def in1_scalar(act):
        for j in range(16):
            b = B_IN + j
            if 4 <= j < 12:
                act.wait_ge(BLOCK_DONE[b % 2], times(b))
                nc.scalar.activation(G[:, j - 4], PS[b % 2][:], ACT.Silu).then_inc(PS_READ[b % 2], 1)
            if j == 15:
                act.wait_ge(BLOCK_DONE[b % 2], times(b))
                act.wait_ge(ROPE_R, 1)
                nc.scalar.activation(T[2][RR], PS[b % 2][RS_], ACT.Copy).then_inc(SWAP1, 1)
            split_hi(act, b + 2)

    def in1_vector(dve, st):
        for j in range(16):
            b = B_IN + j
            if not 4 <= j < 12:
                dve.wait_ge(BLOCK_DONE[b % 2], times(b))
            if j < 4:
                conv(st, Y[:, j], b, lambda k: vec("conv_w", 4 * j + k), vec("conv_b", j), PS_READ[b % 2])
            elif 12 <= j < 15:
                nc.vector.tensor_copy(Y[:, j - 8], PS[b % 2][:]).then_inc(PS_READ[b % 2], 1)
            elif j == 15:
                st(nc.vector.tensor_tensor(Y[RR, 7], PS[b % 2][RR], COS[RR], ALU.mult))
                dve.wait_ge(SWAP1, 1)
                st.link(nc.vector.tensor_tensor(T[2][RR], T[2][RR], SIN[RR], ALU.mult))
                nc.vector.tensor_tensor(Y[RR, 7], Y[RR, 7], T[2][RR], ALU.add).then_inc(PS_READ[b % 2], 1)
            split_lo(dve, b + 2)

    BDZ, BDL = sem("gate_weights_zeroed"), sem("gate_weights_loaded")
    RGP, RGS, RGA, RGW, RGM, RGU = (sem(n) for n in ("rg_products", "rg_gates", "rg_decays", "rg_squares", "rg_roots", "rg_scanned"))
    RGR, RGI, RGAA = RG[0], RG[1], RG[2]

    def rg_pool(pool):
        pool.wait_ge(BLOCK_DONE[KR_BLOCK % 2], times(KR_BLOCK))
        nc.gpsimd.memset(BD[:], 0.0).then_inc(BDZ, 1)

    def rg_loads(sp):
        sp.wait_ge(BDZ, 1)
        for k, name in enumerate(("ab_gate_a_w", "ab_gate_x_w")):
            w = ins[name][0].rearrange("(t r) i j -> r i t j", r=2)
            for r in range(2):
                sp.dma_start(BD[64 * r:64 * r + 64, k, :, 64 * r:64 * r + 64], w[r]).then_inc(BDL, 16)

    def rg_tensor(pe):
        pe.wait_ge(BDL, 64)
        pe.wait_ge(RSTD, 2)
        for t in range(4):
            if t:
                pe.wait_ge(RGS, 2 * t)
            for k in range(2):
                for h in range(2):
                    last = nc.tensor.matmul(PAB[k][:, h * HALF:(h + 1) * HALF], BD[:, k, t], Y[:, t, h * HALF:(h + 1) * HALF],
                                            start=True, stop=True)
                last.then_inc(RGP, 1)

    def rg_scalar(act):
        for t in range(4):
            for k, (dst, b) in enumerate(((RGR, "ga_b"), (RGI, "gx_b"))):
                act.wait_ge(RGP, 2 * t + k + 1)
                nc.scalar.activation(dst[:, t], PAB[k][:], ACT.Sigmoid, bias=vec(b, t)).then_inc(RGS, 1)
        act.wait_ge(RGS, 8)
        for t in range(4):
            c = SM[:, 264 + t:265 + t]
            nc.scalar.activation(RGAA[:, t], RGR[:, t], ACT.Exp, scale=c).then_inc(RGA, 1)
            act.wait_ge(RGA, 2 * t + 1)
            nc.scalar.activation(RGR[:, t], RGR[:, t], ACT.Tanh, scale=c).then_inc(RGA, 1)
        for t in range(4):
            act.wait_ge(RGW, t + 1)
            nc.scalar.activation(RGR[:, t], RGR[:, t], ACT.Sqrt, scale=-1.0).then_inc(RGM, 1)

    def rg_vector(dve, st):
        v = nc.vector
        for t in range(4):
            dve.wait_ge(RGA, 2 * t + 2)
            st.link(v.tensor_tensor(NB[0][:], RGAA[:, t], RGAA[:, t], ALU.mult))
            v.scalar_tensor_tensor(RGR[:, t], NB[0][:], 1.0, RGR[:, t], ALU.add, ALU.mult).then_inc(RGW, 1)
            st.link(v.tensor_tensor(RGI[:, t], RGI[:, t], Y[:, t], ALU.mult))
        for t in range(4):
            dve.wait_ge(RGM, t + 1)
            st.link(v.tensor_tensor(RGI[:, t], RGI[:, t], RGR[:, t], ALU.mult))
            v.tensor_tensor_scan(Y[:, t], RGAA[:, t], RGI[:, t], 0.0, ALU.mult, ALU.add).then_inc(RGU, 1)

    class Attention:

        def __init__(self, name, keys, scale):
            self.keys, self.scale = keys, scale
            self.scored, self.neg_max, self.probs = (sem(f"{name}_{what}") for what in ("scored", "neg_max", "probs"))
            self.probs_turned, self.probs_t = (sem(f"{name}_{what}") for what in ("probs_turned", "probs_t"))
            self.weighted, self.out_read = (sem(f"{name}_{what}") for what in ("weighted", "out_read"))
            self.out_turned, self.out_copied = (sem(f"{name}_{what}") for what in ("out_turned", "out_copied"))

        def queries(self, s):
            return QT[0:self.keys, s] if self.keys != HD else QT[HD * s:HD * s + HD, 0]

        def key_tile(self, s):
            return KTT[0:self.keys, s] if self.keys != HD else KTT[HD * s:HD * s + HD, 0]

        def tensor(self, pe, i, values):
            n = 16 * i
            for j in range(18):
                if j < 17:
                    for q in ([0, 1] if j == 0 else [j + 1]):
                        if q > 15:
                            continue
                        s, qb = divmod(q, TT)
                        if q >= 2:
                            pe.wait_ge(self.probs, n + q - 1)
                        for c in range(0, qb + 1, 4):
                            m = min(4, qb + 1 - c)
                            last = nc.tensor.matmul(PS[q % 2][:, c * P:(c + m) * P], self.queries(s)[:, qb * P:(qb + 1) * P],
                                                    self.key_tile(s)[:, c * P:(c + m) * P], start=True, stop=True)
                        last.then_inc(self.scored, 1)
                if j < 16:
                    pe.wait_ge(self.probs, n + j + 1)
                    if j:
                        pe.wait_ge(self.probs_t, n + j)
                    for kb in range(j % TT + 1):
                        last = nc.tensor.transpose(PA[:, kb * P:(kb + 1) * P], PP[:, j % 2, kb * P:(kb + 1) * P], IDENT[:])
                    last.then_inc(self.probs_turned, 1)
                if 1 <= j < 17:
                    q = j - 1
                    pe.wait_ge(self.probs_t, n + q + 1)
                    if q >= 2:
                        pe.wait_ge(self.out_read, n + q - 1)
                    for kb in range(q % TT + 1):
                        last = nc.tensor.matmul(PB[:, (q % 2) * HALF:(q % 2) * HALF + 2 * HD], PT[:, q % 2, kb * P:(kb + 1) * P],
                                                values(kb, i), start=(kb == 0), stop=(kb == q % TT))
                    last.then_inc(self.weighted, 1)

        def scalar(self, act, i):
            n = 16 * i
            for j in range(17):
                if j < 16:
                    qb = j % TT
                    act.wait_ge(self.neg_max, n + j + 1)
                    if j >= 2:
                        act.wait_ge(self.probs_turned, n + j - 1)
                    if j >= 4:
                        act.wait_ge(self.out_read, n + j - 3)
                    nc.scalar.activation(PP[:, j % 2, 0:(qb + 1) * P], PS[j % 2][:, 0:(qb + 1) * P], ACT.Exp,
                                         bias=SM[:, 8 + j % 4:9 + j % 4], scale=self.scale,
                                         accum_out=SM[:, 16 + j % 4:17 + j % 4]).then_inc(self.probs, 1)
                if j:
                    q = j - 1
                    act.wait_ge(self.probs_turned, n + q + 1)
                    if q >= 2:
                        act.wait_ge(self.weighted, n + q - 1)
                    w = (q % TT + 1) * P
                    nc.scalar.activation(PT[:, q % 2, 0:w], PA[:, 0:w], ACT.Copy).then_inc(self.probs_t, 1)

        def vector(self, dve, st, i, head):
            n = 16 * i
            v = nc.vector
            for j in range(18):
                if j < 16:
                    s, qb = divmod(j, TT)
                    if qb == 0:
                        head(s)
                    if j >= 4:
                        dve.wait_ge(self.probs, n + j - 3)
                    dve.wait_ge(self.scored, n + j + 1)
                    st(v.memset(SM[:, 31:32], 0.0))
                    w = (qb + 1) * P
                    st.link(v.tensor_tensor_reduce(PS[j % 2][:, 0:w], PS[j % 2][:, 0:w], BIAS[:, SEQ - w:], 1.0, NEG, ALU.add,
                                                   ALU.max, SM[:, j % 4:j % 4 + 1]))
                    v.tensor_scalar(SM[:, 8 + j % 4:9 + j % 4], SM[:, j % 4:j % 4 + 1], -self.scale, None,
                                    ALU.mult).then_inc(self.neg_max, 1)
                if j >= 2:
                    q = j - 2
                    s, qb = divmod(q, TT)
                    dve.wait_ge(self.weighted, n + q + 1)
                    st.link(v.reciprocal(SM[:, 24 + q % 4:25 + q % 4], SM[:, 16 + q % 4:17 + q % 4]))
                    v.tensor_scalar(YTOK[:, qb, bass.ds(2 * HD * i + HD * s, HD)], PB[:, (q % 2) * HALF + HD * s:(q % 2) * HALF + HD * s + HD],
                                    SM[:, 24 + q % 4:25 + q % 4], None, ALU.mult).then_inc(self.out_read, 1)

        def turn_tensor(self, pe):
            pe.wait_ge(self.out_read, 64)
            for f in range(4):
                if f >= 2:
                    pe.wait_ge(self.out_copied, f - 1)
                for t in range(TT):
                    last = nc.tensor.transpose(PAB[f % 2][:, t * P:(t + 1) * P], YTOK[:, t, f * P:(f + 1) * P], IDENT[:])
                last.then_inc(self.out_turned, 1)

        def turn_vector(self, dve, dst):
            for f in range(4):
                dve.wait_ge(self.out_turned, f + 1)
                nc.vector.tensor_copy(dst(f), PAB[f % 2][:]).then_inc(self.out_copied, 1)

    QN = sem("latents_normed")
    WQL = [sem(f"head_weights{s}") for s in range(2)]
    WKVL, VPROD, VCOP, QKP, QKC, QKR = (sem(n) for n in ("w_ukv_loaded", "v_products", "v_copied", "qk_products", "qk_copied", "qk_rotated"))
    mla = Attention("mla", NOPE + ROPE, MLA_SCALE)
    w_uq = ins["mla_w_uq"][0].rearrange("(k p) c -> p k c", p=P)
    w_ukv = ins["mla_w_ukv"][0]

    def latent_norms_scalar(act, st):
        norm_squares(act, "q", lambda k: Y[:, 4 + k], wait=lambda k: act.wait_ge(PS_READ[0], 7 + k) if k == 0 else act.wait_ge(PS_READ[1], 7), bufs=NB)
        norm_rstd(act, st, "q", Q_RANK, EPS6, bufs=NB)
        act.wait_ge(QN, 2)
        norm_squares(act, "kv", lambda k: Y[:, 6], bufs=NB)
        norm_rstd(act, st, "kv", KV_RANK, EPS6, bufs=NB)

    def latent_norms_vector(dve, st):
        norm_sum(dve, "q", bufs=NB)
        dve.wait_ge(RSTD, 1)
        for k in range(2):
            nc.vector.scalar_tensor_tensor(Y[:, 4 + k], Y[:, 4 + k], vec("qn", k), NB[1][:], ALU.mult, ALU.mult).then_inc(QN, 1)
        norm_sum(dve, "kv", bufs=NB)
        dve.wait_ge(RSTD, 2)
        nc.vector.scalar_tensor_tensor(Y[:, 6], Y[:, 6], vec("kvn"), NB[1][:], ALU.mult, ALU.mult).then_inc(QN, 1)

    def mla_loads(sp):
        sp.wait_ge(PS_READ[1], 8)
        sp.dma_start(WUKV[:], w_ukv).then_inc(WKVL, 16)
        sp.wait_ge(TRIG, 1)
        for s in range(2):
            head_weights(sp, 0, s)
        with sp.Fori(1, MLA_HEADS // 2) as i:
            sp.wait_ge(QKP, 2 * i)
            for s in range(2):
                head_weights(sp, i, s)

    def head_weights(sp, i, s):
        c = (NOPE + ROPE) * 2 * i + (NOPE + ROPE) * s
        sp.dma_start(WUQ[:, s, :, 0:96], w_uq[:, :, bass.ds(c, 96)]).then_inc(WQL[s], 16)
        sp.dma_start(WUQ[:, s, :, 96:112], w_uq[:, :, bass.ds(c + 80, 16)]).then_inc(WQL[s], 16)
        sp.dma_start(WUQ[:, s, :, 112:128], w_uq[:, :, bass.ds(c + 64, 16)]).then_inc(WQL[s], 16)
        sp.dma_start(WK[:, s], w_ukv[:, bass.ds(2 * P * i + P * s, NOPE)]).then_inc(WQL[s], 16)

    def mla_tensor(pe):
        pe.wait_ge(WKVL, 16)
        pe.wait_ge(RGU, 4)
        for t in range(TT):
            if t >= 2:
                pe.wait_ge(VCOP, t - 1)
            nc.tensor.matmul(PAB[t % 2][:, 0:HALF].rearrange("p (h c) -> p h c", h=MLA_HEADS), Y[:, 6, t * P:(t + 1) * P],
                             WUKV[:].rearrange("p (h c) -> p h c", h=MLA_HEADS)[:, :, NOPE:], start=True,
                             stop=True).then_inc(VPROD, 1)
        pe.wait_ge(VCOP, TT)
        with pe.Fori(0, MLA_HEADS // 2) as i:
            for s, (q, k) in enumerate(((PA, PB), (PS[0], PS[1]))):
                pe.wait_ge(WQL[s], 64 * i + 64)
                for h in range(2):
                    c = slice(h * HALF, (h + 1) * HALF)
                    for kt in range(2):
                        nc.tensor.matmul(q[:, c], WUQ[:, s, kt], Y[:, 4 + kt, c], start=(kt == 0), stop=(kt == 1))
                    last = nc.tensor.matmul(k[0:NOPE, c], WK[:, s], Y[:, 6, c], start=True, stop=True)
                last.then_inc(QKP, 1)
            pe.wait_ge(QKR, 2 * i + 2)
            mla.tensor(pe, i, lambda kb, i: VTOK[:, kb, bass.ds(2 * HD * i, 2 * HD)])
            pe.wait_ge(mla.out_read, 16 * i + 16)
        mla.turn_tensor(pe)

    def mla_scalar(act):
        for t in range(TT):
            act.wait_ge(VPROD, t + 1)
            nc.scalar.activation(VTOK[:, t], PAB[t % 2][:, 0:HALF], ACT.Copy).then_inc(VCOP, 1)
        with act.Fori(0, MLA_HEADS // 2) as i:
            for s, (q, k) in enumerate(((PA, PB), (PS[0], PS[1]))):
                act.wait_ge(QKP, 2 * i + s + 1)
                nc.scalar.activation(QT[0:NOPE, s], q[0:NOPE], ACT.Copy)
                nc.scalar.activation(KTT[0:NOPE, s], k[0:NOPE], ACT.Copy)
                nc.scalar.activation(PP[RR, s], q[RS_], ACT.Copy).then_inc(QKC, 1)
            mla.scalar(act, i)

    def mla_vector(dve, st):
        v = nc.vector
        for s in range(2):
            st(v.tensor_copy(KTT[RR, s], Y[RR, 7]))
        dve.wait_ge(VPROD, TT)
        st(v.memset(BIAS[:, 0:SEQ - P], 0.0))
        st.link(v.tensor_copy(BIAS[:, SEQ - P:], CMASK[:]))
        PER = 2 * 2 + 16 * 3
        with dve.Fori(0, MLA_HEADS // 2) as i:
            st.enter(i, PER)
            for s, q in enumerate((PA, PS[0])):
                dve.wait_ge(QKC, 2 * i + s + 1)
                st(v.tensor_tensor(QT[RR, s], q[RR], COS[RR], ALU.mult))
                st.link(v.tensor_tensor(PP[RR, s], PP[RR, s], SIN[RR], ALU.mult))
                v.tensor_tensor(QT[RR, s], QT[RR, s], PP[RR, s], ALU.add).then_inc(QKR, 1)
            mla.vector(dve, st, i, lambda s: None)
            st.leave(MLA_HEADS // 2)
        mla.turn_vector(dve, lambda f: Y[:, 4 + f])

    GHI = sem("gated")

    def gate1_vector(dve, st):
        for k in range(KT):
            if k >= 4:
                dve.wait_ge(mla.out_copied, k - 3)
            elif k == 0:
                dve.wait_ge(RGU, 4)
            if k >= 2:
                dve.wait_ge(X_OK, TT + k - 1)
            nc.vector.tensor_tensor(T[k % 2][:], Y[:, k], G[:, k], ALU.mult).then_inc(GHI, 1)
            if k:
                gate1_lo(dve, k - 1)
        gate1_lo(dve, KT - 1)

    def gate1_lo(dve, k):
        dve.wait_ge(XHI, TT + k + 1)
        nc.vector.tensor_tensor(HL[:, k], T[k % 2][:], HH[:, k].bitcast(F32), ALU.subtract).then_inc(X_OK, 1)

    def gate1_scalar(act):
        for k in range(KT):
            act.wait_ge(GHI, k + 1)
            nc.scalar.activation(HH[:, k], T[k % 2][:], ACT.Copy).then_inc(XHI, 1)

    w_ab_out = ins["ab_w_out"][0].rearrange("(k p) c -> p k c", p=P)

    def out1_sync(sp):
        for m in range(KT):
            load_block(sp, B_OUT + m, w_ab_out[:, :, m * P:(m + 1) * P])

    def out1_tensor(pe):
        for m in range(KT):
            block_products(pe, B_OUT + m, HH, HL, after=(lambda k: pe.wait_ge(X_OK, TT + k + 1)) if m == 0 else None)

    def acc_vector(dve, st, b0, n=KT):
        for m in range(n):
            b = b0 + m
            dve.wait_ge(BLOCK_DONE[b % 2], times(b))
            nc.vector.tensor_tensor(ACC[:, m], ACC[:, m], PS[b % 2][:], ALU.add).then_inc(PS_READ[b % 2], 1)
            split_lo(dve, b + 2)

    def splits_scalar(act, b0, n):
        for b in range(b0, b0 + n):
            split_hi(act, b + 2)

    XRDY = sem("stream_ready")
    CEN, LNS, LNB = sem("centred"), sem("ln_scaled"), sem("ln_biased")

    def ln_vector(dve, st, turn, name, g, b_last, split):
        v = nc.vector
        dve.wait_ge(PS_READ[(b_last - 1) % 2], times(b_last - 1))
        dve.wait_ge(PS_READ[b_last % 2], times(b_last))
        st.link(v.tensor_tensor(T[2][:], ACC[:, 0], ACC[:, 1], ALU.add))
        for k in range(2, KT):
            i_ = v.tensor_tensor(T[2][:], T[2][:], ACC[:, k], ALU.add)
            if k < KT - 1:
                st.link(i_)
        i_.then_inc(MSUM, 1)
        dve.wait_ge(MROW, turn + 1)
        for k in range(KT):
            v.scalar_tensor_tensor(ACC[:, k], PB[:], -1.0 / D, ACC[:, k], ALU.mult, ALU.add).then_inc(CEN, 1)
        norm_sum(dve, name)
        dve.wait_ge(RSTD, NORM[name][0] + 1)
        for k in range(KT):
            v.scalar_tensor_tensor(ACC[:, k], ACC[:, k], vec(g, k), T[1][:], ALU.mult, ALU.mult).then_inc(LNS, 1)
        if split:
            for k in range(KT):
                dve.wait_ge(LNB, 2 * k + 2)
                v.tensor_tensor(XL[:, k], ACC[:, k], XH[:, k].bitcast(F32), ALU.subtract).then_inc(X_OK, 1)
            for k in range(KT):
                if k == 0:
                    dve.wait_ge(X_OK, 3 * KT)
                st(v.tensor_scalar(ACC[:, k], ACC[:, k], DN_ALPHA, None, ALU.mult))

    def ln_tensor(pe, turn, name):
        pe.wait_ge(MSUM, turn + 1)
        for h in range(2):
            last = nc.tensor.matmul(PB[:, h * HALF:(h + 1) * HALF], ONES[:], T[2][:, h * HALF:(h + 1) * HALF], start=True, stop=True)
        last.then_inc(MROW, 1)
        norm_rows(pe, name)

    def ln_scalar(act, st, turn, name, b, split):
        norm_squares(act, name, lambda k: ACC[:, k], wait=lambda k: act.wait_ge(CEN, KT * turn + k + 1))
        norm_rstd(act, st, name, D, EPS5)
        for k in range(KT):
            act.wait_ge(LNS, KT * turn + k + 1)
            nc.scalar.activation(ACC[:, k], ACC[:, k], ACT.Identity, bias=vec(b, k)).then_inc(LNB if split else XRDY, 1)
            if split:
                act.wait_ge(LNB, 2 * k + 1)
                nc.scalar.activation(XH[:, k], ACC[:, k], ACT.Copy).then_inc(LNB, 1)

    DTX, DTE, DTA, DTP, DTD, ALE = (sem(n) for n in ("dt_abs", "dt_exp", "a_dt", "decay_sums", "decays", "a_exp"))
    w_ssd = ins["ssd_w_in"][0].rearrange("(k p) c -> p k c", p=P)

    def dt_sync(sp):
        load_block(sp, B_DT, w_ssd[:, :, SSD_INNER + SSD_CONV:], cols=KT * SSD_HEADS)

    def dt_tensor(pe):
        pe.wait_ge(X_OK, 3 * KT)
        token_products(pe, B_DT, n_cols=SSD_HEADS)
        pe.wait_ge(DTA, 1)
        adt = ADT[:].rearrange("p t h -> p (t h)")
        n = TT * SSD_HEADS
        nc.tensor.matmul(PA[:, 0:n], LE[:], adt, start=True, stop=True)
        nc.tensor.matmul(PA[:, HALF:HALF + n], GT[:], adt, start=True, stop=True)
        nc.tensor.matmul(PB[:, 0:n], ONES[:], adt, start=True, stop=True).then_inc(DTP, 1)

    def dt_vector(dve, st):
        v = nc.vector
        flat = lambda t: t[:].rearrange("p t h -> p (t h)")
        dve.wait_ge(BLOCK_DONE[B_DT % 2], times(B_DT))
        v.tensor_tensor(DTT[:], PS[B_DT % 2][:].rearrange("p (t c) -> p t c", t=TT)[:, :, 0:SSD_HEADS],
                        vec("dtb", 0, 32).unsqueeze(1).broadcast_to([P, TT, SSD_HEADS]), ALU.add).then_inc(PS_READ[B_DT % 2], 1)
        split_lo(dve, B_DT + 2, cols=1024)
        dve.wait_ge(PS_READ[B_DT % 2], times(B_DT))
        e, s, q = (SEGR[:, k * 2:k * 2 + 2].rearrange("p a b -> p (a b)") for k in range(3))
        st.link(v.tensor_scalar(s, flat(DTT), -1.0, None, ALU.mult))
        v.tensor_tensor(e, s, flat(DTT), ALU.max).then_inc(DTX, 1)
        st(v.tensor_scalar(DTT[:], DTT[:], 0.0, None, ALU.max))
        dve.wait_ge(DTE, 1)
        log1p_exp(st, q, s, e)
        st.link(v.tensor_tensor(flat(DTT), flat(DTT), q, ALU.add))
        dve.wait_ge(ALE, 1)
        v.scalar_tensor_tensor(ADT[:], DTT[:], -1.0, vec("alog", 0, 32).unsqueeze(1).broadcast_to([P, TT, SSD_HEADS]),
                               ALU.mult, ALU.mult).then_inc(DTA, 1)
        dve.wait_ge(DTD, 3)
        st.link(v.tensor_tensor(EDX[:], EDX[:], DTT[:], ALU.mult))

    def dt_scalar(act):
        split_hi(act, B_DT + 2)
        act.wait_ge(DTX, 1)
        e = SEGR[:, 0:2].rearrange("p a b -> p (a b)")
        nc.scalar.activation(e, e, ACT.Exp, scale=-1.0).then_inc(DTE, 1)
        a = vec("alog", 0, 32)
        nc.scalar.activation(a, a, ACT.Exp).then_inc(ALE, 1)
        act.wait_ge(DTP, 1)
        n = TT * SSD_HEADS
        for dst, src in ((ECS, PA[:, 0:n]), (EDX, PA[:, HALF:HALF + n]), (CDEC, PB[:, 0:n])):
            nc.scalar.activation(dst[:].rearrange("p t h -> p (t h)"), src, ACT.Exp).then_inc(DTD, 1)

    (SV, SSILU, STURN, SCOPY, SSEGR, SSEG, SCB, SDEC, SMR, SYO, SYD, SST, SXD, SXDD, SSK, SPREV, SYT_OK, SYOR,
     SYTURN, SGATED, SNS, SYGH, SYGL) = (sem("ssd_" + n) for n in (
        "group_vectors", "silu", "turned", "turned_copied", "segment_rows", "segment_sums", "cb", "decay",
        "mixing", "y_off", "y_diag", "states", "x_dt", "x_decayed", "skip", "state_ready", "y_ready", "y_off_read",
        "y_turned", "gated", "normed", "y_hi", "y_lo"))
    w_ssd_out = ins["ssd_w_out"][0]
    GDT, GAD, GEC, GEX, GCD = (SM[:, 64 * k:64 * k + 64].rearrange("p (t h) -> p t h", h=HPG) for k in range(5))
    GSK = EP[:, 8:16]
    CONVD = ((XST, 0), (XST, 1), (XST, 2), (XST, 3), (BT, None), (CT, None))

    def conv_dst(j):
        t, k = CONVD[j]
        return t[:] if k is None else t[:, k]

    def ssd_cols(j):
        if j < 4:
            return SSD_INNER + j * P, GW
        if j < 6:
            return 2 * SSD_INNER + (j - 4) * SSD_GROUPS * P, P
        return (j - 6) * P, GW

    def ssd_sync(sp):
        with sp.Fori(0, SSD_GROUPS) as i:
            for j in range(10):
                c0, step = ssd_cols(j)
                load_block(sp, B_SSD + j, w_ssd[:, :, bass.ds((i * (step // P) + c0 // P) * P, P)], i=i, per=SSD_BLOCKS)
            for m in range(KT):
                src = w_ssd_out[bass.ds(i * GW, GW), m * P:(m + 1) * P].rearrange("(k p) c -> p k c", p=P)
                load_block(sp, B_SSD + 10 + m, src, cols=512, kt=4, i=i, per=SSD_BLOCKS)

    def cols_of(b):
        j = (b - B_SSD) % SSD_BLOCKS
        return 512 if (B_SSD <= b < B_FFN1 and j >= 10) or B_GLU <= b < B_MIXOUT else 1024

    def ssd_tensor(pe):
        with pe.Fori(0, SSD_GROUPS) as i:
            for j in range(10):
                block_products(pe, B_SSD + j, XH, XL, i=i, per=SSD_BLOCKS)
                if j >= 6:
                    ssd_turn(pe, i, j - 6, conv_dst(j - 6))
            ssd_turn(pe, i, 4, conv_dst(4))
            ssd_scan_tensor(pe, i)
            for f in range(4):
                if f == 0:
                    pe.wait_ge(SYT_OK, i * TT + TT)
                if f >= 2:
                    pe.wait_ge(SGATED, i * 4 + f - 1)
                for t in range(TT):
                    last = nc.tensor.transpose(PAB[f % 2][:, t * P:(t + 1) * P], SYT[:, t, f * P:(f + 1) * P], IDENT[:])
                last.then_inc(SYTURN, 1)
            norm_rows(pe, "g0", i=i)
            for m in range(KT):
                block_products(pe, B_SSD + 10 + m, YGH, YGL, kt=4, i=i, per=SSD_BLOCKS,
                               after=(lambda k: pe.wait_ge(SYGL, i * 4 + k + 1)) if m == 0 else None)

    def ssd_turn(pe, i, f, src):
        pe.wait_ge(SSILU, i * 6 + f + 1)
        if f >= 2:
            pe.wait_ge(SCOPY, i * 5 + f - 1)
        for t in range(TT):
            last = nc.tensor.transpose(PAB[f % 2][:, t * P:(t + 1) * P], src[:, t * P:(t + 1) * P], IDENT[:])
        last.then_inc(STURN, 1)

    def ssd_scan_tensor(pe, i):
        pe.wait_ge(SCOPY, i * 5 + 5)
        pe.wait_ge(SSILU, i * 6 + 6)
        pe.wait_ge(PS_READ[B_SSD % 2], times(B_SSD + 8, i, SSD_BLOCKS))
        pe.wait_ge(PS_READ[1 - B_SSD % 2], times(B_SSD + 9, i, SSD_BLOCKS))
        n = i * TT
        for c in range(TT):
            tok = slice(c * P, (c + 1) * P)
            pe.wait_ge(SSEGR, n + c + 1)
            for h in range(2):
                last = nc.tensor.matmul(PA[:, h * HALF:(h + 1) * HALF], GT[:],
                                        SEGR[:, 4 * h:4 * h + 4].rearrange("p h l -> p (h l)"), start=True, stop=True)
            last.then_inc(SSEG, 1)
            nc.tensor.matmul(PB[:, 0:P], BT[:, tok], CT[:, tok], start=True, stop=True).then_inc(SCB, 1)
            pe.wait_ge(SPREV, i * (TT + 1) + c + 1)
            nc.tensor.matmul(PS[0][:, 0:GW], CT[:, tok], PREV[:], start=True, stop=True).then_inc(SYO, 1)
            pe.wait_ge(SXDD, n + c + 1)
            nc.tensor.matmul(PS[0][:, HALF:HALF + GW], BTOK[:, c], XDD[:], start=True, stop=True).then_inc(SST, 1)
            pe.wait_ge(SXD, n + c + 1)
            pe.wait_ge(SMR, n + c + 1)
            if c:
                pe.wait_ge(SYT_OK, n + c)
            for h in range(HPG):
                last = nc.tensor.matmul(PB[:, HALF + h * SSD_P:HALF + (h + 1) * SSD_P], DEC[:, h],
                                        XDT[:, h * SSD_P:(h + 1) * SSD_P], start=True, stop=True)
            last.then_inc(SYD, 1)

    def ssd_scalar(act, st):
        with act.Fori(0, SSD_GROUPS) as i:
            for j in range(10):
                b = B_SSD + j
                if j >= 6:
                    act.wait_ge(BLOCK_DONE[b % 2], times(b, i, SSD_BLOCKS))
                    nc.scalar.activation(ZT[:, j - 6], PS[b % 2][:], ACT.Silu).then_inc(PS_READ[b % 2], 1)
                split_hi(act, b + 2, i=i, per=SSD_BLOCKS, cols=512 if j + 2 >= 10 else 1024)
                if j < 6:
                    act.wait_ge(PS_READ[b % 2], times(b, i, SSD_BLOCKS))
                    nc.scalar.activation(conv_dst(j), conv_dst(j), ACT.Silu).then_inc(SSILU, 1)
                else:
                    ssd_copy(act, i, j - 6)
            ssd_copy(act, i, 4)
            for c in range(TT):
                act.wait_ge(SSEG, i * TT + c + 1)
                if c:
                    act.wait_ge(SYD, i * TT + c)
                nc.scalar.activation(DEC[:].rearrange("p h l -> p (h l)"), PA[:], ACT.Exp).then_inc(SDEC, 1)
            norm_squares(act, "g0", lambda k: ZT[:, k], wait=lambda k: act.wait_ge(SGATED, i * 4 + k + 1), i=i)
            st.enter(i, 1)
            norm_rstd(act, st, "g0", GW, EPS6, i=i)
            st.leave(SSD_GROUPS)
            for k in range(4):
                act.wait_ge(SNS, i * 4 + k + 1)
                nc.scalar.activation(YGH[:, k], ZT[:, k], ACT.Copy).then_inc(SYGH, 1)
            for m in range(KT):
                split_hi(act, B_SSD + 12 + m, i=i, per=SSD_BLOCKS, cols=512 if m < 6 else 1024)

    def ssd_copy(act, i, f):
        act.wait_ge(STURN, i * 5 + f + 1)
        dst = XTOK[:, :, f * P:(f + 1) * P] if f < 4 else BTOK[:]
        nc.scalar.activation(dst, PAB[f % 2][:].rearrange("p (t c) -> p t c", t=TT), ACT.Copy).then_inc(SCOPY, 1)

    def over_p(t, c):
        return t[:, c].unsqueeze(2).broadcast_to([P, HPG, SSD_P])

    heads = lambda t: t.rearrange("p (h c) -> p h c", h=HPG)

    def ssd_vector(dve, st):
        v = nc.vector
        PER = 7 + 6 * 3 + 4 * TT
        with dve.Fori(0, SSD_GROUPS) as i:
            st.enter(i, PER)
            a = VEC["ssd"][0]
            st(v.tensor_copy(GV[:], VT[:, bass.ds(i * 34 + a, 34)]))
            for dst, src in ((GDT, DTT), (GAD, ADT), (GEC, ECS), (GEX, EDX), (GCD, CDEC)):
                st(v.tensor_copy(dst, src[:, :, bass.ds(i * HPG, HPG)]))
            st(v.tensor_copy(GSK, VT[:, bass.ds(i * HPG + VEC["ssd_d"][0], HPG)]))
            st.wait()
            for j in range(10):
                b = B_SSD + j
                if j < 6:
                    dve.wait_ge(BLOCK_DONE[b % 2], times(b, i, SSD_BLOCKS))
                    conv(st, conv_dst(j), b, lambda k: GV[:, 4 * j + k:4 * j + k + 1], GV[:, 24 + j:25 + j], PS_READ[b % 2])
                split_lo(dve, b + 2, i=i, per=SSD_BLOCKS, cols=512 if j + 2 >= 10 else 1024)
            v.memset(PREV[:], 0.0).then_inc(SPREV, 1)
            ssd_segments(dve, i, 0)
            for c in range(TT):
                n = i * TT + c + 1
                dve.wait_ge(SCB, n)
                st.link(v.tensor_tensor(CBM[:], PB[:, 0:P], LE[:], ALU.mult))
                if c + 1 < TT:
                    ssd_segments(dve, i, c + 1)
                dve.wait_ge(SDEC, n)
                v.tensor_tensor(DEC[:], DEC[:], CBM[:].unsqueeze(1).broadcast_to([P, HPG, P]), ALU.mult).then_inc(SMR, 1)
                dve.wait_ge(SYO, n)
                st.link(v.tensor_tensor(heads(YOS[:]), heads(PS[0][:, 0:GW]), over_p(GEC, c), ALU.mult))
                st.link(v.tensor_tensor(heads(PREV[:]), heads(PREV[:]), over_p(GCD, c), ALU.mult))
                dve.wait_ge(SST, n)
                v.tensor_tensor(PREV[:], PREV[:], PS[0][:, HALF:HALF + GW], ALU.add).then_inc(SPREV, 1)
                dve.wait_ge(SSK, n)
                st.link(v.tensor_tensor(SYT[:, c], SYT[:, c], YOS[:], ALU.add))
                dve.wait_ge(SYD, n)
                v.tensor_tensor(SYT[:, c], SYT[:, c], PB[:, HALF:HALF + GW], ALU.add).then_inc(SYT_OK, 1)
            for f in range(4):
                dve.wait_ge(SYTURN, i * 4 + f + 1)
                v.tensor_tensor(ZT[:, f], ZT[:, f], PAB[f % 2][:], ALU.mult).then_inc(SGATED, 1)
            norm_sum(dve, "g0", i=i)
            dve.wait_ge(RSTD, NORM["g0"][0] + 1 + i)
            for k in range(4):
                v.scalar_tensor_tensor(ZT[:, k], ZT[:, k], GV[:, 30 + k:31 + k], T[1][:], ALU.mult, ALU.mult).then_inc(SNS, 1)
            for k in range(4):
                dve.wait_ge(SYGH, i * 4 + k + 1)
                v.tensor_tensor(YGL[:, k], ZT[:, k], YGH[:, k].bitcast(F32), ALU.subtract).then_inc(SYGL, 1)
            for m in range(KT):
                b = B_SSD + 10 + m
                dve.wait_ge(BLOCK_DONE[b % 2], times(b, i, SSD_BLOCKS))
                v.tensor_tensor(ACC[:, m], ACC[:, m], PS[b % 2][:], ALU.add).then_inc(PS_READ[b % 2], 1)
                split_lo(dve, b + 2, i=i, per=SSD_BLOCKS, cols=512 if m < 6 else 1024)
            st.leave(SSD_GROUPS)

    def ssd_segments(dve, i, c):
        if c:
            dve.wait_ge(SSEG, i * TT + c)
        nc.vector.tensor_tensor(SEGR[:], LE[:].unsqueeze(1).broadcast_to([P, HPG, P]),
                                GAD[:, c].unsqueeze(2).broadcast_to([P, HPG, P]), ALU.mult).then_inc(SSEGR, 1)

    def ssd_pool(pool):
        g = nc.gpsimd
        with pool.Fori(0, SSD_GROUPS) as i:
            pool.wait_ge(SCOPY, i * 5 + 5)
            for c in range(TT):
                x = heads(XTOK[:, c])
                if c:
                    pool.wait_ge(SST, i * TT + c)
                g.tensor_tensor(heads(XDD[:]), x, over_p(GEX, c), ALU.mult).then_inc(SXDD, 1)
                if c:
                    pool.wait_ge(SYD, i * TT + c)
                g.tensor_tensor(heads(XDT[:]), x, over_p(GDT, c), ALU.mult).then_inc(SXD, 1)
                g.tensor_tensor(heads(SYT[:, c]), x, GSK.unsqueeze(2).broadcast_to([P, HPG, SSD_P]), ALU.mult).then_inc(SSK, 1)

    SPILLED, RESID, NSC, NHI = (sem(n) for n in ("spilled", "residual_loaded", "norm_scaled", "norm_hi"))

    def pre_vector(dve, turn, name, g):
        v = nc.vector
        norm_sum(dve, name)
        dve.wait_ge(RSTD, rstd_no(name))
        tmp = (T[0], T[2])
        for k in range(KT + 1):
            if k < KT:
                if k >= 2:
                    dve.wait_ge(X_OK, XOK_PRE + KT * turn + k - 1)
                v.scalar_tensor_tensor(tmp[k % 2][:], ACC[:, k], vec(g, k), T[1][:], ALU.mult, ALU.mult).then_inc(NSC, 1)
            if k:
                dve.wait_ge(NHI, KT * turn + k)
                v.tensor_tensor(XL[:, k - 1], tmp[(k - 1) % 2][:], XH[:, k - 1].bitcast(F32), ALU.subtract).then_inc(X_OK, 1)

    XOK_PRE = 3 * KT

    def rstd_no(name):
        return NORM[name][0] + 1

    def pre_scalar(act, st, turn, name):
        norm_squares(act, name, lambda k: ACC[:, k], wait=lambda k: act.wait_ge(XRDY, KT * turn + k + 1))
        norm_rstd(act, st, name, D, EPS6)
        tmp = (T[0], T[2])
        for k in range(KT):
            act.wait_ge(NSC, KT * turn + k + 1)
            nc.scalar.activation(XH[:, k], tmp[k % 2][:], ACT.Copy).then_inc(NHI, 1)

    def spill_pool(pool, turn):
        pool.wait_ge(XRDY, KT * (turn + 1))
        pool.dma_start(XRES.rearrange("k p t -> p k t"), ACC[:]).then_inc(SPILLED, 16)

    def reload_pool(pool, turn, b_last):
        pool.wait_ge(SPILLED, 16 * (turn + 1))
        for b in (b_last - 1, b_last):
            pool.wait_ge(BLOCK_DONE[b % 2], times(b))
        pool.dma_start(RL[:], XRES.rearrange("k p t -> p k t")).then_inc(RESID, 16)

    def post_vector(dve, turn, name, g, b_last):
        v = nc.vector
        norm_sum(dve, name)
        dve.wait_ge(RSTD, rstd_no(name))
        for k in range(KT):
            v.scalar_tensor_tensor(ACC[:, k], ACC[:, k], vec(g, k), T[1][:], ALU.mult, ALU.mult).then_inc(POSTS, 1)
        dve.wait_ge(RESID, 16 * (turn + 1))
        for k in range(KT):
            dve.wait_ge(POSTS, KT * turn + k + 1)
            v.tensor_tensor(ACC[:, k], ACC[:, k], RL[:, k], ALU.add).then_inc(XRDY, 1)

    POSTS = sem("post_scaled")

    def post_scalar(act, st, turn, name, done):
        norm_squares(act, name, lambda k: ACC[:, k], wait=done)
        norm_rstd(act, st, name, D, EPS6)

    HIDH, HIDL = sem("hidden_hi"), sem("hidden_lo")

    def ffn_sync(sp, b0, w_in, w_out):
        wi = w_in.rearrange("(k p) c -> p k c", p=P)
        b, f0 = b0, 0
        for nf in FFN_PARTS:
            with sp.Fori(0, nf) as i:
                for j in range(2):
                    load_block(sp, b + j, wi[:, :, bass.ds(i * P + f0 * P + j * D_FF, P)], i=i, per=2)
            b += 2 * nf
            with sp.Fori(0, KT // 2) as i:
                for j in range(2):
                    src = w_out[f0 * P:(f0 + nf) * P, bass.ds((i * 2 + j) * P, P)].rearrange("(k p) c -> p k c", p=P)
                    load_block(sp, b + j, src, cols=nf * P, kt=nf, i=i, per=2)
            b += KT
            f0 += nf

    def ffn_tensor(pe, turn, b0):
        x_ready = lambda k: pe.wait_ge(X_OK, XOK_PRE + KT * 2 * turn + k + 1)
        hidden_ready = lambda k: pe.wait_ge(HIDL, FT * turn + f0 + k + 1)
        b, f0 = b0, 0
        for nf in FFN_PARTS:
            with pe.Fori(0, nf) as i:
                for j in range(2):
                    block_products(pe, b + j, XH, XL, i=i, per=2, after=x_ready if f0 == 0 and j == 0 else None)
            b += 2 * nf
            with pe.Fori(0, KT // 2) as i:
                for j in range(2):
                    block_products(pe, b + j, HH, HL, kt=nf, i=i, per=2, after=hidden_ready if j == 0 else None)
            b += KT
            f0 += nf

    def ffn_scalar(act, turn, b0):
        b, f0 = b0, 0
        for nf in FFN_PARTS:
            with act.Fori(0, nf) as i:
                g, u = b % 2, (b + 1) % 2
                act.wait_ge(BLOCK_DONE[g], times(b, i, 2))
                nc.scalar.activation(T[0][:], PS[g][:], ACT.Silu).then_inc(PS_READ[g], 1)
                split_hi(act, b + 2, i=i, per=2)
                act.wait_ge(PS_READ[u], times(b + 1, i, 2))
                nc.scalar.activation(HH[:, bass.ds(i, 1)].rearrange("p a t -> p (a t)"), T[1][:], ACT.Copy).then_inc(HIDH, 1)
                split_hi(act, b + 3, i=i, per=2)
            b += 2 * nf
            turns = KT // 2 - (b + KT == B_END)
            with act.Fori(0, turns) as i:
                for j in range(2):
                    split_hi(act, b + j + 2, i=i, per=2)
            b += KT
            f0 += nf

    def ffn_vector(dve, turn, b0):
        v = nc.vector
        b, f0 = b0, 0
        for nf in FFN_PARTS:
            with dve.Fori(0, nf) as i:
                g, u = b % 2, (b + 1) % 2
                split_lo(dve, b + 2, i=i, per=2)
                dve.wait_ge(PS_READ[g], times(b, i, 2))
                dve.wait_ge(BLOCK_DONE[u], times(b + 1, i, 2))
                v.tensor_tensor(T[1][:], T[0][:], PS[u][:], ALU.mult).then_inc(PS_READ[u], 1)
                dve.wait_ge(HIDH, i + FT * turn + f0 + 1)
                hh = HH[:, bass.ds(i, 1)].rearrange("p a t -> p (a t)").bitcast(F32)
                v.tensor_tensor(HL[:, bass.ds(i, 1)].rearrange("p a t -> p (a t)"), T[1][:], hh, ALU.subtract).then_inc(HIDL, 1)
                split_lo(dve, b + 3, i=i, per=2)
            b += 2 * nf
            if f0 == 0:
                dve.wait_ge(SPILLED, 16 * (1 + 2 * turn))
            turns = KT // 2 - (b + KT == B_END)

            def sum_up(b, j, i, per, split):
                dve.wait_ge(BLOCK_DONE[(b + j) % 2], times(b + j, i, per))
                acc = ACC[:, bass.ds(i * 2 + j, 1)].rearrange("p a t -> p (a t)") if per else ACC[:, KT - 2 + j]
                ps = PS[(b + j) % 2][:]
                (v.tensor_copy(acc, ps) if f0 == 0 else v.tensor_tensor(acc, acc, ps, ALU.add)).then_inc(PS_READ[(b + j) % 2], 1)
                if split:
                    split_lo(dve, b + j + 2, i=i, per=per)
            with dve.Fori(0, turns) as i:
                for j in range(2):
                    sum_up(b, j, i, 2, True)
            if turns < KT // 2:
                for j in range(2):
                    sum_up(b + KT - 2, j, None, 0, False)
            b += KT
            f0 += nf

    MUOK = sem("u_ready")
    w_mix = ins["w_mix_in_2"][0].rearrange("(k p) c -> p k c", p=P)

    def mix_sync(sp):
        for j in range(16):
            load_block(sp, B_MIX + j, w_mix[:, :, j * P:(j + 1) * P])

    def mix_tensor(pe):
        for j in range(16):
            if 8 <= j < 12:
                token_products(pe, B_MIX + j)
            else:
                block_products(pe, B_MIX + j, XH, XL, after=(lambda k: pe.wait_ge(X_OK, XOK_PRE + KT + k + 1)) if j == 0 else None)

    def mix_scalar(act):
        for j in range(16):
            b = B_MIX + j
            if j < 12:
                act.wait_ge(BLOCK_DONE[b % 2], times(b))
                src = PS[b % 2][:]
                dst = MQ[:, j] if j < 4 else MK[:, (j - 4) % 4]
                if j >= 8:
                    dst, src = MV[:, :, (j - 8) * P:(j - 7) * P], src.rearrange("p (t c) -> p t c", t=TT)
                nc.scalar.activation(dst, src, ACT.Copy).then_inc(PS_READ[b % 2], 1)
            split_hi(act, b + 2, cols=cols_of(b + 2))
            if j == 12:
                act.wait_ge(MULT1, 1)
                nc.scalar.activation(LOGC[:], PA[:], ACT.Ln).then_inc(MULT_LN, 1)

    def by_place(t):
        return t.rearrange("p (n j) -> p n j", j=S5_T)

    def mix_vector(dve, st):
        for j in range(16):
            b = B_MIX + j
            if j >= 12:
                dve.wait_ge(BLOCK_DONE[b % 2], times(b))
                nc.vector.tensor_copy(MU[:, j - 12].rearrange("p (j n) -> p n j", j=S5_T), by_place(PS[b % 2][:])).then_inc(PS_READ[b % 2], 1)
            split_lo(dve, b + 2, cols=cols_of(b + 2))
            if j == 8:
                multiplicity(dve, st)
        dve.wait_ge(MULT_LN, 1)
        st.link(nc.vector.scalar_tensor_tensor(LOGC[:], PB[:], -NEG, LOGC[:], ALU.mult, ALU.add))
        st(nc.vector.tensor_scalar(LOGC[:], LOGC[:], 1.0 / DIL_SCALE, None, ALU.mult))

    DISTI = at("DISTI", 200, [P, SEQ], I32)
    LOGI = at("LOGI", 196, [P, SEQ], I32)
    IOTA, MULT1, MULT_LN, PAIR = (sem(n) for n in ("distances", "multiplicity", "log_multiplicity", "pair_ready"))
    DIL_SCALE = HD ** -0.5
    dil = Attention("dil", HD, DIL_SCALE)

    def dist_pool(pool):
        pool.wait_ge(X_OK, XOK_PRE + 2 * KT)
        nc.gpsimd.iota(DISTI[:], pattern=[[-1, SEQ]], base=SEQ - P, channel_multiplier=1).then_inc(IOTA, 1)

    def multiplicity(dve, st):
        v = nc.vector
        dve.wait_ge(IOTA, 1)
        st.link(v.tensor_copy(DIST[:], DISTI[:]))
        st.link(v.tensor_scalar(LOGI[:], DISTI[:], 3, None, ALU.bitwise_and))
        st.link(v.tensor_scalar(PA[:], LOGI[:], 0.0, None, ALU.is_equal))
        st.link(v.scalar_tensor_tensor(PA[:], DIST[:], 512.0, PA[:], ALU.is_le, ALU.mult))
        st.link(v.tensor_scalar(LOGI[:], DISTI[:], 15, None, ALU.bitwise_and))
        st.link(v.scalar_tensor_tensor(PB[:], LOGI[:], 0.0, PA[:], ALU.is_equal, ALU.add))
        st.link(v.scalar_tensor_tensor(PA[:], DIST[:], 128.0, PB[:], ALU.is_le, ALU.add))
        st.link(v.scalar_tensor_tensor(PB[:], DIST[:], 0.0, PA[:], ALU.is_ge, ALU.mult))
        st.link(v.tensor_scalar(PA[:], PB[:], 1.0, None, ALU.max))
        v.tensor_scalar(PB[:], PB[:], 1.0, -1.0, ALU.min, ALU.add).then_inc(MULT1, 1)

    def pair_pool(pool, i, static):
        for dst, src in ((QT, MQ), (KTT, MK)):
            nc.gpsimd.tensor_copy(dst[:, 0], src[:, i] if static else src[:, bass.ds(i, 1)].rearrange("p a t -> p (a t)")).then_inc(PAIR, 1)

    def dil_pool(pool):
        pool.wait_ge(PS_READ[(B_MIX + 14) % 2], times(B_MIX + 14))
        pool.wait_ge(PS_READ[(B_MIX + 15) % 2], times(B_MIX + 15))
        pair_pool(pool, 0, True)
        with pool.Fori(1, ATT_HEADS // 2) as i:
            pool.wait_ge(dil.scored, 16 * i)
            pool.wait_ge(PAIR, 2)
            pair_pool(pool, i, False)

    def dil_tensor(pe):
        for b in (B_MIX + 14, B_MIX + 15):
            pe.wait_ge(PS_READ[b % 2], times(b))
        with pe.Fori(0, ATT_HEADS // 2) as i:
            pe.wait_ge(PAIR, 2 * i + 2)
            dil.tensor(pe, i, lambda kb, i: MV[:, kb, bass.ds(2 * HD * i, 2 * HD)])
        dil.turn_tensor(pe)

    def dil_scalar(act):
        with act.Fori(0, ATT_HEADS // 2) as i:
            dil.scalar(act, i)

    def dil_vector(dve, st):
        v = nc.vector
        st(v.memset(EP[:, 2:3], -0.5 / DIL_SCALE))
        st.wait()
        with dve.Fori(0, ATT_HEADS // 2) as i:
            st.enter(i, 2 * 2 + 16 * 3)

            def head(s):
                st.link(v.scalar_tensor_tensor(BIAS[:], DIST[:], EP[:, 2:3], LOGC[:], ALU.mult, ALU.add))
                st.link(v.tensor_scalar(EP[:, 2:3], EP[:, 2:3], 0.5, None, ALU.mult))
            dil.vector(dve, st, i, head)
            st.leave(ATT_HEADS // 2)
        dve.wait_ge(SPILLED, 32)
        dil.turn_vector(dve, lambda f: ACC[:, f])

    (S5L, S5DT, S5R, S5T, S5P, S5CT, S5CC, S5GP, S5GT, S5GIN, S5CA, S5K, S5KC, S5Z, S5TOE, UD, UGL, S5S, S5ROT, S5V, S5Yp, S5YC,
     YD, S5YL, S5YU, S5G, S5ZH, S5ZL, S5GLU, MIXH, MIXL) = (sem("s5_" + n) for n in (
        "parameters", "dt", "angle", "trig", "phasor", "c_turned", "c_ready", "g_ready", "g_turned", "g_copied", "ca_ready",
        "kernel", "kernel_copied", "toeplitz_zero", "toeplitz", "u_stored", "u_loaded", "inputs", "inputs_read", "states", "y",
        "y_copied", "y_stored", "y_loaded", "y_skip", "gelu", "z_hi", "z_lo", "glu", "mixed_hi", "mixed_lo"))
    U_D = nc.dram_tensor("s5_u", [512, SEQ], F32, kind="Internal").ap()
    Y_D = nc.dram_tensor("s5_y", [512, SEQ], F32, kind="Internal").ap()

    def slot(k):
        return SM[:, 32 + 16 * k:48 + 16 * k]

    (ARE, AIM, DTS, XX, TH, RED, KK, SN, CM, EX, EM, CO, W1, W2, W3, W4, W5) = (slot(k) for k in range(17))

    def s5_half(t, k):
        return t[:, 16 * (k // 2):16 * (k // 2) + 16].rearrange("p (q r) m -> p q r m", r=2)[:, :, k % 2]

    def s5_bank(k):
        return (PA, PB, PS[0], PS[1])[k][:].rearrange("p (q m) -> p q m", q=8)

    def s5_loads(eng):
        eng.wait_ge(dil.out_read, 64)
        ld = lambda d, s: eng.dma_start(d, s, allow_slow_non_contiguous=True).then_inc(S5L, 16)
        ld(ARE, ins["a_re_2"][0].rearrange("(q r) p -> (r p) q", r=2))
        ld(AIM, ins["a_im_2"][0].rearrange("(q r) p -> (r p) q", r=2))
        ldt = ins["log_dt_2"].rearrange("o (q r) -> o r q", r=2)
        for r in range(2):
            ld(DTS[64 * r:64 * r + 64], ldt[:, r].broadcast_to([64, S5_Q]))
        for k, (b, c) in enumerate((("b_re_2", "c_re_2"), ("b_im_2", "c_im_2"))):
            ld(BR[:, k], ins[b][0].rearrange("(q r) p c -> (r p) q c", r=2))
            ld(CN[:, k], ins[c][0].rearrange("(t g) c p -> (g c) t p", t=4))
        eng.wait_ge(PS_READ[(B_MIX + 15) % 2], times(B_MIX + 15))
        eng.wait_ge(PS_READ[(B_MIX + 14) % 2], times(B_MIX + 14))
        eng.dma_start(U_D.rearrange("(i p) t -> p i t", p=P), MU[:]).then_inc(UD, 16)
        nc.gpsimd.memset(TOE[:], 0.0).then_inc(S5Z, 1)
        eng.wait_ge(S5Z, 1)
        eng.wait_ge(UD, 16)
        eng.wait_ge(S5GT, 4)
        u = U_D.rearrange("(g c) (j n) -> j c g n", c=S5_CH, j=S5_T)
        for j in range(S5_T):
            eng.dma_start(UG[16 * j:16 * j + 16], u[j]).then_inc(UGL, 16)
        eng.wait_ge(S5KC, 4)
        for j in range(S5_T):
            eng.dma_start(TOE[16 * j:16 * j + 16, :, 16 * j:], K0S[0:16, :, 0:P - 16 * j]).then_inc(S5TOE, 16)
        eng.wait_ge(S5YC, 4)
        y = Y_D.rearrange("(g c) (j n) -> j c g n", c=S5_CH, j=S5_T)
        for j in range(S5_T):
            eng.dma_start(y[j], UG[16 * j:16 * j + 16]).then_inc(YD, 16)
        eng.wait_ge(YD, 16 * S5_T)
        eng.dma_start(S5Y[:], Y_D.rearrange("(i p) t -> p i t", p=P)).then_inc(S5YL, 16)

    def s5_vector(dve, st):
        v = nc.vector
        tt, stt, ts = v.tensor_tensor, v.scalar_tensor_tensor, v.tensor_scalar
        L = st.link

        def cmul(out, a, b, tmp, neg=False):
            L(tt(out[0], a[0], b[0], ALU.mult))
            L(tt(tmp, a[1], b[1], ALU.mult))
            L(tt(out[0], out[0], tmp, ALU.subtract))
            L(tt(out[1], a[0], b[1], ALU.mult))
            L(tt(tmp, a[1], b[0], ALU.mult))
            L(tt(out[1], out[1], tmp, ALU.add))

        dve.wait_ge(S5DT, 1)
        L(tt(XX, DTS, ARE, ALU.mult))
        L(tt(TH, DTS, AIM, ALU.mult))
        wrap(st, RED, KK, TH, 0.0)
        L(ts(KK, RED, 0.5, None, ALU.mult))
        v.tensor_copy(EP[:, 3:4], EP[:, 0:1]).then_inc(S5R, 1)
        dve.wait_ge(S5T, 4)
        L(stt(CM, CM, -2.0, CM, ALU.mult, ALU.mult))
        L(ts(CO, CM, 1.0, None, ALU.add))
        L(stt(EM, EX, 1.0, EM, ALU.add, ALU.mult))
        L(v.memset(PW[:, 0, 0], 1.0))
        L(v.memset(PW[:, 1, 0], 0.0))
        L(tt(PW[:, 0, 1], EX, CO, ALU.mult))
        L(tt(PW[:, 1, 1], EX, SN, ALU.mult))
        L(tt(W1, EM, CO, ALU.mult))
        L(tt(W1, W1, CM, ALU.add))
        wim = PW[:, 1, 1]
        L(tt(W2, ARE, ARE, ALU.mult))
        L(tt(W3, AIM, AIM, ALU.mult))
        L(tt(W2, W2, W3, ALU.add))
        L(v.reciprocal(W2, W2))
        L(tt(W3, W1, ARE, ALU.mult))
        L(tt(W4, wim, AIM, ALU.mult))
        L(tt(W3, W3, W4, ALU.add))
        L(tt(W3, W3, W2, ALU.mult))
        L(tt(W4, wim, ARE, ALU.mult))
        L(tt(W5, W1, AIM, ALU.mult))
        L(tt(W4, W4, W5, ALU.subtract))
        L(tt(W4, W4, W2, ALU.mult))
        over_c = lambda t: t.unsqueeze(2).broadcast_to([P, S5_Q, S5_CH])
        cmul((BB[:, 0], BB[:, 1]), (over_c(W3), over_c(W4)), (BR[:, 0], BR[:, 1]), BTMP[:])
        for k in range(2, S5_T + 1):
            cmul((PW[:, 0, k], PW[:, 1, k]), (PW[:, 0, k - 1], PW[:, 1, k - 1]), (PW[:, 0, 1], PW[:, 1, 1]), W1)
        for k in range(S5_T):
            c = slice(16 * (S5_T - 1 - k), 16 * (S5_T - k))
            cmul((GP[:, 0, :, c], GP[:, 1, :, c]), (over_c(PW[:, 0, k]), over_c(PW[:, 1, k])), (BB[:, 0], BB[:, 1]), BTMP[:])
        v.tensor_copy(EP[:, 3:4], EP[:, 0:1]).then_inc(S5GP, 1)
        dve.wait_ge(S5CC, 2)
        shape = [P, S5_Q, S5_T + 1, S5_CH]
        c = [CC[:, k].unsqueeze(2).broadcast_to(shape) for k in range(2)]
        a = [PW[:, k].rearrange("p k q -> p q k").unsqueeze(3).broadcast_to(shape) for k in range(2)]
        cmul((CA[:, 0], CA[:, 1]), c, a, CTMP[:])
        ts(CA[:, 1], CA[:, 1], -1.0, None, ALU.mult).then_inc(S5CA, 1)
        def square():
            L(tt(W1, CO, CO, ALU.mult))
            L(tt(W2, SN, SN, ALU.mult))
            L(stt(SN, CO, 2.0, SN, ALU.mult, ALU.mult))
            L(tt(CO, W1, W2, ALU.subtract))
        for _ in range(3):
            square()
            L(tt(EX, EX, EX, ALU.mult))
        L(v.memset(RE[:, :, 0:1], 1.0))
        L(v.memset(RI[:, :, 0:1], 0.0))
        m = 1
        while m < S5_N:
            b = [t.unsqueeze(2).broadcast_to([P, S5_Q, m]) for t in (CO, SN)]
            cmul((RE[:, :, m:2 * m], RI[:, :, m:2 * m]), (RE[:, :, 0:m], RI[:, :, 0:m]), b, VI[:, :, 0:m])
            square()
            m *= 2
        dve.wait_ge(S5KC, 4)
        dve.wait_ge(S5TOE, 16 * S5_T)
        for h, (pr, pi) in enumerate(((PA, PB), (PS[0], PS[1]))):
            q = slice(8 * h, 8 * h + 8)
            flat = lambda t: t[:, q].rearrange("p q n -> p (q n)")
            dve.wait_ge(S5S, h + 1)
            L(tt(flat(VR), pr[:], flat(RE), ALU.mult))
            L(tt(flat(SR), pi[:], flat(RI), ALU.mult))
            L(tt(flat(VR), flat(VR), flat(SR), ALU.add))
            L(tt(flat(VI), pi[:], flat(RE), ALU.mult))
            tt(flat(SI), pr[:], flat(RI), ALU.mult).then_inc(S5ROT, 1)
            dve.wait_ge(S5ROT, h + 1)
            L(tt(flat(VI), flat(VI), flat(SI), ALU.subtract))
        L(v.tensor_copy(RMT[:], EX.unsqueeze(2).broadcast_to([P, S5_Q, S5_N])))
        L(v.memset(RMT[:, :, 0:1], 0.0))
        whole = lambda t: t[:].rearrange("p q n -> p (q n)")
        st(v.tensor_tensor_scan(whole(SR), whole(RMT), whole(VR), 0.0, ALU.mult, ALU.add))
        L(v.tensor_tensor_scan(whole(SI), whole(RMT), whole(VI), 0.0, ALU.mult, ALU.add))
        for t in (VR, VI):
            L(v.memset(t[:, :, 0:1], 0.0))
        first, last = (lambda t: t[:, :, 0:S5_N - 1]), (lambda t: t[:, :, 1:])
        cmul((last(VR), last(VI)), (first(SR), first(SI)), (first(RE), first(RI)), first(TMP))
        v.tensor_copy(EP[:, 3:4], EP[:, 0:1]).then_inc(S5V, 1)
        dve.wait_ge(S5YL, 16)
        for k in range(4):
            stt(S5Y[:, k], MU[:, k], vec("dsk", k), S5Y[:, k], ALU.mult, ALU.add).then_inc(S5YU, 1)
        for k in range(4):
            dve.wait_ge(S5ZH, k + 1)
            tt(ZL[:, k], ACC[:, 4 + k], ZH[:, k].bitcast(F32), ALU.subtract).then_inc(S5ZL, 1)
        for m in range(4):
            b = B_GLU + m
            dve.wait_ge(PS_READ[b % 2], times(b))
            tt(ACC[:, 4 + m], ACC[:, 4 + m], T[m % 2][:], ALU.mult).then_inc(S5GLU, 1)
            split_lo(dve, b + 2, cols=cols_of(b + 2))
        for k in range(KT):
            dve.wait_ge(MIXH, k + 1)
            tt(XL[:, k], ACC[:, k], XH[:, k].bitcast(F32), ALU.subtract).then_inc(MIXL, 1)
        for m in range(KT):
            b = B_MIXOUT + m
            dve.wait_ge(BLOCK_DONE[b % 2], times(b))
            v.tensor_copy(ACC[:, m], PS[b % 2][:]).then_inc(PS_READ[b % 2], 1)
            split_lo(dve, b + 2, cols=cols_of(b + 2))

    def s5_scalar(act):
        act.wait_ge(S5L, 16 * 8)
        nc.scalar.activation(DTS, DTS, ACT.Exp).then_inc(S5DT, 1)
        act.wait_ge(S5CT, 1)
        for r in range(2):
            src = PA[0:64].rearrange("p (k q r c) -> p k q r c", k=2, q=S5_Q, r=2)[:, :, :, r]
            nc.scalar.activation(CC[64 * r:64 * r + 64], src, ACT.Copy).then_inc(S5CC, 1)
        act.wait_ge(S5R, 1)
        for dst, src, f, sc in ((EX, XX, ACT.Exp, 1.0), (EM, XX, ACT.Tanh, 0.5), (SN, RED, ACT.Sin, 1.0), (CM, KK, ACT.Sin, 1.0)):
            nc.scalar.activation(dst, src, f, scale=sc).then_inc(S5T, 1)
        for k in range(4):
            act.wait_ge(S5GT, k + 1)
            nc.scalar.activation(GIN[:, 4 * k:4 * k + 4].rearrange("p q r m -> p (q r m)"), PAB[k % 2][:], ACT.Copy).then_inc(S5GIN, 1)
        for k in range(4):
            act.wait_ge(S5K, k + 1)
            nc.scalar.activation(s5_half(K0S, k)[0:16], s5_bank(k)[0:16], ACT.Copy).then_inc(S5KC, 1)
        for k in range(4):
            act.wait_ge(S5Yp, k + 1)
            nc.scalar.activation(s5_half(UG, k), s5_bank(k), ACT.Copy).then_inc(S5YC, 1)
        for k in range(4):
            act.wait_ge(S5YU, k + 1)
            nc.scalar.activation(by_place(ACC[:, 4 + k]), S5Y[:, k].rearrange("p (j n) -> p n j", j=S5_T), ACT.Gelu_apprx_tanh).then_inc(S5G, 1)
            act.wait_ge(S5G, k + 1)
            nc.scalar.activation(ZH[:, k], ACC[:, 4 + k], ACT.Copy).then_inc(S5ZH, 1)
        for m in range(4):
            b = B_GLU + m
            act.wait_ge(BLOCK_DONE[b % 2], times(b))
            if m >= 2:
                act.wait_ge(S5GLU, m - 1)
            nc.scalar.activation(T[m % 2][:], PS[b % 2][:], ACT.Sigmoid, bias=vec("bglu", m)).then_inc(PS_READ[b % 2], 1)
            split_hi(act, b + 2, cols=cols_of(b + 2))
        for k in range(KT):
            if k >= 4:
                act.wait_ge(S5GLU, k - 3)
            nc.scalar.activation(XH[:, k], ACC[:, k], ACT.Copy).then_inc(MIXH, 1)
        for m in range(KT):
            split_hi(act, B_MIXOUT + m + 2, cols=cols_of(B_MIXOUT + m + 2))

    def s5_tensor(pe):
        pe.wait_ge(S5L, 16 * 8)
        pe.wait_ge(dil.out_copied, 4)
        for k in range(2):
            for t in range(4):
                last = nc.tensor.transpose(PA[0:64, (4 * k + t) * P:(4 * k + t + 1) * P], CN[:, k, t], IDENT[:])
        last.then_inc(S5CT, 1)
        pe.wait_ge(S5CC, 2)
        pe.wait_ge(S5GP, 1)
        for k in range(4):
            if k >= 2:
                pe.wait_ge(S5GIN, k - 1)
            for t in range(8):
                q, ri = 4 * k + t // 2, t % 2
                last = nc.tensor.transpose(PAB[k % 2][:, t * P:(t + 1) * P], GP[:, ri, q], IDENT[:])
            last.then_inc(S5GT, 1)
        pe.wait_ge(S5CA, 1)
        pe.wait_ge(S5GIN, 4)
        for h, pair in enumerate(((PA, PB), (PS[0], PS[1]))):
            for r in range(2):
                rows = slice(64 * r, 64 * r + 64)
                for t in range(8):
                    for ri in range(2):
                        last = nc.tensor.matmul(pair[r][0:16, t * P:(t + 1) * P], BB[rows, ri, 8 * h + t],
                                                CA[rows, ri, 8 * h + t, 0:S5_T].rearrange("p k c -> p (k c)"),
                                                start=(ri == 0), stop=(ri == 1))
                last.then_inc(S5K, 1)
        pe.wait_ge(UGL, 16 * S5_T)
        pe.wait_ge(S5KC, 4)
        for h, pair in enumerate(((PA, PB), (PS[0], PS[1]))):
            for t in range(8):
                q = 8 * h + t
                for r in range(2):
                    rows = slice(64 * r, 64 * r + 64)
                    for ri in range(2):
                        last = nc.tensor.matmul(pair[ri][rows, t * P:(t + 1) * P], GIN[:, q, ri, rows], UG[:, 2 * q + r], start=True, stop=True)
            last.then_inc(S5S, 1)
        pe.wait_ge(S5V, 1)
        pe.wait_ge(S5TOE, 16 * S5_T)
        pe.wait_ge(S5ROT, 2)
        for h, pair in enumerate(((PA, PB), (PS[0], PS[1]))):
            for r in range(2):
                rows = slice(64 * r, 64 * r + 64)
                for t in range(8):
                    q = 8 * h + t
                    y = pair[r][:, t * P:(t + 1) * P]
                    nc.tensor.matmul(y, TOE[:, 2 * q + r], UG[:, 2 * q + r], start=True, stop=False)
                    for ri, s in enumerate((VR, VI)):
                        last = nc.tensor.matmul(y, CA[rows, ri, q, 1:].rearrange("p k c -> p (k c)"), s[rows, q],
                                                start=False, stop=(ri == 1))
                last.then_inc(S5Yp, 1)
        pe.wait_ge(S5YC, 4)
        for m in range(4):
            block_products(pe, B_GLU + m, ZH, ZL, kt=4, after=(lambda k: pe.wait_ge(S5ZL, k + 1)) if m == 0 else None)
        for m in range(KT):
            block_products(pe, B_MIXOUT + m, XH, XL, after=(lambda k: pe.wait_ge(MIXL, k + 1)) if m == 0 else None)

    def s5_sync(sp):
        wg = ins["w_glu_2"][0].rearrange("(k p) c -> p k c", p=P)
        for m in range(4):
            load_block(sp, B_GLU + m, wg[:, :, m * P:(m + 1) * P], cols=512, kt=4)
        wo = ins["w_mix_out_2"][0].rearrange("(k p) c -> p k c", p=P)
        for m in range(KT):
            load_block(sp, B_MIXOUT + m, wo[:, :, m * P:(m + 1) * P])

    FTURN, FCOPY, OUT_DMA = sem("final_turned"), sem("final_copied"), [sem(f"out_stored{s}") for s in range(2)]

    def out_tensor(pe):
        for t in range(TT):
            pe.wait_ge(XRDY, 4 * KT)
            if t >= 2:
                pe.wait_ge(FCOPY, t - 1)
            for k in range(KT):
                last = nc.tensor.transpose(PAB[t % 2][:, k * P:(k + 1) * P], ACC[:, k, t * P:(t + 1) * P], IDENT[:])
            last.then_inc(FTURN, 1)

    def out_scalar(act):
        for t in range(TT):
            act.wait_ge(FTURN, t + 1)
            if t >= 2:
                act.wait_ge(OUT_DMA[t % 2], 16 * (t // 2))
            nc.scalar.activation(T[t % 2][:], PAB[t % 2][:], ACT.Copy).then_inc(FCOPY, 1)

    def out_sync(sp):
        for t in range(TT):
            sp.wait_ge(FCOPY, t + 1)
            sp.dma_start(out[0, t * P:(t + 1) * P, :], T[t % 2][:]).then_inc(OUT_DMA[t % 2], 16)
        for s in range(2):
            sp.wait_ge(OUT_DMA[s], 16 * (TT // 2))

    def last_block_read(b_end):
        return lambda act: (lambda k: act.wait_ge(PS_READ[(b_end - KT + k) % 2], times(b_end - KT + k)))

    block = ctx.enter_context(nc.Block())

    @block.sync
    def _(sp):
        x_sync(sp)
        in1_sync(sp)
        out1_sync(sp)
        dt_sync(sp)
        ssd_sync(sp)
        ffn_sync(sp, B_FFN1, ins["ffn1_w_in_2"][0], ins["ffn1_w_out_2"][0])
        mix_sync(sp)
        s5_sync(sp)
        ffn_sync(sp, B_FFN2, ins["ffn2_w_in_2"][0], ins["ffn2_w_out_2"][0])
        out_sync(sp)

    @block.gpsimd
    def _(pool):
        st = Steps(pool, sem("pool_steps"))
        const_pool(pool, st)
        rg_pool(pool)
        rg_loads(pool)
        mla_loads(pool)
        ssd_pool(pool)
        spill_pool(pool, 0)
        reload_pool(pool, 0, B_MIX - 1)
        spill_pool(pool, 1)
        dist_pool(pool)
        dil_pool(pool)
        s5_loads(pool)
        reload_pool(pool, 1, B_FFN2 - 1)
        spill_pool(pool, 2)
        reload_pool(pool, 2, B_END - 1)

    @block.tensor
    def _(pe):
        x_tensor(pe)
        rope_tensor(pe)
        in1_tensor(pe)
        norm_rows(pe, "q", bufs=NB)
        norm_rows(pe, "kv", bufs=NB)
        rg_tensor(pe)
        mla_tensor(pe)
        out1_tensor(pe)
        ln_tensor(pe, 0, "ln1")
        dt_tensor(pe)
        ssd_tensor(pe)
        ln_tensor(pe, 1, "ln2")
        norm_rows(pe, "f1pre")
        ffn_tensor(pe, 0, B_FFN1)
        norm_rows(pe, "f1post")
        norm_rows(pe, "mpre")
        mix_tensor(pe)
        dil_tensor(pe)
        s5_tensor(pe)
        norm_rows(pe, "mpost")
        norm_rows(pe, "f2pre")
        ffn_tensor(pe, 1, B_FFN2)
        norm_rows(pe, "f2post")
        out_tensor(pe)

    @block.scalar
    def _(act):
        st = Steps(act, sem("act_steps"))
        vecs_sync(act)
        x_scalar(act)
        split_hi(act, 0)
        split_hi(act, 1)
        rope_scalar(act)
        in1_scalar(act)
        latent_norms_scalar(act, st)
        rg_scalar(act)
        mla_scalar(act)
        gate1_scalar(act)
        splits_scalar(act, B_OUT, KT)
        ln_scalar(act, st, 0, "ln1", "ln1_b", True)
        dt_scalar(act)
        ssd_scalar(act, st)
        ln_scalar(act, st, 1, "ln2", "ln2_b", False)
        pre_scalar(act, st, 0, "f1pre")
        ffn_scalar(act, 0, B_FFN1)
        post_scalar(act, st, 0, "f1post", last_block_read(B_MIX)(act))
        pre_scalar(act, st, 1, "mpre")
        mix_scalar(act)
        dil_scalar(act)
        s5_scalar(act)
        post_scalar(act, st, 1, "mpost", last_block_read(B_FFN2)(act))
        pre_scalar(act, st, 2, "f2pre")
        ffn_scalar(act, 1, B_FFN2)
        post_scalar(act, st, 2, "f2post", last_block_read(B_END)(act))
        out_scalar(act)

    @block.vector
    def _(dve):
        st = Steps(dve, sem("dve_steps"))
        x_vector(dve, st)
        split_lo(dve, 0)
        split_lo(dve, 1)
        rope_vector(dve, st)
        in1_vector(dve, st)
        latent_norms_vector(dve, st)
        rg_vector(dve, st)
        mla_vector(dve, st)
        gate1_vector(dve, st)
        acc_vector(dve, st, B_OUT)
        ln_vector(dve, st, 0, "ln1", "ln1_g", B_OUT + 7, True)
        dt_vector(dve, st)
        ssd_vector(dve, st)
        ln_vector(dve, st, 1, "ln2", "ln2_g", B_FFN1 - 1, False)
        pre_vector(dve, 0, "f1pre", "f1_pre")
        ffn_vector(dve, 0, B_FFN1)
        post_vector(dve, 0, "f1post", "f1_post", B_MIX - 1)
        pre_vector(dve, 1, "mpre", "m_pre")
        mix_vector(dve, st)
        dil_vector(dve, st)
        s5_vector(dve, st)
        post_vector(dve, 1, "mpost", "m_post", B_FFN2 - 1)
        pre_vector(dve, 2, "f2pre", "f2_pre")
        ffn_vector(dve, 1, B_FFN2)
        post_vector(dve, 2, "f2post", "f2_post", B_END - 1)


def kernel(**inputs):
    import concourse.bacc as bacc
    from concourse.bass_utils import run_bass_kernel_spmd

    nc = bacc.Bacc("TRN2", target_bir_lowering=False, num_devices=1)
    arrays, ins = {}, {}
    for name, value in inputs.items():
        a = np.ascontiguousarray(value)
        arrays[f"in_{name}_dram"] = a
        ins[name] = nc.dram_tensor(f"in_{name}_dram", a.shape, mybir.dt.from_np(a.dtype), kind="ExternalInput").ap()
    out = nc.dram_tensor("out_dram", (1, SEQ, D), F32, kind="ExternalOutput").ap()
    build(nc, ins, out)
    result = run_bass_kernel_spmd(nc, [arrays], core_ids=[0])
    return result.results[0]["out_dram"]
```

```python
import math
from contextlib import ExitStack

import numpy as np

import concourse.bass as bass
from concourse import mybir

F32 = mybir.dt.float32
F32R = mybir.dt.float32r
I32 = mybir.dt.int32
ALU = mybir.AluOpType
ACT = mybir.ActivationFunctionType

P = 128
SEQ = 1024
D = 1024
KT = D // P
TT = SEQ // P
HALF = 512

RNN = 512
MLA_HEADS, NOPE, ROPE = 8, 64, 32
Q_RANK, KV_RANK = 256, 128
AB_IN = RNN + 1024 + Q_RANK + KV_RANK + ROPE
MLA_SCALE = (NOPE + ROPE) ** -0.5
DN_ALPHA = 4.0 ** 0.25

SSD_INNER, SSD_HEADS, SSD_GROUPS, SSD_P = 2048, 32, 4, 64
HPG = SSD_HEADS // SSD_GROUPS
GW = SSD_INNER // SSD_GROUPS
SSD_CONV = SSD_INNER + 2 * SSD_GROUPS * P

D_FF = 2816
FT = D_FF // P
FFN_PARTS = (8, 7, 7)
ATT_HEADS, HD = 8, 64
NEG = -1.0e30

S5_GROUPS, S5_STATE, S5_CH = 32, 64, 16
S5_T = 8
S5_N = SEQ // S5_T
S5_Q = S5_GROUPS // 2

B_IN = 0
B_OUT = B_IN + 16
B_DT = B_OUT + KT
B_SSD = B_DT + 1
SSD_BLOCKS = 18
B_FFN1 = B_SSD + SSD_GROUPS * SSD_BLOCKS
FFN_BLOCKS = 2 * FT + KT * len(FFN_PARTS)
B_MIX = B_FFN1 + FFN_BLOCKS
B_GLU = B_MIX + 16
B_MIXOUT = B_GLU + 4
B_FFN2 = B_MIXOUT + KT
B_END = B_FFN2 + FFN_BLOCKS

VEC = {}


def _vec_layout():
    at = 0
    for name, n in (("conv_w", 16), ("conv_b", 4), ("ga_b", 4), ("gx_b", 4), ("lam", 4), ("qn", 2), ("kvn", 1),
                    ("ln1_g", 8), ("ln1_b", 8), ("ssd", SSD_GROUPS * 34), ("ln2_g", 8), ("ln2_b", 8),
                    ("f1_pre", 8), ("f1_post", 8), ("m_pre", 8), ("m_post", 8), ("f2_pre", 8), ("f2_post", 8),
                    ("dsk", 4), ("bglu", 4), ("dtb", 32), ("alog", 32), ("ssd_d", 32)):
        VEC[name] = (at, n)
        at += n
    return at


VEC_COLS = _vec_layout()


class Steps:

    def __init__(self, eng, sem):
        self.eng, self.sem, self.n, self.i, self.per = eng, sem, 0, None, 0

    def __call__(self, ins):
        self.n += 1
        ins.then_inc(self.sem, 1)
        return self.n

    def wait(self, mark=None):
        k = self.n if mark is None else mark
        self.eng.wait_ge(self.sem, k if self.i is None else k + self.i * self.per)

    def link(self, ins):
        self(ins)
        self.wait()

    def enter(self, i, per):
        self.i, self.per, self.start = i, per, self.n

    def leave(self, turns):
        assert self.n - self.start == self.per, (self.n - self.start, self.per)
        self.n, self.i = self.start + turns * self.per, None


def build(nc, ins, out):
    ctx = ExitStack()
    with ctx:
        _build(nc, ctx, ins, out)


def _build(nc, ctx, ins, out):
    sems = {}

    def sem(name):
        if name not in sems:
            sems[name] = ctx.enter_context(nc.semaphore(name))
        return sems[name]

    base = 16512
    def at(name, kib, shape, dt=F32):
        return nc.alloc_sbuf_tensor_at(name, shape, dt, offset=base + int(kib * 1024))

    WS = at("WS", 0, [P, 2, 1024])
    WH = at("WH", 8, [P, 2, 1024], F32R)
    WL = at("WL", 16, [P, 2, 1024], F32R)
    IDENT = at("IDENT", 24, [P, P])
    ONES = at("ONES", 24.5, [P, P])
    GT = at("GT", 25, [P, P])
    LE = at("LE", 25.5, [P, P])
    CMASK = at("CMASK", 26, [P, P])
    VT = at("VT", 26.5, [P, VEC_COLS])
    SM = at("SM", 28.25, [P, 320])
    GV = at("GV", 29.5, [P, 34])
    EP = at("EP", 29.65625, [P, 24])
    EDX = at("EDX", 29.75, [P, TT, SSD_HEADS])
    CDEC = at("CDEC", 30.75, [P, TT, SSD_HEADS])
    ACC = at("ACC", 32, [P, KT, SEQ])
    XH = at("XH", 64, [P, KT, SEQ], F32R)
    XL = at("XL", 96, [P, KT, SEQ], F32R)
    HH = at("HH", 128, [P, KT, SEQ], F32R)
    HL = at("HL", 160, [P, KT, SEQ], F32R)
    T = [at(f"T{k}", 192 + 4 * k, [P, SEQ]) for k in range(3)]
    DTT = at("DTT", 204, [P, TT, SSD_HEADS])
    ADT = at("ADT", 205, [P, TT, SSD_HEADS])
    ECS = at("ECS", 206, [P, TT, SSD_HEADS])
    XIN = at("XIN", 128, [P, TT, D])
    G = at("G", 128, [P, KT, SEQ])
    Y = at("Y", 160, [P, KT, SEQ])
    RG = [at(f"RG{k}", 64 + 16 * k, [P, 4, SEQ]) for k in range(4)]
    BD = at("BD", 112, [P, 2, 4, P])
    NB = [at(f"NB{k}", 116 + 4 * k, [P, SEQ]) for k in range(3)]
    POSI = at("POSI", 200, [P, SEQ], I32)
    QT = at("QT", 64, [P, 2, SEQ])
    KTT = at("KTT", 72, [P, 2, SEQ])
    VTOK = at("VTOK", 80, [P, TT, 512])
    PP = at("PP", 96, [P, 2, SEQ])
    PT = at("PT", 104, [P, 2, SEQ])
    YTOK = at("YTOK", 112, [P, TT, 512])
    WUQ = at("WUQ", 204, [P, 2, 2, P])
    WUKV = at("WUKV", 200, [P, 1024])
    WK = at("WK", 206, [P, 2, NOPE])
    COS = at("COS", 192, [P, SEQ])
    SIN = at("SIN", 196, [P, SEQ])
    YGH = at("YGH", 128, [P, 4, SEQ], F32R)
    YGL = at("YGL", 144, [P, 4, SEQ], F32R)
    XST = at("XST", 128, [P, 4, SEQ])
    SYT = at("SYT", 128, [P, TT, GW])
    BT = at("BT", 144, [P, SEQ])
    CT = at("CT", 148, [P, SEQ])
    BTOK = at("BTOK", 152, [P, TT, P])
    PREV = at("PREV", 156, [P, GW])
    YOS = at("YOS", 158, [P, GW])
    ZT = at("ZT", 160, [P, 4, SEQ])
    XTOK = at("XTOK", 176, [P, TT, GW])
    SEGR = at("SEGR", 192, [P, HPG, P])
    DEC = at("DEC", 196, [P, HPG, P])
    XDT = at("XDT", 200, [P, GW])
    XDD = at("XDD", 202, [P, GW])
    CBM = at("CBM", 26, [P, P])
    MQ = at("MQ", 128, [P, 4, SEQ])
    MK = at("MK", 144, [P, 4, SEQ])
    MV = at("MV", 160, [P, TT, 512])
    MU = at("MU", 176, [P, 4, SEQ])
    DIST = at("DIST", 192, [P, SEQ])
    LOGC = at("LOGC", 196, [P, SEQ])
    BIAS = at("BIAS", 200, [P, SEQ])
    UG = at("UG", 64, [P, S5_GROUPS, P])
    GP = at("GP", 80, [P, 2, S5_Q, P])
    TOE = at("TOE", 80, [P, S5_GROUPS, P])
    GIN = at("GIN", 96, [P, S5_Q, 2, P])
    RMT = at("RMT", 192, [P, S5_Q, S5_N])
    TMP = at("TMP", 162, [P, S5_Q, S5_N])
    CA = at("CA", 112, [P, 2, S5_Q, S5_T + 1, S5_CH])
    RE = at("RE", 130, [P, S5_Q, S5_N])
    RI = at("RI", 138, [P, S5_Q, S5_N])
    SR = at("SR", 146, [P, S5_Q, S5_N])
    SI = at("SI", 154, [P, S5_Q, S5_N])
    K0S = at("K0S", 146, [P, S5_GROUPS, P])
    VR = at("VR", 48, [P, S5_Q, S5_N])
    VI = at("VI", 56, [P, S5_Q, S5_N])
    CTMP = at("CTMP", 146, [P, S5_Q, S5_T + 1, S5_CH])
    GTMP = at("GTMP", 32, [P, S5_Q, S5_T, S5_CH])
    PW = at("PW", 48, [P, 2, S5_T + 1, S5_Q])
    BB = at("BB", 50.5, [P, 2, S5_Q, S5_CH])
    CC = at("CC", 52.5, [P, 2, S5_Q, S5_CH])
    BR = at("BR", 54.5, [P, 2, S5_Q, S5_CH])
    BTMP = at("BTMP", 56.5, [P, S5_Q, S5_CH])
    RPW = at("RPW", 57.5, [P, 2, S5_T, S5_Q])
    CN = at("CN", 58.5, [P, 2, 4, S5_STATE])
    S5Y = at("S5Y", 64, [P, 4, SEQ])
    ZH = at("ZH", 128, [P, 4, SEQ], F32R)
    ZL = at("ZL", 144, [P, 4, SEQ], F32R)
    OB = at("OB", 64, [P, 2, SEQ])
    RL = at("RL", 128, [P, KT, SEQ])

    PS = [ctx.enter_context(nc.psum_tensor(f"PS{k}", [P, 1024], F32)) for k in range(2)]
    PA = ctx.enter_context(nc.psum_tensor("PA", [P, 1024], F32))
    PB = ctx.enter_context(nc.psum_tensor("PB", [P, 1024], F32))

    XRES = nc.dram_tensor("x_residual", [KT, P, SEQ], F32, kind="Internal").ap()

    def vec(name, k=0, n=1):
        a = VEC[name][0] + k
        return VT[:, a:a + n]

    W_LOADED = [sem(f"w_loaded{s}") for s in range(2)]
    W_HI = [sem(f"w_hi{s}") for s in range(2)]
    W_LO = [sem(f"w_lo{s}") for s in range(2)]
    BLOCK_DONE = [sem(f"block_done{s}") for s in range(2)]
    PS_READ = [sem(f"ps_read{s}") for s in range(2)]

    def times(b, i=None, per=0):
        n = b // 2 + 1
        return n if i is None else n + i * (per // 2)

    def load_block(sp, b, src, cols=1024, i=None, per=0, kt=KT, view=None):
        s, n = b % 2, times(b, i, per)
        if i is not None or n > 1:
            sp.wait_ge(W_LO[s], n - 1)
        for dst, part in (view(WS[:, s]) if view else [(WS[:, s, 0:cols].rearrange("p (k c) -> p k c", k=kt), src)]):
            sp.dma_start(dst, part).then_inc(W_LOADED[s], 16)

    def split_hi(act, b, i=None, per=0, cols=1024):
        if b >= B_END:
            return
        s, n = b % 2, times(b, i, per)
        act.wait_ge(W_LOADED[s], load_count(b, i, per))
        if i is not None or n > 1:
            act.wait_ge(BLOCK_DONE[s], n - 1)
        nc.scalar.activation(WH[:, s, 0:cols], WS[:, s, 0:cols], ACT.Copy).then_inc(W_HI[s], 1)

    def split_lo(dve, b, i=None, per=0, cols=1024):
        if b >= B_END:
            return
        s, n = b % 2, times(b, i, per)
        dve.wait_ge(W_HI[s], n)
        nc.vector.tensor_tensor(WL[:, s, 0:cols], WS[:, s, 0:cols], WH[:, s, 0:cols].bitcast(F32),
                                ALU.subtract).then_inc(W_LO[s], 1)

    KR_BLOCK = B_IN + 15
    KR_DMAS = 8

    def load_count(b, i=None, per=0):
        n = 16 * (b // 2 + 1)
        if b >= KR_BLOCK and b % 2 == KR_BLOCK % 2:
            n += 16 * (KR_DMAS - 1)
        return n if i is None else n + i * (8 * per)

    def block_products(pe, b, hi, lo, kt=KT, i=None, per=0, after=None, width=P):
        s, n = b % 2, times(b, i, per)
        pe.wait_ge(W_LO[s], n)
        if i is not None or n > 1:
            pe.wait_ge(PS_READ[s], n - 1)
        for k in range(kt):
            if after:
                after(k)
            terms = [(WH, hi), (WH, lo), (WL, hi)]
            for j, (w, x) in enumerate(terms):
                for h in range(2):
                    last = nc.tensor.matmul(PS[s][0:width, h * HALF:(h + 1) * HALF], w[:, s, k * width:(k + 1) * width],
                                            x[:, k, h * HALF:(h + 1) * HALF],
                                            start=(k == 0 and j == 0), stop=(k == kt - 1 and j == 2))
        last.then_inc(BLOCK_DONE[s], 1)

    SQ, SUMMED, RSTD = (sem(n) for n in ("squares", "squares_summed", "rstd"))
    MSUM, MROW = sem("mean_summed"), sem("mean_row_sums")
    NORM = {}
    at_sq = 0
    for name, kts in (("q", 2), ("kv", 1), ("ln1", 8), ("g0", 4), ("g1", 4), ("g2", 4), ("g3", 4), ("ln2", 8),
                      ("f1pre", 8), ("f1post", 8), ("mpre", 8), ("mpost", 8), ("f2pre", 8), ("f2post", 8)):
        NORM[name] = (len(NORM), at_sq, kts)
        at_sq += kts

    def norm_squares(act, name, x, wait=None, i=None, bufs=T):
        turn, sq0, kts = NORM[name]
        d_sq = 0 if i is None else i * kts
        for k in range(kts):
            if wait:
                wait(k)
            if k >= 2:
                act.wait_ge(SUMMED, sq0 + k - 1 + d_sq)
            nc.scalar.activation(bufs[k % 2][:], x(k), ACT.Square).then_inc(SQ, 1)

    def norm_rstd(act, steps, name, n, eps, i=None, bufs=T):
        turn, sq0, kts = NORM[name]
        act.wait_ge(SUMMED, sq0 + kts + (0 if i is None else i * kts))
        steps.link(nc.scalar.activation(bufs[0][:], PA[:], ACT.Ln, bias=EP[:, eps:eps + 1], scale=1.0 / n))
        nc.scalar.activation(bufs[1][:], bufs[0][:], ACT.Exp, scale=-0.5).then_inc(RSTD, 1)

    def norm_rows(pe, name, i=None, bufs=T):
        turn, sq0, kts = NORM[name]
        d_sq = 0 if i is None else i * kts
        for k in range(kts):
            pe.wait_ge(SQ, sq0 + k + 1 + d_sq)
            for h in range(2):
                last = nc.tensor.matmul(PA[:, h * HALF:(h + 1) * HALF], ONES[:], bufs[k % 2][:, h * HALF:(h + 1) * HALF],
                                        start=(k == 0), stop=(k == kts - 1))
            last.then_inc(SUMMED, 1)

    X_OK = sem("x_parts")
    CONST, VECS = sem("constants"), sem("vectors_loaded")
    EPS6, EPS5 = 0, 1

    def const_pool(pool, st):
        ms = nc.gpsimd.memset
        for tile in (IDENT, CMASK):
            st(ms(tile[:], 0.0))
        st(ms(ONES[:], 1.0))
        st(ms(SM[:], 0.0))
        st(ms(EP[:, 0:1], 1e-6))
        st(ms(EP[:, 1:2], 1e-5))
        st(ms(EP[:, 2:3], 0.5))
        st.wait()
        sel = nc.gpsimd.affine_select
        st(sel(out=IDENT[:], in_=IDENT[:], compare_op=ALU.not_equal, fill=1.0, base=0, pattern=[[-1, P]], channel_multiplier=1))
        st(sel(out=CMASK[:], in_=CMASK[:], compare_op=ALU.is_ge, fill=NEG, base=0, pattern=[[-1, P]], channel_multiplier=1))
        st(sel(out=GT[:], in_=ONES[:], compare_op=ALU.is_gt, fill=0.0, base=0, pattern=[[-1, P]], channel_multiplier=1))
        st(sel(out=LE[:], in_=ONES[:], compare_op=ALU.is_ge, fill=0.0, base=0, pattern=[[1, P]], channel_multiplier=-1))
        for k in range(ROPE // 2):
            f = float(np.float32(10000.0) ** np.float32(-2.0 * k / ROPE))
            for half, sign in ((0, -1.0), (1, 1.0)):
                c = NOPE + 16 * half + k
                st(ms(SM[0:1, c:c + 1], f))
                st(ms(SM[0:1, P + c:P + c + 1], sign))
        st.wait()
        ms(EP[:, 20:21], 0.0).then_inc(CONST, 1)


    def vec_loads():
        rows = lambda a: a.rearrange("(k p) -> p k", p=P)
        yield vec("conv_w", 0, 16).rearrange("p (t k) -> p t k", k=4), ins["ab_conv_w"][0].rearrange("k (t p) -> p t k", p=P)
        for name, src in (("conv_b", "ab_conv_b"), ("ga_b", "ab_gate_a_b"), ("gx_b", "ab_gate_x_b"), ("lam", "ab_lambda"),
                          ("qn", "mla_q_norm"), ("kvn", "mla_kv_norm"), ("ln1_g", "ab_ln_g"), ("ln1_b", "ab_ln_b"),
                          ("ln2_g", "ssd_ln_g"), ("ln2_b", "ssd_ln_b"), ("f1_pre", "ffn1_pre_g_2"),
                          ("f1_post", "ffn1_post_g_2"), ("m_pre", "mix_pre_g_2"), ("m_post", "mix_post_g_2"),
                          ("f2_pre", "ffn2_pre_g_2"), ("f2_post", "ffn2_post_g_2"), ("dsk", "d_skip_2"), ("bglu", "b_glu_2")):
            yield vec(name, 0, VEC[name][1]), rows(ins[src][0])
        for g in range(SSD_GROUPS):
            for c0, n, ch in ((0, 4, g * GW), (4, 1, SSD_INNER + g * P), (5, 1, SSD_INNER + SSD_GROUPS * P + g * P)):
                yield (vec("ssd", 34 * g + 4 * c0, 4 * n).rearrange("p (t k) -> p t k", k=4),
                       ins["ssd_conv_w"][0][:, ch:ch + n * P].rearrange("k (t p) -> p t k", p=P))
                yield vec("ssd", 34 * g + 24 + c0, n), rows(ins["ssd_conv_b"][0][ch:ch + n * P])
            yield vec("ssd", 34 * g + 30, 4), rows(ins["ssd_norm"][0][g * GW:(g + 1) * GW])
        for name, src in (("dtb", "ssd_dt_bias"), ("alog", "ssd_a_log"), ("ssd_d", "ssd_d")):
            yield vec(name, 0, SSD_HEADS), ins[src].broadcast_to([P, SSD_HEADS])


    def vecs_sync(eng):
        eng.dma_start(POSI[NOPE:NOPE + ROPE, :], ins["positions"].broadcast_to([ROPE, SEQ])).then_inc(VECS1, 16)
        for n, (d, s) in enumerate(vec_parts()):
            eng.dma_start(d, s, allow_slow_non_contiguous=True).then_inc(VECS1 if n < 8 else VECS, 16)

    def vec_parts():
        for dst, src in vec_loads():
            yield from [(dst[:, t], src[:, t]) for t in range(dst.shape[1])] if len(dst.shape) == 3 else [(dst, src)]

    VECS1 = sem("first_vectors_loaded")
    N_VECS1 = 16 * 9
    N_VECS = 16 * (len(list(vec_parts())) - 8)

    XLD = [sem(f"x_tile_loaded{s}") for s in range(TT)]
    XTURNED, XHI, XCOP = sem("x_tile_turned"), sem("x_tile_hi"), sem("x_tile_copied")
    PAB = (PA, PB)

    def x_sync(sp):
        for t in range(TT):
            sp.dma_start(XIN[:, t], ins["x"][0, t * P:(t + 1) * P, :]).then_inc(XLD[t], 16)

    def x_tensor(pe):
        pe.wait_ge(CONST, 1)
        for t in range(TT):
            pe.wait_ge(XLD[t], 16)
            if t >= 2:
                pe.wait_ge(X_OK, t - 1)
            for k in range(KT):
                last = nc.tensor.transpose(PAB[t % 2][:, k * P:(k + 1) * P], XIN[:, t, k * P:(k + 1) * P], IDENT[:])
            last.then_inc(XTURNED, 1)

    def x_scalar(act):
        for t in range(TT):
            act.wait_ge(XCOP, t + 1)
            nc.scalar.activation(XH[:, :, t * P:(t + 1) * P], ACC[:, :, t * P:(t + 1) * P], ACT.Copy).then_inc(XHI, 1)

    def x_vector(dve, st):
        for t in range(TT):
            tok = slice(t * P, (t + 1) * P)
            dve.wait_ge(XTURNED, t + 1)
            nc.vector.tensor_copy(ACC[:, :, tok], PAB[t % 2][:].rearrange("p (k c) -> p k c", k=KT)).then_inc(XCOP, 1)
            dve.wait_ge(XHI, t + 1)
            nc.vector.tensor_tensor(XL[:, :, tok], ACC[:, :, tok], XH[:, :, tok].bitcast(F32), ALU.subtract).then_inc(X_OK, 1)
            dve.wait_ge(X_OK, t + 1)
            st(nc.vector.tensor_scalar(ACC[:, :, tok], ACC[:, :, tok], DN_ALPHA, None, ALU.mult))

    MAGIC, INV2PI = 12582912.0, 1.0 / (2.0 * math.pi)
    C1 = 6.28125
    C2 = float(np.float32(np.floor((2 * math.pi - C1) * 2 ** 20) / 2 ** 20))
    C3 = float(np.float32(2 * math.pi - C1 - C2))
    PI_LOW = 3.1415925

    def wrap(st, r, k, x, turns):
        v = nc.vector
        st.link(v.tensor_scalar(k, x, INV2PI, turns, ALU.mult, ALU.add))
        st.link(v.tensor_scalar(k, k, MAGIC, None, ALU.add))
        st.link(v.tensor_scalar(k, k, -MAGIC, None, ALU.add))
        st.link(v.scalar_tensor_tensor(r, k, -C1, x, ALU.mult, ALU.add))
        st.link(v.scalar_tensor_tensor(r, k, -C2, r, ALU.mult, ALU.add))
        st.link(v.scalar_tensor_tensor(r, k, -C3, r, ALU.mult, ALU.add))
        st.link(v.tensor_scalar(r, r, 2 * math.pi * turns, PI_LOW, ALU.add, ALU.min))
        st.link(v.tensor_scalar(r, r, -PI_LOW, None, ALU.max))

    def log1p_exp(st, q, s, e):
        v = nc.vector
        st.link(v.tensor_scalar(q, e, 2.0, None, ALU.add))
        st.link(v.reciprocal(s, q))
        st.link(v.tensor_tensor(s, s, e, ALU.mult))
        st.link(v.tensor_tensor(e, s, s, ALU.mult))
        st.link(v.tensor_scalar(q, e, 1.0 / 19, None, ALU.mult))
        for k in range(8, 0, -1):
            st.link(v.scalar_tensor_tensor(q, q, 1.0 / (2 * k + 1), e, ALU.add, ALU.mult))
        st.link(v.scalar_tensor_tensor(q, q, 1.0, s, ALU.add, ALU.mult))
        st.link(v.tensor_scalar(q, q, 2.0, None, ALU.mult))

    ROPE_F, ROPE_R, SWAP1 = sem("rope_columns"), sem("rope_angles"), sem("rope_swapped")
    TRIG = sem("rope_tables")
    LAM_ABS, LAM_EXP = sem("lambda_abs"), sem("lambda_exp")
    RR = slice(NOPE, NOPE + ROPE)
    RS_ = slice(NOPE + ROPE, P)
    w_ab = ins["ab_w_in"][0].rearrange("(k p) c -> p k c", p=P)

    def in1_cols(j):
        return j * P if j < 4 else (RNN + (j - 4) * P if j < 12 else RNN + 1024 + (j - 12) * P)

    def kr_view(ws):
        w = ws.rearrange("p (k c) -> p k c", k=KT)
        c0 = AB_IN - ROPE
        for r in range(4):
            for half in range(2):
                src = c0 + 16 * (half if r % 2 == 0 else 1 - half)
                yield w[:, :, 32 * r + 16 * half:32 * r + 16 * half + 16], w_ab[:, :, src:src + 16]

    def in1_sync(sp):
        for j in range(15):
            if j == 2:
                vecs_sync(sp)
            load_block(sp, B_IN + j, w_ab[:, :, in1_cols(j):in1_cols(j) + P])
        load_block(sp, KR_BLOCK, None, view=kr_view)

    def rope_tensor(pe):
        pe.wait_ge(X_OK, TT)
        nc.tensor.matmul(PB[:, 0:1], SM[0:1, 0:P], ONES[0:1, 0:1], start=True, stop=True)
        nc.tensor.matmul(PB[:, 1:2], SM[0:1, P:2 * P], ONES[0:1, 0:1], start=True, stop=True).then_inc(ROPE_F, 1)

    def rope_vector(dve, st, part):
        v = nc.vector
        lam = vec("lam", 0, 4)
        if part == 0:
            dve.wait_ge(ROPE_F, 1)
            st.link(v.tensor_copy(SM[:, 300:302], PB[:, 0:2]))
            st.link(v.tensor_copy(COS[RR], POSI[RR]))
            st.link(v.tensor_scalar(T[2][RR], COS[RR], SM[RR, 300:301], None, ALU.mult))
            wrap(st, SIN[RR], PB[RR], T[2][RR], 0.0)
        elif part == 1:
            wrap(st, COS[RR], PB[RR], T[2][RR], 0.25)
            v.tensor_copy(SM[:, 302:303], SM[:, 301:302]).then_inc(ROPE_R, 1)
        elif part == 2:
            dve.wait_ge(TRIG, 1)
            st.link(v.tensor_scalar(SIN[RR], SIN[RR], SM[RR, 301:302], None, ALU.mult))
            st.link(v.tensor_scalar(SM[:, 256:260], lam, -1.0, None, ALU.mult))
            v.tensor_tensor(SM[:, 260:264], SM[:, 256:260], lam, ALU.max).then_inc(LAM_ABS, 1)
        else:
            dve.wait_ge(LAM_EXP, 1)
            log1p_exp(st, SM[:, 264:268], SM[:, 268:272], SM[:, 272:276])
            st.link(v.tensor_scalar(SM[:, 256:260], SM[:, 256:260], 0.0, None, ALU.max))
            st.link(v.tensor_tensor(SM[:, 264:268], SM[:, 264:268], SM[:, 256:260], ALU.add))
            st.link(v.tensor_scalar(SM[:, 264:268], SM[:, 264:268], -8.0, None, ALU.mult))

    def rope_scalar(act, part):
        if part == 0:
            act.wait_ge(ROPE_R, 1)
            nc.scalar.activation(COS[RR], COS[RR], ACT.Sin)
            nc.scalar.activation(SIN[RR], SIN[RR], ACT.Sin).then_inc(TRIG, 1)
        else:
            act.wait_ge(LAM_ABS, 1)
            nc.scalar.activation(SM[:, 272:276], SM[:, 260:264], ACT.Exp, scale=-1.0).then_inc(LAM_EXP, 1)

    def conv(st, dst, b, taps, bias, last_sem):
        v, src = nc.vector, PS[b % 2]
        st.link(v.tensor_scalar(dst, src[:], taps(3), bias, ALU.mult, ALU.add))
        for d in range(1, 4):
            i_ = v.scalar_tensor_tensor(dst[:, d:], src[:, :SEQ - d], taps(3 - d), dst[:, d:], ALU.mult, ALU.add)
            if d < 3:
                st.link(i_)
        i_.then_inc(last_sem, 1)

    def in1_tensor(pe):
        pe.wait_ge(X_OK, TT)
        for j in range(16):
            block_products(pe, B_IN + j, XH, XL)
            if j == 1:
                rope_tensor(pe)

    def in1_scalar(act):
        for j in range(16):
            b = B_IN + j
            if 4 <= j < 12:
                act.wait_ge(BLOCK_DONE[b % 2], times(b))
                nc.scalar.activation(G[:, j - 4], PS[b % 2][:], ACT.Silu).then_inc(PS_READ[b % 2], 1)
            if j == 15:
                act.wait_ge(BLOCK_DONE[b % 2], times(b))
                act.wait_ge(ROPE_R, 1)
                nc.scalar.activation(T[2][RR], PS[b % 2][RS_], ACT.Copy).then_inc(SWAP1, 1)
            split_hi(act, b + 2)
            if j in (8, 10):
                rope_scalar(act, (j - 8) // 2)

    def in1_vector(dve, st):
        dve.wait_ge(VECS1, N_VECS1)
        for j in range(16):
            b = B_IN + j
            if not 4 <= j < 12:
                dve.wait_ge(BLOCK_DONE[b % 2], times(b))
            if j < 4:
                conv(st, Y[:, j], b, lambda k: vec("conv_w", 4 * j + k), vec("conv_b", j), PS_READ[b % 2])
            elif 12 <= j < 15:
                nc.vector.tensor_copy(Y[:, j - 8], PS[b % 2][:]).then_inc(PS_READ[b % 2], 1)
            elif j == 15:
                st(nc.vector.tensor_tensor(Y[RR, 7], PS[b % 2][RR], COS[RR], ALU.mult))
                dve.wait_ge(SWAP1, 1)
                st.link(nc.vector.tensor_tensor(T[2][RR], T[2][RR], SIN[RR], ALU.mult))
                nc.vector.tensor_tensor(Y[RR, 7], Y[RR, 7], T[2][RR], ALU.add).then_inc(PS_READ[b % 2], 1)
            split_lo(dve, b + 2)
            if j in (5, 7, 9, 11):
                rope_vector(dve, st, (j - 5) // 2)

    BDZ, BDL = sem("gate_weights_zeroed"), sem("gate_weights_loaded")
    RGP, RGS, RGA, RGW, RGM, RGU = (sem(n) for n in ("rg_products", "rg_gates", "rg_decays", "rg_squares", "rg_roots", "rg_scanned"))
    RGR, RGI, RGAA = RG[0], RG[1], RG[2]

    def rg_pool(pool):
        pool.wait_ge(BLOCK_DONE[KR_BLOCK % 2], times(KR_BLOCK))
        nc.gpsimd.memset(BD[:], 0.0).then_inc(BDZ, 1)

    def rg_loads(sp):
        sp.wait_ge(BDZ, 1)
        for k, name in enumerate(("ab_gate_a_w", "ab_gate_x_w")):
            w = ins[name][0].rearrange("(t r) i j -> r i t j", r=2)
            for r in range(2):
                sp.dma_start(BD[64 * r:64 * r + 64, k, :, 64 * r:64 * r + 64], w[r]).then_inc(BDL, 16)

    def rg_tensor(pe):
        pe.wait_ge(BDL, 64)
        for s in range(2):
            pe.wait_ge(PS_READ[s], 8)
        for t in range(4):
            if t:
                pe.wait_ge(RGS, 2 * t)
            for k in range(2):
                for h in range(2):
                    last = nc.tensor.matmul(PAB[k][:, h * HALF:(h + 1) * HALF], BD[:, k, t], Y[:, t, h * HALF:(h + 1) * HALF],
                                            start=True, stop=True)
                last.then_inc(RGP, 1)

    def rg_scalar(act, st):
        for t in range(4):
            for k, (dst, b) in enumerate(((RGR, "ga_b"), (RGI, "gx_b"))):
                act.wait_ge(RGP, 2 * t + k + 1)
                nc.scalar.activation(dst[:, t], PAB[k][:], ACT.Sigmoid, bias=vec(b, t)).then_inc(RGS, 1)
        act.wait_ge(RGS, 8)
        for t in range(4):
            c = SM[:, 264 + t:265 + t]
            nc.scalar.activation(RGAA[:, t], RGR[:, t], ACT.Exp, scale=c).then_inc(RGA, 1)
            act.wait_ge(RGA, 2 * t + 1)
            nc.scalar.activation(RGR[:, t], RGR[:, t], ACT.Tanh, scale=c).then_inc(RGA, 1)
        q_norm_scalar(act, st)
        for t in range(4):
            act.wait_ge(RGW, t + 1)
            nc.scalar.activation(RGR[:, t], RGR[:, t], ACT.Sqrt, scale=-1.0).then_inc(RGM, 1)
        kv_norm_scalar(act, st)

    def rg_vector(dve, st):
        v = nc.vector
        for t in range(4):
            dve.wait_ge(RGA, 2 * t + 2)
            st.link(v.tensor_tensor(NB[0][:], RGAA[:, t], RGAA[:, t], ALU.mult))
            v.scalar_tensor_tensor(RGR[:, t], NB[0][:], 1.0, RGR[:, t], ALU.add, ALU.mult).then_inc(RGW, 1)
            st.link(v.tensor_tensor(RGI[:, t], RGI[:, t], Y[:, t], ALU.mult))
        q_norm_vector(dve, st)
        for t in range(4):
            dve.wait_ge(RGM, t + 1)
            st.link(v.tensor_tensor(RGI[:, t], RGI[:, t], RGR[:, t], ALU.mult))
            v.tensor_tensor_scan(Y[:, t], RGAA[:, t], RGI[:, t], 0.0, ALU.mult, ALU.add).then_inc(RGU, 1)
        kv_norm_vector(dve, st)

    class Attention:

        def __init__(self, name, keys, scale):
            self.keys, self.scale = keys, scale
            self.scored, self.neg_max, self.probs = (sem(f"{name}_{what}") for what in ("scored", "neg_max", "probs"))
            self.probs_turned, self.probs_t = (sem(f"{name}_{what}") for what in ("probs_turned", "probs_t"))
            self.weighted, self.out_read = (sem(f"{name}_{what}") for what in ("weighted", "out_read"))
            self.out_turned, self.out_copied = (sem(f"{name}_{what}") for what in ("out_turned", "out_copied"))

        def queries(self, s):
            return QT[0:self.keys, s] if self.keys != HD else QT[HD * s:HD * s + HD, 0]

        def key_tile(self, s):
            return KTT[0:self.keys, s] if self.keys != HD else KTT[HD * s:HD * s + HD, 0]

        def tensor(self, pe, i, values):
            n = 16 * i
            for j in range(18):
                if j < 17:
                    for q in ([0, 1] if j == 0 else [j + 1]):
                        if q > 15:
                            continue
                        s, qb = divmod(q, TT)
                        if q >= 2:
                            pe.wait_ge(self.probs, n + q - 1)
                        for c in range(0, qb + 1, 4):
                            m = min(4, qb + 1 - c)
                            last = nc.tensor.matmul(PS[q % 2][:, c * P:(c + m) * P], self.queries(s)[:, qb * P:(qb + 1) * P],
                                                    self.key_tile(s)[:, c * P:(c + m) * P], start=True, stop=True)
                        last.then_inc(self.scored, 1)
                if j < 16:
                    pe.wait_ge(self.probs, n + j + 1)
                    if j:
                        pe.wait_ge(self.probs_t, n + j)
                    for kb in range(j % TT + 1):
                        last = nc.tensor.transpose(PA[:, kb * P:(kb + 1) * P], PP[:, j % 2, kb * P:(kb + 1) * P], IDENT[:])
                    last.then_inc(self.probs_turned, 1)
                if 1 <= j < 17:
                    q = j - 1
                    pe.wait_ge(self.probs_t, n + q + 1)
                    if q >= 2:
                        pe.wait_ge(self.out_read, n + q - 1)
                    for kb in range(q % TT + 1):
                        last = nc.tensor.matmul(PB[:, (q % 2) * HALF:(q % 2) * HALF + 2 * HD], PT[:, q % 2, kb * P:(kb + 1) * P],
                                                values(kb, i), start=(kb == 0), stop=(kb == q % TT))
                    last.then_inc(self.weighted, 1)

        def scalar(self, act, i):
            n = 16 * i
            for j in range(17):
                if j < 16:
                    qb = j % TT
                    act.wait_ge(self.neg_max, n + j + 1)
                    if j >= 2:
                        act.wait_ge(self.probs_turned, n + j - 1)
                    if j >= 4:
                        act.wait_ge(self.out_read, n + j - 3)
                    nc.scalar.activation(PP[:, j % 2, 0:(qb + 1) * P], PS[j % 2][:, 0:(qb + 1) * P], ACT.Exp,
                                         bias=SM[:, 8 + j % 4:9 + j % 4], scale=self.scale,
                                         accum_out=SM[:, 16 + j % 4:17 + j % 4]).then_inc(self.probs, 1)
                if j:
                    q = j - 1
                    act.wait_ge(self.probs_turned, n + q + 1)
                    if q >= 2:
                        act.wait_ge(self.weighted, n + q - 1)
                    w = (q % TT + 1) * P
                    nc.scalar.activation(PT[:, q % 2, 0:w], PA[:, 0:w], ACT.Copy).then_inc(self.probs_t, 1)

        def vector(self, dve, st, i, head):
            n = 16 * i
            v = nc.vector
            for j in range(18):
                if j < 16:
                    s, qb = divmod(j, TT)
                    if qb == 0:
                        head(s)
                    if j >= 4:
                        dve.wait_ge(self.probs, n + j - 3)
                    dve.wait_ge(self.scored, n + j + 1)
                    st(v.memset(SM[:, 31:32], 0.0))
                    w = (qb + 1) * P
                    st.link(v.tensor_tensor_reduce(PS[j % 2][:, 0:w], PS[j % 2][:, 0:w], BIAS[:, SEQ - w:], 1.0, NEG, ALU.add,
                                                   ALU.max, SM[:, j % 4:j % 4 + 1]))
                    v.tensor_scalar(SM[:, 8 + j % 4:9 + j % 4], SM[:, j % 4:j % 4 + 1], -self.scale, None,
                                    ALU.mult).then_inc(self.neg_max, 1)
                if j >= 2:
                    q = j - 2
                    s, qb = divmod(q, TT)
                    dve.wait_ge(self.weighted, n + q + 1)
                    st.link(v.reciprocal(SM[:, 24 + q % 4:25 + q % 4], SM[:, 16 + q % 4:17 + q % 4]))
                    v.tensor_scalar(YTOK[:, qb, bass.ds(2 * HD * i + HD * s, HD)], PB[:, (q % 2) * HALF + HD * s:(q % 2) * HALF + HD * s + HD],
                                    SM[:, 24 + q % 4:25 + q % 4], None, ALU.mult).then_inc(self.out_read, 1)

        def turn_tensor(self, pe):
            pe.wait_ge(self.out_read, 64)
            for f in range(4):
                if f >= 2:
                    pe.wait_ge(self.out_copied, f - 1)
                for t in range(TT):
                    last = nc.tensor.transpose(PAB[f % 2][:, t * P:(t + 1) * P], YTOK[:, t, f * P:(f + 1) * P], IDENT[:])
                last.then_inc(self.out_turned, 1)

        def turn_vector(self, dve, dst):
            for f in range(4):
                dve.wait_ge(self.out_turned, f + 1)
                nc.vector.tensor_copy(dst(f), PAB[f % 2][:]).then_inc(self.out_copied, 1)

    QN = sem("latents_normed")
    WQL = [sem(f"head_weights{s}") for s in range(2)]
    WKVL, VPROD, VCOP, QKP, QKC, QKR = (sem(n) for n in ("w_ukv_loaded", "v_products", "v_copied", "qk_products", "qk_copied", "qk_rotated"))
    mla = Attention("mla", NOPE + ROPE, MLA_SCALE)
    w_uq = ins["mla_w_uq"][0].rearrange("(k p) c -> p k c", p=P)
    w_ukv = ins["mla_w_ukv"][0]

    LB = (NB[1], NB[2])

    def q_norm_scalar(act, st):
        norm_squares(act, "q", lambda k: Y[:, 4 + k], bufs=LB)
        norm_rstd(act, st, "q", Q_RANK, EPS6, bufs=LB)

    def kv_norm_scalar(act, st):
        act.wait_ge(QN, 2)
        norm_squares(act, "kv", lambda k: Y[:, 6], bufs=LB)
        norm_rstd(act, st, "kv", KV_RANK, EPS6, bufs=LB)

    def q_norm_vector(dve, st):
        dve.wait_ge(VECS, N_VECS)
        for name in ("f1_post", "f2_post"):
            st.link(nc.vector.tensor_scalar(vec(name, 0, 8), vec(name, 0, 8), 0.5, None, ALU.mult))
        dve.wait_ge(RSTD, 1)
        for k in range(2):
            nc.vector.scalar_tensor_tensor(Y[:, 4 + k], Y[:, 4 + k], vec("qn", k), NB[2][:], ALU.mult, ALU.mult).then_inc(QN, 1)

    def kv_norm_vector(dve, st):
        dve.wait_ge(RSTD, 2)
        nc.vector.scalar_tensor_tensor(Y[:, 6], Y[:, 6], vec("kvn"), NB[2][:], ALU.mult, ALU.mult).then_inc(QN, 1)

    def mla_loads(sp):
        sp.wait_ge(PS_READ[1], 8)
        sp.dma_start(WUKV[:], w_ukv).then_inc(WKVL, 16)
        sp.wait_ge(TRIG, 1)
        for s in range(2):
            head_weights(sp, 0, s)
        with sp.Fori(1, MLA_HEADS // 2) as i:
            sp.wait_ge(QKP, 2 * i)
            for s in range(2):
                head_weights(sp, i, s)

    def head_weights(sp, i, s):
        c = (NOPE + ROPE) * 2 * i + (NOPE + ROPE) * s
        sp.dma_start(WUQ[:, s, :, 0:96], w_uq[:, :, bass.ds(c, 96)]).then_inc(WQL[s], 16)
        sp.dma_start(WUQ[:, s, :, 96:112], w_uq[:, :, bass.ds(c + 80, 16)]).then_inc(WQL[s], 16)
        sp.dma_start(WUQ[:, s, :, 112:128], w_uq[:, :, bass.ds(c + 64, 16)]).then_inc(WQL[s], 16)
        sp.dma_start(WK[:, s], w_ukv[:, bass.ds(2 * P * i + P * s, NOPE)]).then_inc(WQL[s], 16)

    def mla_tensor(pe):
        pe.wait_ge(WKVL, 16)
        pe.wait_ge(RGU, 4)
        pe.wait_ge(QN, 3)
        for t in range(TT):
            if t >= 2:
                pe.wait_ge(VCOP, t - 1)
            nc.tensor.matmul(PAB[t % 2][:, 0:HALF].rearrange("p (h c) -> p h c", h=MLA_HEADS), Y[:, 6, t * P:(t + 1) * P],
                             WUKV[:].rearrange("p (h c) -> p h c", h=MLA_HEADS)[:, :, NOPE:], start=True,
                             stop=True).then_inc(VPROD, 1)
        pe.wait_ge(VCOP, TT)
        with pe.Fori(0, MLA_HEADS // 2) as i:
            for s, (q, k) in enumerate(((PA, PB), (PS[0], PS[1]))):
                pe.wait_ge(WQL[s], 64 * i + 64)
                for h in range(2):
                    c = slice(h * HALF, (h + 1) * HALF)
                    for kt in range(2):
                        nc.tensor.matmul(q[:, c], WUQ[:, s, kt], Y[:, 4 + kt, c], start=(kt == 0), stop=(kt == 1))
                    last = nc.tensor.matmul(k[0:NOPE, c], WK[:, s], Y[:, 6, c], start=True, stop=True)
                last.then_inc(QKP, 1)
            pe.wait_ge(QKR, 2 * i + 2)
            mla.tensor(pe, i, lambda kb, i: VTOK[:, kb, bass.ds(2 * HD * i, 2 * HD)])
            pe.wait_ge(mla.out_read, 16 * i + 16)
        mla.turn_tensor(pe)

    def mla_scalar(act):
        for t in range(TT):
            act.wait_ge(VPROD, t + 1)
            nc.scalar.activation(VTOK[:, t], PAB[t % 2][:, 0:HALF], ACT.Copy).then_inc(VCOP, 1)
        with act.Fori(0, MLA_HEADS // 2) as i:
            for s, (q, k) in enumerate(((PA, PB), (PS[0], PS[1]))):
                act.wait_ge(QKP, 2 * i + s + 1)
                nc.scalar.activation(QT[0:NOPE, s], q[0:NOPE], ACT.Copy)
                nc.scalar.activation(PP[RR, s], q[RS_], ACT.Copy).then_inc(QKC, 1)
            mla.scalar(act, i)

    def mla_vector(dve, st):
        v = nc.vector
        for s in range(2):
            st(v.tensor_copy(KTT[RR, s], Y[RR, 7]))
        dve.wait_ge(VPROD, TT)
        st(v.memset(BIAS[:, 0:SEQ - P], 0.0))
        st.link(v.tensor_copy(BIAS[:, SEQ - P:], CMASK[:]))
        PER = 2 * 3 + 16 * 3
        with dve.Fori(0, MLA_HEADS // 2) as i:
            st.enter(i, PER)
            for s, (q, k) in enumerate(((PA, PB), (PS[0], PS[1]))):
                dve.wait_ge(QKP, 2 * i + s + 1)
                st(v.tensor_copy(KTT[0:NOPE, s], k[0:NOPE]))
                dve.wait_ge(QKC, 2 * i + s + 1)
                st(v.tensor_tensor(QT[RR, s], q[RR], COS[RR], ALU.mult))
                st.link(v.tensor_tensor(PP[RR, s], PP[RR, s], SIN[RR], ALU.mult))
                v.tensor_tensor(QT[RR, s], QT[RR, s], PP[RR, s], ALU.add).then_inc(QKR, 1)
            mla.vector(dve, st, i, lambda s: None)
            st.leave(MLA_HEADS // 2)
        mla.turn_vector(dve, lambda f: Y[:, 4 + f])

    GHI = sem("gated")

    def gate1_vector(dve, st):
        for k in range(KT):
            if k >= 4:
                dve.wait_ge(mla.out_copied, k - 3)
            elif k == 0:
                dve.wait_ge(RGU, 4)
            if k >= 2:
                dve.wait_ge(X_OK, TT + k - 1)
            nc.vector.tensor_tensor(T[k % 2][:], Y[:, k], G[:, k], ALU.mult).then_inc(GHI, 1)
            if k:
                gate1_lo(dve, k - 1)
        gate1_lo(dve, KT - 1)

    def gate1_lo(dve, k):
        dve.wait_ge(XHI, TT + k + 1)
        nc.vector.tensor_tensor(HL[:, k], T[k % 2][:], HH[:, k].bitcast(F32), ALU.subtract).then_inc(X_OK, 1)

    def gate1_scalar(act):
        for k in range(KT):
            act.wait_ge(GHI, k + 1)
            nc.scalar.activation(HH[:, k], T[k % 2][:], ACT.Copy).then_inc(XHI, 1)

    w_ab_out = ins["ab_w_out"][0].rearrange("(k p) c -> p k c", p=P)

    def out1_sync(sp):
        for m in range(KT):
            load_block(sp, B_OUT + m, w_ab_out[:, :, m * P:(m + 1) * P])

    def out1_tensor(pe):
        for m in range(KT):
            block_products(pe, B_OUT + m, HH, HL, after=(lambda k: pe.wait_ge(X_OK, TT + k + 1)) if m == 0 else None)

    def acc_vector(dve, st, b0, n=KT):
        for m in range(n):
            b = b0 + m
            dve.wait_ge(BLOCK_DONE[b % 2], times(b))
            nc.vector.tensor_tensor(ACC[:, m], ACC[:, m], PS[b % 2][:], ALU.add).then_inc(PS_READ[b % 2], 1)
            split_lo(dve, b + 2)

    def splits_scalar(act, b0, n):
        for b in range(b0, b0 + n):
            split_hi(act, b + 2)

    XRDY = sem("stream_ready")
    CEN, LNS, LNB = sem("centred"), sem("ln_scaled"), sem("ln_biased")

    def ln_vector(dve, st, turn, name, g, b_last, split):
        v = nc.vector
        dve.wait_ge(PS_READ[(b_last - 1) % 2], times(b_last - 1))
        dve.wait_ge(PS_READ[b_last % 2], times(b_last))
        st.link(v.tensor_tensor(T[2][:], ACC[:, 0], ACC[:, 1], ALU.add))
        for k in range(2, KT):
            i_ = v.tensor_tensor(T[2][:], T[2][:], ACC[:, k], ALU.add)
            if k < KT - 1:
                st.link(i_)
        i_.then_inc(MSUM, 1)
        dve.wait_ge(MROW, turn + 1)
        for k in range(KT):
            v.scalar_tensor_tensor(ACC[:, k], PB[:], -1.0 / D, ACC[:, k], ALU.mult, ALU.add).then_inc(CEN, 1)
        dve.wait_ge(RSTD, NORM[name][0] + 1)
        for k in range(KT + 2):
            if k < KT:
                v.scalar_tensor_tensor(ACC[:, k], ACC[:, k], vec(g, k), T[1][:], ALU.mult, ALU.mult).then_inc(LNS, 1)
            if split and k >= 2:
                dve.wait_ge(LNB, 2 * k - 2)
                v.tensor_tensor(XL[:, k - 2], ACC[:, k - 2], XH[:, k - 2].bitcast(F32), ALU.subtract).then_inc(X_OK, 1)
        if split:
            for k in range(KT):
                if k == 0:
                    dve.wait_ge(X_OK, 3 * KT)
                st(v.tensor_scalar(ACC[:, k], ACC[:, k], DN_ALPHA, None, ALU.mult))

    def ln_tensor(pe, turn, name):
        pe.wait_ge(MSUM, turn + 1)
        for h in range(2):
            last = nc.tensor.matmul(PB[:, h * HALF:(h + 1) * HALF], ONES[:], T[2][:, h * HALF:(h + 1) * HALF], start=True, stop=True)
        last.then_inc(MROW, 1)
        norm_rows(pe, name)

    def ln_scalar(act, st, turn, name, b, split):
        norm_squares(act, name, lambda k: ACC[:, k], wait=lambda k: act.wait_ge(CEN, KT * turn + k + 1))
        norm_rstd(act, st, name, D, EPS5)
        for k in range(KT):
            act.wait_ge(LNS, KT * turn + k + 1)
            nc.scalar.activation(ACC[:, k], ACC[:, k], ACT.Identity, bias=vec(b, k)).then_inc(LNB if split else XRDY, 1)
            if split:
                act.wait_ge(LNB, 2 * k + 1)
                nc.scalar.activation(XH[:, k], ACC[:, k], ACT.Copy).then_inc(LNB, 1)

    DTT_T = sem("dt_turned")
    DTX, DTE, DTA, DTP, DTD, ALE = (sem(n) for n in ("dt_abs", "dt_exp", "a_dt", "decay_sums", "decays", "a_exp"))
    w_ssd = ins["ssd_w_in"][0].rearrange("(k p) c -> p k c", p=P)

    def dt_sync(sp):
        load_block(sp, B_DT, w_ssd[:, :, SSD_INNER + SSD_CONV:], cols=KT * SSD_HEADS)

    def dt_tensor(pe):
        block_products(pe, B_DT, XH, XL, width=SSD_HEADS, after=lambda k: pe.wait_ge(X_OK, 2 * KT + k + 1))
        pe.wait_ge(PS_READ[B_DT % 2], times(B_DT))
        for t in range(TT):
            last = nc.tensor.transpose(PB[:, t * SSD_HEADS:(t + 1) * SSD_HEADS], XST[0:SSD_HEADS, 0, t * P:(t + 1) * P],
                                       IDENT[0:SSD_HEADS, 0:SSD_HEADS])
        last.then_inc(DTT_T, 1)
        pe.wait_ge(DTA, 1)
        adt = ADT[:].rearrange("p t h -> p (t h)")
        n = TT * SSD_HEADS
        nc.tensor.matmul(PA[:, 0:n], LE[:], adt, start=True, stop=True)
        nc.tensor.matmul(PA[:, HALF:HALF + n], GT[:], adt, start=True, stop=True)
        nc.tensor.matmul(PB[:, 0:n], ONES[:], adt, start=True, stop=True).then_inc(DTP, 1)

    def dt_vector(dve, st):
        v = nc.vector
        flat = lambda t: t[:].rearrange("p t h -> p (t h)")
        dve.wait_ge(BLOCK_DONE[B_DT % 2], times(B_DT))
        v.tensor_copy(XST[0:SSD_HEADS, 0], PS[B_DT % 2][0:SSD_HEADS]).then_inc(PS_READ[B_DT % 2], 1)
        split_lo(dve, B_DT + 2, cols=1024)
        dve.wait_ge(DTT_T, 1)
        st.link(v.tensor_tensor(DTT[:], PB[:, 0:TT * SSD_HEADS].rearrange("p (t c) -> p t c", t=TT),
                                vec("dtb", 0, 32).unsqueeze(1).broadcast_to([P, TT, SSD_HEADS]), ALU.add))
        e, s, q = (SEGR[:, k * 2:k * 2 + 2].rearrange("p a b -> p (a b)") for k in range(3))
        st.link(v.tensor_scalar(s, flat(DTT), -1.0, None, ALU.mult))
        v.tensor_tensor(e, s, flat(DTT), ALU.max).then_inc(DTX, 1)
        st(v.tensor_scalar(DTT[:], DTT[:], 0.0, None, ALU.max))
        dve.wait_ge(DTE, 1)
        log1p_exp(st, q, s, e)
        st.link(v.tensor_tensor(flat(DTT), flat(DTT), q, ALU.add))
        dve.wait_ge(ALE, 1)
        v.scalar_tensor_tensor(ADT[:], DTT[:], -1.0, vec("alog", 0, 32).unsqueeze(1).broadcast_to([P, TT, SSD_HEADS]),
                               ALU.mult, ALU.mult).then_inc(DTA, 1)
        dve.wait_ge(DTD, 3)
        st.link(v.tensor_tensor(EDX[:], EDX[:], DTT[:], ALU.mult))

    def dt_scalar(act):
        split_hi(act, B_DT + 2)
        act.wait_ge(DTX, 1)
        e = SEGR[:, 0:2].rearrange("p a b -> p (a b)")
        nc.scalar.activation(e, e, ACT.Exp, scale=-1.0).then_inc(DTE, 1)
        a = vec("alog", 0, 32)
        nc.scalar.activation(a, a, ACT.Exp).then_inc(ALE, 1)
        act.wait_ge(DTP, 1)
        n = TT * SSD_HEADS
        for dst, src in ((ECS, PA[:, 0:n]), (EDX, PA[:, HALF:HALF + n]), (CDEC, PB[:, 0:n])):
            nc.scalar.activation(dst[:].rearrange("p t h -> p (t h)"), src, ACT.Exp).then_inc(DTD, 1)

    (SSILU, STURN, SCOPY, SSEGR, SSEG, SCB, SDEC, SMR, SYO, SYD, SST, SXD, SXDD, SSK, SPREV, SYT_OK,
     SYTURN, SGATED, SNS, SYGH, SYGL) = (sem("ssd_" + n) for n in (
        "silu", "turned", "turned_copied", "segment_rows", "segment_sums", "cb", "decay",
        "mixing", "y_off", "y_diag", "states", "x_dt", "x_decayed", "skip", "state_ready", "y_ready",
        "y_turned", "gated", "normed", "y_hi", "y_lo"))
    SPSC = sem("ssd_state_decayed")
    w_ssd_out = ins["ssd_w_out"][0]
    GDT, GAD, GEC, GEX, GCD = (SM[:, 64 * k:64 * k + 64].rearrange("p (t h) -> p t h", h=HPG) for k in range(5))
    GSK = EP[:, 8:16]
    CONVD = ((XST, 0), (XST, 1), (XST, 2), (XST, 3), (BT, None), (CT, None))

    def conv_dst(j):
        t, k = CONVD[j]
        return t[:] if k is None else t[:, k]

    def ssd_cols(j):
        if j < 4:
            return SSD_INNER + j * P, GW
        if j < 6:
            return 2 * SSD_INNER + (j - 4) * SSD_GROUPS * P, P
        return (j - 6) * P, GW

    def ssd_sync(sp):
        with sp.Fori(0, SSD_GROUPS) as i:
            for j in range(10):
                c0, step = ssd_cols(j)
                load_block(sp, B_SSD + j, w_ssd[:, :, bass.ds((i * (step // P) + c0 // P) * P, P)], i=i, per=SSD_BLOCKS)
            for m in range(KT):
                src = w_ssd_out[bass.ds(i * GW, GW), m * P:(m + 1) * P].rearrange("(k p) c -> p k c", p=P)
                load_block(sp, B_SSD + 10 + m, src, cols=512, kt=4, i=i, per=SSD_BLOCKS)

    def cols_of(b):
        j = (b - B_SSD) % SSD_BLOCKS
        return 512 if (B_SSD <= b < B_FFN1 and j >= 10) or B_GLU <= b < B_MIXOUT else 1024

    def ssd_tensor(pe):
        with pe.Fori(0, SSD_GROUPS) as i:
            for j in range(10):
                block_products(pe, B_SSD + j, XH, XL, i=i, per=SSD_BLOCKS)
                if j >= 6:
                    ssd_turn(pe, i, j - 6, conv_dst(j - 6))
            ssd_turn(pe, i, 4, conv_dst(4))
            ssd_scan_tensor(pe, i)
            for f in range(4):
                if f == 0:
                    pe.wait_ge(SYT_OK, i * TT + TT)
                if f >= 2:
                    pe.wait_ge(SGATED, i * 4 + f - 1)
                for t in range(TT):
                    last = nc.tensor.transpose(PAB[f % 2][:, t * P:(t + 1) * P], SYT[:, t, f * P:(f + 1) * P], IDENT[:])
                last.then_inc(SYTURN, 1)
            pe.wait_ge(SGATED, i * 4 + 3)
            norm_rows(pe, "g0", i=i)
            for m in range(KT):
                block_products(pe, B_SSD + 10 + m, YGH, YGL, kt=4, i=i, per=SSD_BLOCKS,
                               after=(lambda k: pe.wait_ge(SYGL, i * 4 + k + 1)) if m == 0 else None)

    def ssd_turn(pe, i, f, src):
        pe.wait_ge(SSILU, i * 6 + f + 1)
        if f >= 2:
            pe.wait_ge(SCOPY, i * 5 + f - 1)
        for t in range(TT):
            last = nc.tensor.transpose(PAB[f % 2][:, t * P:(t + 1) * P], src[:, t * P:(t + 1) * P], IDENT[:])
        last.then_inc(STURN, 1)

    def ssd_scan_tensor(pe, i):
        pe.wait_ge(SCOPY, i * 5 + 5)
        pe.wait_ge(SSILU, i * 6 + 6)
        pe.wait_ge(PS_READ[B_SSD % 2], times(B_SSD + 8, i, SSD_BLOCKS))
        pe.wait_ge(PS_READ[1 - B_SSD % 2], times(B_SSD + 9, i, SSD_BLOCKS))
        n = i * TT
        for c in range(TT):
            tok = slice(c * P, (c + 1) * P)
            if c == 0:
                ssd_segment_sums(pe, i, 0)
            pe.wait_ge(SPREV, i * (TT + 1) + c + 1)
            nc.tensor.matmul(PS[0][:, 0:GW], CT[:, tok], PREV[:], start=True, stop=True).then_inc(SYO, 1)
            pe.wait_ge(SXDD, n + c + 1)
            nc.tensor.matmul(PS[0][:, HALF:HALF + GW], BTOK[:, c], XDD[:], start=True, stop=True).then_inc(SST, 1)
            if c + 1 < TT:
                pe.wait_ge(SDEC, n + c + 1)
                ssd_segment_sums(pe, i, c + 1)
            pe.wait_ge(SXD, n + c + 1)
            pe.wait_ge(SMR, n + c + 1)
            if c:
                pe.wait_ge(SYT_OK, n + c)
            for h in range(HPG):
                last = nc.tensor.matmul(PB[:, HALF + h * SSD_P:HALF + (h + 1) * SSD_P], DEC[:, h],
                                        XDT[:, h * SSD_P:(h + 1) * SSD_P], start=True, stop=True)
            last.then_inc(SYD, 1)

    def ssd_segment_sums(pe, i, c):
        pe.wait_ge(SSEGR, i * TT + c + 1)
        for h in range(2):
            last = nc.tensor.matmul(PA[:, h * HALF:(h + 1) * HALF], GT[:],
                                    SEGR[:, 4 * h:4 * h + 4].rearrange("p h l -> p (h l)"), start=True, stop=True)
        last.then_inc(SSEG, 1)
        tok = slice(c * P, (c + 1) * P)
        nc.tensor.matmul(PB[:, 0:P], BT[:, tok], CT[:, tok], start=True, stop=True).then_inc(SCB, 1)

    def ssd_scalar(act, st):
        with act.Fori(0, SSD_GROUPS) as i:
            for j in range(10):
                b = B_SSD + j
                if j >= 6:
                    act.wait_ge(BLOCK_DONE[b % 2], times(b, i, SSD_BLOCKS))
                    nc.scalar.activation(ZT[:, j - 6], PS[b % 2][:], ACT.Silu).then_inc(PS_READ[b % 2], 1)
                split_hi(act, b + 2, i=i, per=SSD_BLOCKS, cols=512 if j + 2 >= 10 else 1024)
                if j < 6:
                    act.wait_ge(PS_READ[b % 2], times(b, i, SSD_BLOCKS))
                    nc.scalar.activation(conv_dst(j), conv_dst(j), ACT.Silu).then_inc(SSILU, 1)
                else:
                    ssd_copy(act, i, j - 6)
            ssd_copy(act, i, 4)
            for c in range(TT):
                act.wait_ge(SSEG, i * TT + c + 1)
                if c:
                    act.wait_ge(SYD, i * TT + c)
                nc.scalar.activation(DEC[:].rearrange("p h l -> p (h l)"), PA[:], ACT.Exp).then_inc(SDEC, 1)
            norm_squares(act, "g0", lambda k: ZT[:, k], wait=lambda k: act.wait_ge(SGATED, i * 4 + k + 1), i=i)
            st.enter(i, 1)
            norm_rstd(act, st, "g0", GW, EPS6, i=i)
            st.leave(SSD_GROUPS)
            for k in range(4):
                act.wait_ge(SNS, i * 4 + k + 1)
                nc.scalar.activation(YGH[:, k], ZT[:, k], ACT.Copy).then_inc(SYGH, 1)
            for m in range(KT):
                split_hi(act, B_SSD + 12 + m, i=i, per=SSD_BLOCKS, cols=512 if m < 6 else 1024)

    def ssd_copy(act, i, f):
        act.wait_ge(STURN, i * 5 + f + 1)
        dst = XTOK[:, :, f * P:(f + 1) * P] if f < 4 else BTOK[:]
        nc.scalar.activation(dst, PAB[f % 2][:].rearrange("p (t c) -> p t c", t=TT), ACT.Copy).then_inc(SCOPY, 1)

    def over_p(t, c):
        return t[:, c].unsqueeze(2).broadcast_to([P, HPG, SSD_P])

    heads = lambda t: t.rearrange("p (h c) -> p h c", h=HPG)

    def ssd_vector(dve, st):
        v = nc.vector
        PER = 7 + 6 * 3 + 3 * TT
        with dve.Fori(0, SSD_GROUPS) as i:
            st.enter(i, PER)
            a = VEC["ssd"][0]
            st(v.tensor_copy(GV[:], VT[:, bass.ds(i * 34 + a, 34)]))
            for dst, src in ((GDT, DTT), (GAD, ADT), (GEC, ECS), (GEX, EDX), (GCD, CDEC)):
                st(v.tensor_copy(dst, src[:, :, bass.ds(i * HPG, HPG)]))
            st(v.tensor_copy(GSK, VT[:, bass.ds(i * HPG + VEC["ssd_d"][0], HPG)]))
            st.wait()
            for j in range(10):
                b = B_SSD + j
                if j < 6:
                    dve.wait_ge(BLOCK_DONE[b % 2], times(b, i, SSD_BLOCKS))
                    conv(st, conv_dst(j), b, lambda k: GV[:, 4 * j + k:4 * j + k + 1], GV[:, 24 + j:25 + j], PS_READ[b % 2])
                split_lo(dve, b + 2, i=i, per=SSD_BLOCKS, cols=512 if j + 2 >= 10 else 1024)
            v.memset(PREV[:], 0.0).then_inc(SPREV, 1)
            ssd_segments(dve, i, 0)
            for c in range(TT):
                n = i * TT + c + 1
                dve.wait_ge(SCB, n)
                if c:
                    dve.wait_ge(SMR, n - 1)
                st.link(v.tensor_tensor(CBM[:], PB[:, 0:P], LE[:], ALU.mult))
                if c + 1 < TT:
                    ssd_segments(dve, i, c + 1)
                dve.wait_ge(SDEC, n)
                v.tensor_tensor(DEC[:], DEC[:], CBM[:].unsqueeze(1).broadcast_to([P, HPG, P]), ALU.mult).then_inc(SMR, 1)
                if c:
                    ssd_add_diagonal(dve, i, c - 1)
                dve.wait_ge(SYO, n)
                st.link(v.tensor_tensor(heads(YOS[:]), heads(PS[0][:, 0:GW]), over_p(GEC, c), ALU.mult))
                dve.wait_ge(SPSC, n)
                dve.wait_ge(SST, n)
                v.tensor_tensor(PREV[:], PREV[:], PS[0][:, HALF:HALF + GW], ALU.add).then_inc(SPREV, 1)
                dve.wait_ge(SSK, n)
                st.link(v.tensor_tensor(SYT[:, c], SYT[:, c], YOS[:], ALU.add))
            ssd_add_diagonal(dve, i, TT - 1)
            for f in range(4):
                dve.wait_ge(SYTURN, i * 4 + f + 1)
                v.tensor_tensor(ZT[:, f], ZT[:, f], PAB[f % 2][:], ALU.mult).then_inc(SGATED, 1)
            dve.wait_ge(RSTD, NORM["g0"][0] + 1 + i)
            for k in range(5):
                if k < 4:
                    v.scalar_tensor_tensor(ZT[:, k], ZT[:, k], GV[:, 30 + k:31 + k], T[1][:], ALU.mult, ALU.mult).then_inc(SNS, 1)
                if k:
                    dve.wait_ge(SYGH, i * 4 + k)
                    v.tensor_tensor(YGL[:, k - 1], ZT[:, k - 1], YGH[:, k - 1].bitcast(F32), ALU.subtract).then_inc(SYGL, 1)
            for m in range(KT):
                b = B_SSD + 10 + m
                dve.wait_ge(BLOCK_DONE[b % 2], times(b, i, SSD_BLOCKS))
                v.tensor_tensor(ACC[:, m], ACC[:, m], PS[b % 2][:], ALU.add).then_inc(PS_READ[b % 2], 1)
                split_lo(dve, b + 2, i=i, per=SSD_BLOCKS, cols=512 if m < 6 else 1024)
            st.leave(SSD_GROUPS)

    def ssd_add_diagonal(dve, i, c):
        dve.wait_ge(SYD, i * TT + c + 1)
        nc.vector.tensor_tensor(SYT[:, c], SYT[:, c], PB[:, HALF:HALF + GW], ALU.add).then_inc(SYT_OK, 1)

    def ssd_segments(dve, i, c):
        if c:
            dve.wait_ge(SSEG, i * TT + c)
        nc.vector.tensor_tensor(SEGR[:], LE[:].unsqueeze(1).broadcast_to([P, HPG, P]),
                                GAD[:, c].unsqueeze(2).broadcast_to([P, HPG, P]), ALU.mult).then_inc(SSEGR, 1)

    def ssd_pool(pool):
        g = nc.gpsimd
        with pool.Fori(0, SSD_GROUPS) as i:
            pool.wait_ge(SCOPY, i * 5 + 5)
            for c in range(TT):
                x = heads(XTOK[:, c])
                if c:
                    pool.wait_ge(SST, i * TT + c)
                g.tensor_tensor(heads(XDD[:]), x, over_p(GEX, c), ALU.mult).then_inc(SXDD, 1)
                if c:
                    pool.wait_ge(SYD, i * TT + c)
                g.tensor_tensor(heads(XDT[:]), x, over_p(GDT, c), ALU.mult).then_inc(SXD, 1)
                pool.wait_ge(SYO, i * TT + c + 1)
                g.tensor_tensor(heads(PREV[:]), heads(PREV[:]), over_p(GCD, c), ALU.mult).then_inc(SPSC, 1)
                g.tensor_tensor(heads(SYT[:, c]), x, GSK.unsqueeze(2).broadcast_to([P, HPG, SSD_P]), ALU.mult).then_inc(SSK, 1)

    SPILLED, RESID, NSC, NHI = (sem(n) for n in ("spilled", "residual_loaded", "norm_scaled", "norm_hi"))

    PRE_SQ = (T[0], T[2])

    def pre_vector(dve, turn, name, g):
        v = nc.vector
        dve.wait_ge(RSTD, rstd_no(name))
        tmp = (T[0], T[2])
        for k in range(KT + 1):
            if k < KT:
                if k >= 2:
                    dve.wait_ge(X_OK, XOK_PRE + KT * turn + k - 1)
                v.scalar_tensor_tensor(tmp[k % 2][:], ACC[:, k], vec(g, k), T[1][:], ALU.mult, ALU.mult).then_inc(NSC, 1)
            if k:
                dve.wait_ge(NHI, KT * turn + k)
                v.tensor_tensor(XL[:, k - 1], tmp[(k - 1) % 2][:], XH[:, k - 1].bitcast(F32), ALU.subtract).then_inc(X_OK, 1)

    XOK_PRE = 3 * KT

    def rstd_no(name):
        return NORM[name][0] + 1

    def pre_scalar(act, st, turn, name):
        norm_squares(act, name, lambda k: ACC[:, k], wait=lambda k: act.wait_ge(XRDY, KT * turn + k + 1), bufs=PRE_SQ)
        norm_rstd(act, st, name, D, EPS6)
        tmp = (T[0], T[2])
        for k in range(KT):
            act.wait_ge(NSC, KT * turn + k + 1)
            nc.scalar.activation(XH[:, k], tmp[k % 2][:], ACT.Copy).then_inc(NHI, 1)

    def spill_pool(pool, turn):
        pool.wait_ge(XRDY, KT * (turn + 1))
        pool.dma_start(XRES.rearrange("k p t -> p k t"), ACC[:]).then_inc(SPILLED, 16)

    def reload_pool(pool, turn, b_last):
        pool.wait_ge(SPILLED, 16 * (turn + 1))
        for b in (b_last - 1, b_last):
            pool.wait_ge(BLOCK_DONE[b % 2], times(b))
        pool.dma_start(RL[:], XRES.rearrange("k p t -> p k t")).then_inc(RESID, 16)

    def post_vector(dve, turn, name, g, b_last):
        v = nc.vector
        dve.wait_ge(RSTD, rstd_no(name))
        dve.wait_ge(RESID, 16 * (turn + 1))
        for k in range(KT + 1):
            if k < KT:
                v.scalar_tensor_tensor(ACC[:, k], ACC[:, k], vec(g, k), T[1][:], ALU.mult, ALU.mult).then_inc(POSTS, 1)
            if k:
                dve.wait_ge(POSTS, KT * turn + k)
                v.tensor_tensor(ACC[:, k - 1], ACC[:, k - 1], RL[:, k - 1], ALU.add).then_inc(XRDY, 1)

    POSTS = sem("post_scaled")

    def post_scalar(act, st, turn, name, done):
        norm_squares(act, name, lambda k: ACC[:, k], wait=done)
        norm_rstd(act, st, name, D, EPS6)

    HIDH, HIDL = sem("hidden_hi"), sem("hidden_lo")

    def ffn_sync(sp, b0, w_in, w_out):
        wi = w_in.rearrange("(k p) c -> p k c", p=P)
        b, f0 = b0, 0
        for nf in FFN_PARTS:
            with sp.Fori(0, nf) as i:
                for j in range(2):
                    load_block(sp, b + j, wi[:, :, bass.ds(i * P + f0 * P + j * D_FF, P)], i=i, per=2)
            b += 2 * nf
            with sp.Fori(0, KT // 2) as i:
                for j in range(2):
                    src = w_out[f0 * P:(f0 + nf) * P, bass.ds((i * 2 + j) * P, P)].rearrange("(k p) c -> p k c", p=P)
                    load_block(sp, b + j, src, cols=nf * P, kt=nf, i=i, per=2)
            b += KT
            f0 += nf

    def ffn_tensor(pe, turn, b0):
        x_ready = lambda k: pe.wait_ge(X_OK, XOK_PRE + KT * 2 * turn + k + 1)
        hidden_ready = lambda k: pe.wait_ge(HIDL, FT * turn + f0 + k + 1)
        b, f0 = b0, 0
        for nf in FFN_PARTS:
            with pe.Fori(0, nf) as i:
                for j in range(2):
                    block_products(pe, b + j, XH, XL, i=i, per=2, after=x_ready if f0 == 0 and j == 0 else None)
            b += 2 * nf
            with pe.Fori(0, KT // 2) as i:
                for j in range(2):
                    block_products(pe, b + j, HH, HL, kt=nf, i=i, per=2, after=hidden_ready if j == 0 else None)
            b += KT
            f0 += nf

    def ffn_scalar(act, turn, b0):
        b, f0 = b0, 0
        for nf in FFN_PARTS:
            with act.Fori(0, nf) as i:
                g, u = b % 2, (b + 1) % 2
                act.wait_ge(BLOCK_DONE[g], times(b, i, 2))
                nc.scalar.activation(T[0][:], PS[g][:], ACT.Silu).then_inc(PS_READ[g], 1)
                split_hi(act, b + 2, i=i, per=2)
                act.wait_ge(PS_READ[u], times(b + 1, i, 2))
                nc.scalar.activation(HH[:, bass.ds(i, 1)].rearrange("p a t -> p (a t)"), T[1][:], ACT.Copy).then_inc(HIDH, 1)
                split_hi(act, b + 3, i=i, per=2)
            b += 2 * nf
            turns = KT // 2 - (b + KT == B_END)
            with act.Fori(0, turns) as i:
                for j in range(2):
                    split_hi(act, b + j + 2, i=i, per=2)
            b += KT
            f0 += nf

    def ffn_vector(dve, turn, b0):
        v = nc.vector
        b, f0 = b0, 0
        for nf in FFN_PARTS:
            with dve.Fori(0, nf) as i:
                g, u = b % 2, (b + 1) % 2
                split_lo(dve, b + 2, i=i, per=2)
                dve.wait_ge(PS_READ[g], times(b, i, 2))
                dve.wait_ge(BLOCK_DONE[u], times(b + 1, i, 2))
                v.tensor_tensor(T[1][:], T[0][:], PS[u][:], ALU.mult).then_inc(PS_READ[u], 1)
                dve.wait_ge(HIDH, i + FT * turn + f0 + 1)
                hh = HH[:, bass.ds(i, 1)].rearrange("p a t -> p (a t)").bitcast(F32)
                v.tensor_tensor(HL[:, bass.ds(i, 1)].rearrange("p a t -> p (a t)"), T[1][:], hh, ALU.subtract).then_inc(HIDL, 1)
                split_lo(dve, b + 3, i=i, per=2)
            b += 2 * nf
            if f0 == 0:
                dve.wait_ge(SPILLED, 16 * (1 + 2 * turn))
            turns = KT // 2 - (b + KT == B_END)

            def sum_up(b, j, i, per, split):
                dve.wait_ge(BLOCK_DONE[(b + j) % 2], times(b + j, i, per))
                acc = ACC[:, bass.ds(i * 2 + j, 1)].rearrange("p a t -> p (a t)") if per else ACC[:, KT - 2 + j]
                ps = PS[(b + j) % 2][:]
                (v.tensor_copy(acc, ps) if f0 == 0 else v.tensor_tensor(acc, acc, ps, ALU.add)).then_inc(PS_READ[(b + j) % 2], 1)
                if split:
                    split_lo(dve, b + j + 2, i=i, per=per)
            with dve.Fori(0, turns) as i:
                for j in range(2):
                    sum_up(b, j, i, 2, True)
            if turns < KT // 2:
                for j in range(2):
                    sum_up(b + KT - 2, j, None, 0, False)
            b += KT
            f0 += nf

    MVT, MVC = sem("mix_v_turned"), sem("mix_v_copied")
    w_mix = ins["w_mix_in_2"][0].rearrange("(k p) c -> p k c", p=P)

    def mix_sync(sp):
        for j in range(16):
            load_block(sp, B_MIX + j, w_mix[:, :, j * P:(j + 1) * P])

    def mix_tensor(pe):
        for j in range(16):
            block_products(pe, B_MIX + j, XH, XL, after=(lambda k: pe.wait_ge(X_OK, XOK_PRE + KT + k + 1)) if j == 0 else None)
            if 9 <= j < 13:
                f, b = j - 9, B_MIX + j - 1
                pe.wait_ge(PS_READ[b % 2], times(b))
                if f >= 2:
                    pe.wait_ge(MVC, f - 1)
                for t in range(TT):
                    last = nc.tensor.transpose(PAB[f % 2][:, t * P:(t + 1) * P], T[f % 2][:, t * P:(t + 1) * P], IDENT[:])
                last.then_inc(MVT, 1)

    def mix_scalar(act):
        for j in range(16):
            b = B_MIX + j
            if j < 12:
                act.wait_ge(BLOCK_DONE[b % 2], times(b))
                src = PS[b % 2][:]
                dst = MQ[:, j] if j < 4 else (MK[:, j - 4] if j < 8 else T[j % 2][:])
                if j >= 10:
                    act.wait_ge(MVT, j - 9)
                nc.scalar.activation(dst, src, ACT.Copy).then_inc(PS_READ[b % 2], 1)
            split_hi(act, b + 2, cols=cols_of(b + 2))
            if 9 <= j < 13:
                act.wait_ge(MVT, j - 8)
                nc.scalar.activation(MV[:, :, (j - 9) * P:(j - 8) * P], PAB[(j - 9) % 2][:].rearrange("p (t c) -> p t c", t=TT),
                                     ACT.Copy).then_inc(MVC, 1)
            if j == 1:
                act.wait_ge(S5L, 16 * 8)
                nc.scalar.activation(DTS, DTS, ACT.Exp).then_inc(S5DT, 1)
            if j == 2:
                act.wait_ge(S5R, 1)
                for dst, src, f, sc in ((EX, XX, ACT.Exp, 1.0), (EM, XX, ACT.Tanh, 0.5), (SN, RED, ACT.Sin, 1.0), (CM, KK, ACT.Sin, 1.0)):
                    nc.scalar.activation(dst, src, f, scale=sc).then_inc(S5T, 1)
            if j == 15:
                act.wait_ge(MULT1, 1)
                nc.scalar.activation(LOGC[:], PA[:], ACT.Ln).then_inc(MULT_LN, 1)

    def by_place(t):
        return t.rearrange("p (n j) -> p n j", j=S5_T)

    def mix_vector(dve, st):
        for j in range(16):
            b = B_MIX + j
            if j >= 12:
                dve.wait_ge(BLOCK_DONE[b % 2], times(b))
                nc.vector.tensor_copy(MU[:, j - 12].rearrange("p (j n) -> p n j", j=S5_T), by_place(PS[b % 2][:])).then_inc(PS_READ[b % 2], 1)
            split_lo(dve, b + 2, cols=cols_of(b + 2))
            if 2 <= j < 9:
                s5_powers(dve, st, j - 2)
            if j == 12:
                multiplicity(dve, st)
        dve.wait_ge(MULT_LN, 1)
        st.link(nc.vector.scalar_tensor_tensor(LOGC[:], PB[:], -NEG, LOGC[:], ALU.mult, ALU.add))
        st(nc.vector.tensor_scalar(LOGC[:], LOGC[:], 1.0 / DIL_SCALE, None, ALU.mult))

    DISTI = at("DISTI", 200, [P, SEQ], I32)
    LOGI = at("LOGI", 196, [P, SEQ], I32)
    IOTA, MULT1, MULT_LN, PAIR = (sem(n) for n in ("distances", "multiplicity", "log_multiplicity", "pair_ready"))
    DIL_SCALE = HD ** -0.5
    dil = Attention("dil", HD, DIL_SCALE)

    def dist_pool(pool):
        pool.wait_ge(X_OK, XOK_PRE + 2 * KT)
        nc.gpsimd.iota(DISTI[:], pattern=[[-1, SEQ]], base=SEQ - P, channel_multiplier=1).then_inc(IOTA, 1)

    def multiplicity(dve, st):
        v = nc.vector
        dve.wait_ge(IOTA, 1)
        dve.wait_ge(MVC, 4)
        st.link(v.tensor_copy(DIST[:], DISTI[:]))
        st.link(v.tensor_scalar(LOGI[:], DISTI[:], 3, None, ALU.bitwise_and))
        st.link(v.tensor_scalar(PA[:], LOGI[:], 0.0, None, ALU.is_equal))
        st.link(v.scalar_tensor_tensor(PA[:], DIST[:], 512.0, PA[:], ALU.is_le, ALU.mult))
        st.link(v.tensor_scalar(LOGI[:], DISTI[:], 15, None, ALU.bitwise_and))
        st.link(v.scalar_tensor_tensor(PB[:], LOGI[:], 0.0, PA[:], ALU.is_equal, ALU.add))
        st.link(v.scalar_tensor_tensor(PA[:], DIST[:], 128.0, PB[:], ALU.is_le, ALU.add))
        st.link(v.scalar_tensor_tensor(PB[:], DIST[:], 0.0, PA[:], ALU.is_ge, ALU.mult))
        st.link(v.tensor_scalar(PA[:], PB[:], 1.0, None, ALU.max))
        v.tensor_scalar(PB[:], PB[:], 1.0, -1.0, ALU.min, ALU.add).then_inc(MULT1, 1)

    def pair_pool(pool, i, static):
        for dst, src in ((QT, MQ), (KTT, MK)):
            nc.gpsimd.tensor_copy(dst[:, 0], src[:, i] if static else src[:, bass.ds(i, 1)].rearrange("p a t -> p (a t)")).then_inc(PAIR, 1)

    def dil_pool(pool, st):
        pool.wait_ge(PS_READ[(B_MIX + 14) % 2], times(B_MIX + 14))
        pool.wait_ge(PS_READ[(B_MIX + 15) % 2], times(B_MIX + 15))
        pair_pool(pool, 0, True)
        s5_inputs_pool(pool, st)
        with pool.Fori(1, ATT_HEADS // 2) as i:
            pool.wait_ge(dil.scored, 16 * i)
            pool.wait_ge(PAIR, 2)
            pair_pool(pool, i, False)

    def dil_tensor(pe):
        for b in (B_MIX + 14, B_MIX + 15):
            pe.wait_ge(PS_READ[b % 2], times(b))
        with pe.Fori(0, ATT_HEADS // 2) as i:
            pe.wait_ge(PAIR, 2 * i + 2)
            dil.tensor(pe, i, lambda kb, i: MV[:, kb, bass.ds(2 * HD * i, 2 * HD)])
        dil.turn_tensor(pe)

    def dil_scalar(act):
        with act.Fori(0, ATT_HEADS // 2) as i:
            dil.scalar(act, i)

    def dil_vector(dve, st):
        v = nc.vector
        st(v.memset(EP[:, 2:3], -0.5 / DIL_SCALE))
        st.wait()
        with dve.Fori(0, ATT_HEADS // 2) as i:
            st.enter(i, 2 * 2 + 16 * 3)

            def head(s):
                st.link(v.scalar_tensor_tensor(BIAS[:], DIST[:], EP[:, 2:3], LOGC[:], ALU.mult, ALU.add))
                st.link(v.tensor_scalar(EP[:, 2:3], EP[:, 2:3], 0.5, None, ALU.mult))
            dil.vector(dve, st, i, head)
            st.leave(ATT_HEADS // 2)
        dve.wait_ge(SPILLED, 32)
        dil.turn_vector(dve, lambda f: ACC[:, f])

    (S5L, S5DT, S5R, S5T, S5CT, S5CC, S5GP, S5GT, S5GIN, S5CA, S5K, S5KC, S5Z, S5TOE, UD, UGL, S5S, S5ROT, S5V, S5Yp, S5YC,
     YD, S5YU, S5G, S5ZH, S5ZL, S5GLU, MIXH, MIXL) = (sem("s5_" + n) for n in (
        "parameters", "dt", "angle", "trig", "c_turned", "c_ready", "g_ready", "g_turned", "g_copied", "ca_ready",
        "kernel", "kernel_copied", "toeplitz_zero", "toeplitz", "u_stored", "u_loaded", "inputs", "inputs_read", "states", "y",
        "y_copied", "y_stored", "y_skip", "gelu", "z_hi", "z_lo", "glu", "mixed_hi", "mixed_lo"))
    S5PW = sem("s5_powers")
    S5YL = [sem(f"s5_y_loaded{h}") for h in range(2)]
    U_D = nc.dram_tensor("s5_u", [512, SEQ], F32, kind="Internal").ap()
    Y_D = nc.dram_tensor("s5_y", [512, SEQ], F32, kind="Internal").ap()

    def slot(k):
        return SM[:, 32 + 16 * k:48 + 16 * k]

    (ARE, AIM, DTS, XX, TH, RED, KK, SN, CM, EX, EM, CO, W1, W2, W3, W4, W5) = (slot(k) for k in range(17))

    def s5_half(t, k):
        return t[:, 16 * (k // 2):16 * (k // 2) + 16].rearrange("p (q r) m -> p q r m", r=2)[:, :, k % 2]

    def s5_bank(k):
        return (PA, PB, PS[0], PS[1])[k][:].rearrange("p (q m) -> p q m", q=8)

    def s5_parameter_loads(eng):
        eng.wait_ge(SPILLED, 32)
        eng.wait_ge(X_OK, XOK_PRE + 2 * KT)
        ld = lambda d, s: eng.dma_start(d, s, allow_slow_non_contiguous=True).then_inc(S5L, 16)
        ld(ARE, ins["a_re_2"][0].rearrange("(q r) p -> (r p) q", r=2))
        ld(AIM, ins["a_im_2"][0].rearrange("(q r) p -> (r p) q", r=2))
        ldt = ins["log_dt_2"].rearrange("o (q r) -> o r q", r=2)
        for r in range(2):
            ld(DTS[64 * r:64 * r + 64], ldt[:, r].broadcast_to([64, S5_Q]))
        for k, (b, c) in enumerate((("b_re_2", "c_re_2"), ("b_im_2", "c_im_2"))):
            ld(BR[:, k], ins[b][0].rearrange("(q r) p c -> (r p) q c", r=2))
            ld(CN[:, k], ins[c][0].rearrange("(t g) c p -> (g c) t p", t=4))

    def s5_inputs_pool(pool, st):
        tt = nc.gpsimd.tensor_tensor
        pool.wait_ge(S5PW, 1)
        shape = [P, S5_Q, S5_T, S5_CH]
        a = [RPW[:, k].rearrange("p j q -> p q j").unsqueeze(3).broadcast_to(shape) for k in range(2)]
        b = [BB[:, k].unsqueeze(2).broadcast_to(shape) for k in range(2)]
        g = [GP[:, k].rearrange("p q (j c) -> p q j c", j=S5_T) for k in range(2)]
        for out, x, y, op in ((g[0], (a[0], b[0]), (a[1], b[1]), ALU.subtract), (g[1], (a[0], b[1]), (a[1], b[0]), ALU.add)):
            st(tt(out, x[0], x[1], ALU.mult))
            st.link(tt(GTMP[:], y[0], y[1], ALU.mult))
            st.link(tt(out, out, GTMP[:], op))
        nc.gpsimd.tensor_copy(EP[:, 4:5], EP[:, 0:1]).then_inc(S5GP, 1)

    def s5_loads(eng):
        eng.dma_start(U_D.rearrange("(i p) t -> p i t", p=P), MU[:]).then_inc(UD, 16)
        eng.wait_ge(dil.out_read, 64)
        eng.wait_ge(UD, 16)
        u = U_D.rearrange("(g c) (j n) -> j c g n", c=S5_CH, j=S5_T)
        for j in range(S5_T):
            eng.dma_start(UG[16 * j:16 * j + 16], u[j]).then_inc(UGL, 16)
        eng.wait_ge(S5GT, 4)
        nc.gpsimd.memset(TOE[:], 0.0).then_inc(S5Z, 1)
        eng.wait_ge(S5Z, 1)
        eng.wait_ge(S5KC, 4)
        for j in range(S5_T):
            eng.dma_start(TOE[16 * j:16 * j + 16, :, 16 * j:], K0S[0:16, :, 0:P - 16 * j]).then_inc(S5TOE, 16)
        y = Y_D.rearrange("(g c) (j n) -> j c g n", c=S5_CH, j=S5_T)
        for h in range(2):
            g = slice(16 * h, 16 * h + 16)
            eng.wait_ge(S5YC, 2 * h + 2)
            for j in range(S5_T):
                eng.dma_start(y[j][:, g], UG[16 * j:16 * j + 16, g]).then_inc(YD, 16)
            eng.wait_ge(YD, 16 * S5_T * (h + 1))
            eng.dma_start(S5Y[:, 2 * h:2 * h + 2], Y_D.rearrange("(i p) t -> p i t", p=P)[:, 2 * h:2 * h + 2]).then_inc(S5YL[h], 16)

    def cmul(st, out, a, b, tmp):
        tt = nc.vector.tensor_tensor
        st.link(tt(out[0], a[0], b[0], ALU.mult))
        st.link(tt(tmp, a[1], b[1], ALU.mult))
        st.link(tt(out[0], out[0], tmp, ALU.subtract))
        st.link(tt(out[1], a[0], b[1], ALU.mult))
        st.link(tt(tmp, a[1], b[0], ALU.mult))
        st.link(tt(out[1], out[1], tmp, ALU.add))

    def s5_powers(dve, st, part):
        v = nc.vector
        tt, stt, ts = v.tensor_tensor, v.scalar_tensor_tensor, v.tensor_scalar
        L = st.link
        if part == 0:
            dve.wait_ge(S5DT, 1)
            L(tt(XX, DTS, ARE, ALU.mult))
            L(tt(TH, DTS, AIM, ALU.mult))
            wrap(st, RED, KK, TH, 0.0)
            L(ts(KK, RED, 0.5, None, ALU.mult))
            v.tensor_copy(EP[:, 3:4], EP[:, 0:1]).then_inc(S5R, 1)
        elif part == 1:
            dve.wait_ge(S5T, 4)
            L(stt(CM, CM, -2.0, CM, ALU.mult, ALU.mult))
            L(ts(CO, CM, 1.0, None, ALU.add))
            L(stt(EM, EX, 1.0, EM, ALU.add, ALU.mult))
            L(v.memset(PW[:, 0, 0], 1.0))
            L(v.memset(PW[:, 1, 0], 0.0))
            L(tt(PW[:, 0, 1], EX, CO, ALU.mult))
            L(tt(PW[:, 1, 1], EX, SN, ALU.mult))
            L(tt(W1, EM, CO, ALU.mult))
            L(tt(W1, W1, CM, ALU.add))
            wim = PW[:, 1, 1]
            L(tt(W2, ARE, ARE, ALU.mult))
            L(tt(W3, AIM, AIM, ALU.mult))
            L(tt(W2, W2, W3, ALU.add))
            L(v.reciprocal(W2, W2))
            L(tt(W3, W1, ARE, ALU.mult))
            L(tt(W4, wim, AIM, ALU.mult))
            L(tt(W3, W3, W4, ALU.add))
            L(tt(W3, W3, W2, ALU.mult))
            L(tt(W4, wim, ARE, ALU.mult))
            L(tt(W5, W1, AIM, ALU.mult))
            L(tt(W4, W4, W5, ALU.subtract))
            L(tt(W4, W4, W2, ALU.mult))
        elif part == 2:
            over_c = lambda t: t.unsqueeze(2).broadcast_to([P, S5_Q, S5_CH])
            cmul(st, (BB[:, 0], BB[:, 1]), (over_c(W3), over_c(W4)), (BR[:, 0], BR[:, 1]), BTMP[:])
        else:
            for k in range(2 * part - 4, min(2 * part - 2, S5_T + 1)):
                cmul(st, (PW[:, 0, k], PW[:, 1, k]), (PW[:, 0, k - 1], PW[:, 1, k - 1]), (PW[:, 0, 1], PW[:, 1, 1]), W1)
            if part == 6:
                for k in range(S5_T):
                    L(v.tensor_copy(RPW[:, :, k], PW[:, :, S5_T - 1 - k]))
                v.tensor_copy(EP[:, 3:4], EP[:, 0:1]).then_inc(S5PW, 1)

    def s5_vector(dve, st):
        v = nc.vector
        tt, stt, ts = v.tensor_tensor, v.scalar_tensor_tensor, v.tensor_scalar
        L = st.link
        dve.wait_ge(S5CC, 2)
        shape = [P, S5_Q, S5_T + 1, S5_CH]
        c = [CC[:, k].unsqueeze(2).broadcast_to(shape) for k in range(2)]
        a = [PW[:, k].rearrange("p k q -> p q k").unsqueeze(3).broadcast_to(shape) for k in range(2)]
        cmul(st, (CA[:, 0], CA[:, 1]), c, a, CTMP[:])
        ts(CA[:, 1], CA[:, 1], -1.0, None, ALU.mult).then_inc(S5CA, 1)
        def square():
            L(tt(W1, CO, CO, ALU.mult))
            L(tt(W2, SN, SN, ALU.mult))
            L(stt(SN, CO, 2.0, SN, ALU.mult, ALU.mult))
            L(tt(CO, W1, W2, ALU.subtract))
        for _ in range(3):
            square()
            L(tt(EX, EX, EX, ALU.mult))
        L(v.memset(RE[:, :, 0:1], 1.0))
        L(v.memset(RI[:, :, 0:1], 0.0))
        m = 1
        while m < S5_N:
            b = [t.unsqueeze(2).broadcast_to([P, S5_Q, m]) for t in (CO, SN)]
            cmul(st, (RE[:, :, m:2 * m], RI[:, :, m:2 * m]), (RE[:, :, 0:m], RI[:, :, 0:m]), b, VI[:, :, 0:m])
            square()
            m *= 2
        dve.wait_ge(S5KC, 4)
        dve.wait_ge(S5TOE, 16 * S5_T)
        L(v.tensor_copy(RMT[:], EX.unsqueeze(2).broadcast_to([P, S5_Q, S5_N])))
        L(v.memset(RMT[:, :, 0:1], 0.0))
        for h, (pr, pi) in enumerate(((PA, PB), (PS[0], PS[1]))):
            flat = lambda t: t[:, 8 * h:8 * h + 8].rearrange("p q n -> p (q n)")
            dve.wait_ge(S5S, h + 1)
            L(tt(flat(VR), pr[:], flat(RE), ALU.mult))
            L(tt(flat(SR), pi[:], flat(RI), ALU.mult))
            L(tt(flat(VR), flat(VR), flat(SR), ALU.add))
            L(tt(flat(VI), pi[:], flat(RE), ALU.mult))
            tt(flat(SI), pr[:], flat(RI), ALU.mult).then_inc(S5ROT, 1)
            dve.wait_ge(S5ROT, h + 1)
            L(tt(flat(VI), flat(VI), flat(SI), ALU.subtract))
            st(v.tensor_tensor_scan(flat(SR), flat(RMT), flat(VR), 0.0, ALU.mult, ALU.add))
            L(v.tensor_tensor_scan(flat(SI), flat(RMT), flat(VI), 0.0, ALU.mult, ALU.add))
            part = lambda t, c: t[:, 8 * h:8 * h + 8, c]
            for t in (VR, VI):
                L(v.memset(part(t, slice(0, 1)), 0.0))
            old, new = slice(0, S5_N - 1), slice(1, S5_N)
            cmul(st, (part(VR, new), part(VI, new)), (part(SR, old), part(SI, old)), (part(RE, old), part(RI, old)), part(TMP, old))
            v.tensor_copy(EP[:, 3:4], EP[:, 0:1]).then_inc(S5V, 1)
        for k in range(4):
            if k % 2 == 0:
                dve.wait_ge(S5YL[k // 2], 16)
            stt(S5Y[:, k], MU[:, k], vec("dsk", k), S5Y[:, k], ALU.mult, ALU.add).then_inc(S5YU, 1)
        for k in range(4):
            dve.wait_ge(S5ZH, k + 1)
            tt(ZL[:, k], ACC[:, 4 + k], ZH[:, k].bitcast(F32), ALU.subtract).then_inc(S5ZL, 1)
        for m in range(4):
            b = B_GLU + m
            dve.wait_ge(PS_READ[b % 2], times(b))
            tt(ACC[:, 4 + m], ACC[:, 4 + m], T[m % 2][:], ALU.mult).then_inc(S5GLU, 1)
            split_lo(dve, b + 2, cols=cols_of(b + 2))
        for k in range(KT):
            dve.wait_ge(MIXH, k + 1)
            tt(XL[:, k], ACC[:, k], XH[:, k].bitcast(F32), ALU.subtract).then_inc(MIXL, 1)
        for m in range(KT):
            b = B_MIXOUT + m
            dve.wait_ge(BLOCK_DONE[b % 2], times(b))
            v.tensor_copy(ACC[:, m], PS[b % 2][:]).then_inc(PS_READ[b % 2], 1)
            split_lo(dve, b + 2, cols=cols_of(b + 2))

    def s5_scalar(act):
        act.wait_ge(S5CT, 1)
        for r in range(2):
            src = PA[0:64].rearrange("p (k q r c) -> p k q r c", k=2, q=S5_Q, r=2)[:, :, :, r]
            nc.scalar.activation(CC[64 * r:64 * r + 64], src, ACT.Copy).then_inc(S5CC, 1)
        for k in range(4):
            act.wait_ge(S5GT, k + 1)
            nc.scalar.activation(GIN[:, 4 * k:4 * k + 4].rearrange("p q r m -> p (q r m)"), PAB[k % 2][:], ACT.Copy).then_inc(S5GIN, 1)
        for k in range(4):
            act.wait_ge(S5K, k + 1)
            nc.scalar.activation(s5_half(K0S, k)[0:16], s5_bank(k)[0:16], ACT.Copy).then_inc(S5KC, 1)
        for k in range(4):
            act.wait_ge(S5Yp, k + 1)
            nc.scalar.activation(s5_half(UG, k), s5_bank(k), ACT.Copy).then_inc(S5YC, 1)
        for k in range(4):
            act.wait_ge(S5YU, k + 1)
            nc.scalar.activation(by_place(ACC[:, 4 + k]), S5Y[:, k].rearrange("p (j n) -> p n j", j=S5_T), ACT.Gelu_apprx_tanh).then_inc(S5G, 1)
            act.wait_ge(S5G, k + 1)
            nc.scalar.activation(ZH[:, k], ACC[:, 4 + k], ACT.Copy).then_inc(S5ZH, 1)
        for m in range(4):
            b = B_GLU + m
            act.wait_ge(BLOCK_DONE[b % 2], times(b))
            if m >= 2:
                act.wait_ge(S5GLU, m - 1)
            nc.scalar.activation(T[m % 2][:], PS[b % 2][:], ACT.Sigmoid, bias=vec("bglu", m)).then_inc(PS_READ[b % 2], 1)
            split_hi(act, b + 2, cols=cols_of(b + 2))
        for k in range(KT):
            if k >= 4:
                act.wait_ge(S5GLU, k - 3)
            nc.scalar.activation(XH[:, k], ACC[:, k], ACT.Copy).then_inc(MIXH, 1)
        for m in range(KT):
            split_hi(act, B_MIXOUT + m + 2, cols=cols_of(B_MIXOUT + m + 2))

    def s5_tensor(pe):
        pe.wait_ge(S5L, 16 * 8)
        pe.wait_ge(dil.out_copied, 4)
        for k in range(2):
            for t in range(4):
                last = nc.tensor.transpose(PA[0:64, (4 * k + t) * P:(4 * k + t + 1) * P], CN[:, k, t], IDENT[:])
        last.then_inc(S5CT, 1)
        pe.wait_ge(S5CC, 2)
        pe.wait_ge(S5GP, 1)
        for k in range(4):
            if k >= 2:
                pe.wait_ge(S5GIN, k - 1)
            for t in range(8):
                q, ri = 4 * k + t // 2, t % 2
                last = nc.tensor.transpose(PAB[k % 2][:, t * P:(t + 1) * P], GP[:, ri, q], IDENT[:])
            last.then_inc(S5GT, 1)
        pe.wait_ge(S5CA, 1)
        pe.wait_ge(S5GIN, 4)
        for h, pair in enumerate(((PA, PB), (PS[0], PS[1]))):
            for r in range(2):
                rows = slice(64 * r, 64 * r + 64)
                for t in range(8):
                    for ri in range(2):
                        last = nc.tensor.matmul(pair[r][0:16, t * P:(t + 1) * P], BB[rows, ri, 8 * h + t],
                                                CA[rows, ri, 8 * h + t, 0:S5_T].rearrange("p k c -> p (k c)"),
                                                start=(ri == 0), stop=(ri == 1))
                last.then_inc(S5K, 1)
        pe.wait_ge(UGL, 16 * S5_T)
        pe.wait_ge(S5KC, 4)
        for h, pair in enumerate(((PA, PB), (PS[0], PS[1]))):
            for t in range(8):
                q = 8 * h + t
                for r in range(2):
                    rows = slice(64 * r, 64 * r + 64)
                    for ri in range(2):
                        last = nc.tensor.matmul(pair[ri][rows, t * P:(t + 1) * P], GIN[:, q, ri, rows], UG[:, 2 * q + r], start=True, stop=True)
            last.then_inc(S5S, 1)
        pe.wait_ge(S5TOE, 16 * S5_T)
        for h, pair in enumerate(((PA, PB), (PS[0], PS[1]))):
            pe.wait_ge(S5V, h + 1)
            for r in range(2):
                rows = slice(64 * r, 64 * r + 64)
                for t in range(8):
                    q = 8 * h + t
                    y = pair[r][:, t * P:(t + 1) * P]
                    nc.tensor.matmul(y, TOE[:, 2 * q + r], UG[:, 2 * q + r], start=True, stop=False)
                    for ri, s in enumerate((VR, VI)):
                        last = nc.tensor.matmul(y, CA[rows, ri, q, 1:].rearrange("p k c -> p (k c)"), s[rows, q],
                                                start=False, stop=(ri == 1))
                last.then_inc(S5Yp, 1)
        pe.wait_ge(S5YC, 4)
        for m in range(4):
            block_products(pe, B_GLU + m, ZH, ZL, kt=4, after=(lambda k: pe.wait_ge(S5ZL, k + 1)) if m == 0 else None)
        for m in range(KT):
            block_products(pe, B_MIXOUT + m, XH, XL, after=(lambda k: pe.wait_ge(MIXL, k + 1)) if m == 0 else None)

    def s5_sync(sp):
        wg = ins["w_glu_2"][0].rearrange("(k p) c -> p k c", p=P)
        for m in range(4):
            load_block(sp, B_GLU + m, wg[:, :, m * P:(m + 1) * P], cols=512, kt=4)
        wo = ins["w_mix_out_2"][0].rearrange("(k p) c -> p k c", p=P)
        for m in range(KT):
            load_block(sp, B_MIXOUT + m, wo[:, :, m * P:(m + 1) * P])

    FTURN, FCOPY, OUT_DMA = sem("final_turned"), sem("final_copied"), [sem(f"out_stored{s}") for s in range(2)]

    def out_tensor(pe):
        for k in range(KT):
            pe.wait_ge(XRDY, 3 * KT + k + 1)
            if k >= 2:
                pe.wait_ge(FCOPY, k - 1)
            for t in range(TT):
                last = nc.tensor.transpose(PAB[k % 2][:, t * P:(t + 1) * P], ACC[:, k, t * P:(t + 1) * P], IDENT[:])
            last.then_inc(FTURN, 1)

    def out_scalar(act):
        for k in range(KT):
            act.wait_ge(FTURN, k + 1)
            if k >= 2:
                act.wait_ge(OUT_DMA[k % 2], 16 * (k // 2))
            nc.scalar.activation(OB[:, k % 2], PAB[k % 2][:], ACT.Copy).then_inc(FCOPY, 1)

    def out_sync(sp):
        rows = out[0].rearrange("(t p) c -> p t c", p=P)
        for k in range(KT):
            sp.wait_ge(FCOPY, k + 1)
            sp.dma_start(rows[:, :, k * P:(k + 1) * P], OB[:, k % 2].rearrange("p (t c) -> p t c", t=TT)).then_inc(OUT_DMA[k % 2], 16)
        for s in range(2):
            sp.wait_ge(OUT_DMA[s], 16 * (KT // 2))

    def last_block_read(b_end):
        return lambda act: (lambda k: act.wait_ge(PS_READ[(b_end - KT + k) % 2], times(b_end - KT + k)))

    block = ctx.enter_context(nc.Block())

    @block.sync
    def _(sp):
        x_sync(sp)
        in1_sync(sp)
        out1_sync(sp)
        dt_sync(sp)
        ssd_sync(sp)
        ffn_sync(sp, B_FFN1, ins["ffn1_w_in_2"][0], ins["ffn1_w_out_2"][0])
        mix_sync(sp)
        s5_sync(sp)
        ffn_sync(sp, B_FFN2, ins["ffn2_w_in_2"][0], ins["ffn2_w_out_2"][0])
        out_sync(sp)

    @block.gpsimd
    def _(pool):
        st = Steps(pool, sem("pool_steps"))
        const_pool(pool, st)
        rg_pool(pool)
        rg_loads(pool)
        mla_loads(pool)
        ssd_pool(pool)
        spill_pool(pool, 0)
        reload_pool(pool, 0, B_MIX - 1)
        spill_pool(pool, 1)
        s5_parameter_loads(pool)
        dist_pool(pool)
        dil_pool(pool, st)
        s5_loads(pool)
        reload_pool(pool, 1, B_FFN2 - 1)
        spill_pool(pool, 2)
        reload_pool(pool, 2, B_END - 1)

    @block.tensor
    def _(pe):
        x_tensor(pe)
        in1_tensor(pe)
        rg_tensor(pe)
        pe.wait_ge(RGS, 8)
        norm_rows(pe, "q", bufs=LB)
        norm_rows(pe, "kv", bufs=LB)
        mla_tensor(pe)
        out1_tensor(pe)
        ln_tensor(pe, 0, "ln1")
        dt_tensor(pe)
        ssd_tensor(pe)
        ln_tensor(pe, 1, "ln2")
        norm_rows(pe, "f1pre", bufs=PRE_SQ)
        ffn_tensor(pe, 0, B_FFN1)
        norm_rows(pe, "f1post")
        norm_rows(pe, "mpre", bufs=PRE_SQ)
        mix_tensor(pe)
        dil_tensor(pe)
        s5_tensor(pe)
        norm_rows(pe, "mpost")
        norm_rows(pe, "f2pre", bufs=PRE_SQ)
        ffn_tensor(pe, 1, B_FFN2)
        norm_rows(pe, "f2post")
        out_tensor(pe)

    @block.scalar
    def _(act):
        st = Steps(act, sem("act_steps"))
        x_scalar(act)
        split_hi(act, 0)
        split_hi(act, 1)
        in1_scalar(act)
        rg_scalar(act, st)
        mla_scalar(act)
        gate1_scalar(act)
        splits_scalar(act, B_OUT, KT)
        ln_scalar(act, st, 0, "ln1", "ln1_b", True)
        dt_scalar(act)
        ssd_scalar(act, st)
        ln_scalar(act, st, 1, "ln2", "ln2_b", False)
        pre_scalar(act, st, 0, "f1pre")
        ffn_scalar(act, 0, B_FFN1)
        post_scalar(act, st, 0, "f1post", last_block_read(B_MIX)(act))
        pre_scalar(act, st, 1, "mpre")
        mix_scalar(act)
        dil_scalar(act)
        s5_scalar(act)
        post_scalar(act, st, 1, "mpost", last_block_read(B_FFN2)(act))
        pre_scalar(act, st, 2, "f2pre")
        ffn_scalar(act, 1, B_FFN2)
        post_scalar(act, st, 2, "f2post", last_block_read(B_END)(act))
        out_scalar(act)

    @block.vector
    def _(dve):
        st = Steps(dve, sem("dve_steps"))
        x_vector(dve, st)
        split_lo(dve, 0)
        split_lo(dve, 1)
        in1_vector(dve, st)
        rg_vector(dve, st)
        mla_vector(dve, st)
        gate1_vector(dve, st)
        acc_vector(dve, st, B_OUT)
        ln_vector(dve, st, 0, "ln1", "ln1_g", B_OUT + 7, True)
        dt_vector(dve, st)
        ssd_vector(dve, st)
        ln_vector(dve, st, 1, "ln2", "ln2_g", B_FFN1 - 1, False)
        pre_vector(dve, 0, "f1pre", "f1_pre")
        ffn_vector(dve, 0, B_FFN1)
        post_vector(dve, 0, "f1post", "f1_post", B_MIX - 1)
        pre_vector(dve, 1, "mpre", "m_pre")
        mix_vector(dve, st)
        dil_vector(dve, st)
        s5_vector(dve, st)
        post_vector(dve, 1, "mpost", "m_post", B_FFN2 - 1)
        pre_vector(dve, 2, "f2pre", "f2_pre")
        ffn_vector(dve, 1, B_FFN2)
        post_vector(dve, 2, "f2post", "f2_post", B_END - 1)


def kernel(**inputs):
    import concourse.bacc as bacc
    from concourse.bass_utils import run_bass_kernel_spmd

    nc = bacc.Bacc("TRN2", target_bir_lowering=False, num_devices=1)
    arrays, ins = {}, {}
    for name, value in inputs.items():
        a = np.ascontiguousarray(value)
        arrays[f"in_{name}_dram"] = a
        ins[name] = nc.dram_tensor(f"in_{name}_dram", a.shape, mybir.dt.from_np(a.dtype), kind="ExternalInput").ap()
    out = nc.dram_tensor("out_dram", (1, SEQ, D), F32, kind="ExternalOutput").ap()
    build(nc, ins, out)
    result = run_bass_kernel_spmd(nc, [arrays], core_ids=[0])
    return result.results[0]["out_dram"]
```
